# Optimizing a Trainium2 kernel written in Bass

```python
import math
import jax
import jax.numpy as jnp
from jax import lax
import numpy as np
import jax, jax.numpy as jnp

D_MODEL = 2048
BATCH = 1
SEQ = 256
DEPTH = 1

BLOCK = 128
N_BRANCH = 4
BRANCH_W = D_MODEL // 4
A_HEADS = 4
A_HD = BRANCH_W // (2 * A_HEADS)
B_WIDTH = BRANCH_W
B_BLOCKS = 8
B_CONV = 4
B_C = 8.0
C_HEADS = 4
C_HD = BRANCH_W // C_HEADS
D_HEADS = 8
D_KV = 2
D_GROUP = D_HEADS // D_KV
D_HD = BRANCH_W // D_HEADS
WINDOW = 128
D_FF = -(-8 * D_MODEL // (3 * 256)) * 256

IN_SIZES = (
    2 * A_HEADS * A_HD, 2 * A_HEADS * A_HD, 2 * A_HEADS * A_HD,
    B_WIDTH, B_WIDTH,
    C_HEADS * C_HD, C_HEADS * C_HD, C_HEADS * C_HD, C_HEADS,
    D_HEADS * D_HD, D_KV * D_HD, D_KV * D_HD,
    N_BRANCH * D_MODEL,
)
IN_COLS = sum(IN_SIZES)
RMS_EPS = 1e-6
NEG_INF = -1e30


def rms_norm(x, g):
    xf = x.astype(jnp.float32)
    y = xf * lax.rsqrt(jnp.mean(xf * xf, axis=-1, keepdims=True) + RMS_EPS)
    return (y * g.astype(jnp.float32)).astype(x.dtype)

def alibi_slopes(n):
    return jnp.exp2(-8.0 * jnp.arange(1, n + 1, dtype=jnp.float32) / n)

def diff_attention(q, k, v, lam, slopes):
    B, S, H, _, dh = q.shape
    nb = S // BLOCK
    scale = dh ** -0.5
    qb = q.reshape(B, nb, BLOCK, H, 2, dh).transpose(1, 0, 2, 3, 4, 5)
    kpos = jnp.arange(S)

    def one_block(args):
        qblk, i = args
        qpos = i * BLOCK + jnp.arange(BLOCK)
        dist = (qpos[:, None] - kpos[None, :]).astype(jnp.float32)
        logits = jnp.einsum('bqhmd,bshmd->bmhqs', qblk, k).astype(jnp.float32) * scale
        logits = logits - slopes[:, None, None] * dist
        logits = jnp.where(dist >= 0, logits, NEG_INF)
        p = jax.nn.softmax(logits, axis=-1)
        w = p[:, 0] - lam * p[:, 1]
        return jnp.einsum('bhqs,bshe->bqhe', w.astype(v.dtype), v)

    out = lax.map(one_block, (qb, jnp.arange(nb)))
    return out.transpose(1, 0, 2, 3, 4).reshape(B, S, H, 2 * dh)

def rg_lru_branch(xb, gb, conv_w, conv_b, wa, ba, wx, bx, lam):
    B, S, C = xb.shape
    xc = lax.conv_general_dilated(xb, conv_w[:, None, :], window_strides=(1,),
                                  padding=[(B_CONV - 1, 0)],
                                  dimension_numbers=('NWC', 'WIO', 'NWC'),
                                  feature_group_count=C) + conv_b
    xg = xc.reshape(B, S, B_BLOCKS, C // B_BLOCKS)
    r = jax.nn.sigmoid(jnp.einsum('bsnc,ncd->bsnd', xg, wa).reshape(B, S, C) + ba)
    i = jax.nn.sigmoid(jnp.einsum('bsnc,ncd->bsnd', xg, wx).reshape(B, S, C) + bx)
    log_a = -B_C * r.astype(jnp.float32) * jax.nn.softplus(-lam.astype(jnp.float32))
    a = jnp.exp(log_a)
    u = jnp.sqrt(-jnp.expm1(2.0 * log_a)) * (i * xc).astype(jnp.float32)

    def combine(left, right):
        a1, b1 = left
        a2, b2 = right
        return a1 * a2, a2 * b1 + b2

    _, h = lax.associative_scan(combine, (a, u), axis=1)
    return jax.nn.gelu(gb) * h.astype(xb.dtype)

def forgetting_attention(q, k, v, logf):
    B, S, H, dh = q.shape
    nb = S // BLOCK
    scale = dh ** -0.5
    cum = jnp.cumsum(logf, axis=1).transpose(0, 2, 1)
    qb = q.reshape(B, nb, BLOCK, H, dh).transpose(1, 0, 2, 3, 4)
    cqb = cum.reshape(B, H, nb, BLOCK).transpose(2, 0, 1, 3)
    kpos = jnp.arange(S)

    def one_block(args):
        qblk, cq, i = args
        qpos = i * BLOCK + jnp.arange(BLOCK)
        causal = qpos[:, None] >= kpos[None, :]
        logits = jnp.einsum('bqhd,bshd->bhqs', qblk, k).astype(jnp.float32) * scale
        logits = logits + cq[..., None] - cum[:, :, None, :]
        logits = jnp.where(causal, logits, NEG_INF)
        p = jax.nn.softmax(logits, axis=-1)
        return jnp.einsum('bhqs,bshd->bqhd', p.astype(v.dtype), v)

    out = lax.map(one_block, (qb, cqb, jnp.arange(nb)))
    return out.transpose(1, 0, 2, 3, 4).reshape(B, S, H * dh)

def sliding_window_sink_attention(q, k, v, sinks, slopes):
    B, S, KV, G, dh = q.shape
    nb = S // BLOCK
    scale = dh ** -0.5
    pad = ((0, 0), (BLOCK, 0), (0, 0), (0, 0))

    def band(t):
        tp = jnp.pad(t, pad)
        prev = tp[:, :S].reshape(B, nb, BLOCK, KV, dh)
        cur = tp[:, BLOCK:].reshape(B, nb, BLOCK, KV, dh)
        return jnp.concatenate([prev, cur], axis=2)

    kb, vb = band(k), band(v)
    qb = q.reshape(B, nb, BLOCK, KV, G, dh)
    qi = jnp.arange(BLOCK)
    kj = jnp.arange(2 * BLOCK) - BLOCK
    dist = (qi[:, None] - kj[None, :]).astype(jnp.float32)
    key_pos = jnp.arange(nb)[:, None] * BLOCK + kj[None, :]
    valid = ((dist >= 0) & (dist < WINDOW))[None] & (key_pos >= 0)[:, None, :]
    logits = jnp.einsum('bnqkgd,bnskd->bnkgqs', qb, kb).astype(jnp.float32) * scale
    logits = logits - slopes.reshape(KV, G)[:, :, None, None] * dist
    logits = jnp.where(valid[None, :, None, None], logits, NEG_INF)
    sink = sinks.astype(jnp.float32).reshape(KV, G)[None, None, :, :, None, None]
    m = jnp.maximum(jnp.max(logits, axis=-1, keepdims=True), sink)
    e = jnp.exp(logits - m)
    p = e / (jnp.sum(e, axis=-1, keepdims=True) + jnp.exp(sink - m))
    out = jnp.einsum('bnkgqs,bnskd->bnqkgd', p.astype(v.dtype), vb)
    return out.reshape(B, S, KV * G * dh)

def first_inputs(seed: int = 0) -> dict:
    key = jax.random.key(seed)
    ks = jax.random.split(key, 26)
    f32 = jnp.float32

    def nrm(k, shape, scale):
        return jax.random.normal(k, shape, f32) * scale

    bw = B_WIDTH // B_BLOCKS
    a8 = jax.random.uniform(ks[15], (DEPTH, B_WIDTH), f32, 0.9, 0.999)
    a0 = a8 ** (1.0 / B_C)
    return {
        'x': nrm(ks[0], (BATCH, SEQ, D_MODEL), 1.0),
        'norm_mix': 1.0 + nrm(ks[1], (DEPTH, D_MODEL), 0.02),
        'w_in': nrm(ks[2], (DEPTH, D_MODEL, IN_COLS), D_MODEL ** -0.5),
        'b_gate': nrm(ks[3], (DEPTH, N_BRANCH * D_MODEL), 0.02),
        'diff_lq1': nrm(ks[4], (DEPTH, A_HD), 0.1),
        'diff_lk1': nrm(ks[5], (DEPTH, A_HD), 0.1),
        'diff_lq2': nrm(ks[6], (DEPTH, A_HD), 0.1),
        'diff_lk2': nrm(ks[7], (DEPTH, A_HD), 0.1),
        'diff_subln': 1.0 + nrm(ks[8], (DEPTH, 2 * A_HD), 0.02),
        'lru_conv_w': nrm(ks[9], (DEPTH, B_CONV, B_WIDTH), B_CONV ** -0.5),
        'lru_conv_b': nrm(ks[10], (DEPTH, B_WIDTH), 0.02),
        'lru_wa': nrm(ks[11], (DEPTH, B_BLOCKS, bw, bw), bw ** -0.5),
        'lru_ba': nrm(ks[12], (DEPTH, B_WIDTH), 0.02),
        'lru_wx': nrm(ks[13], (DEPTH, B_BLOCKS, bw, bw), bw ** -0.5),
        'lru_bx': nrm(ks[14], (DEPTH, B_WIDTH), 0.02),
        'lru_lambda': jnp.log(a0) - jnp.log1p(-a0),
        'fox_b_f': 2.0 + nrm(ks[16], (DEPTH, C_HEADS), 0.5),
        'swa_sinks': nrm(ks[17], (DEPTH, D_HEADS), 0.5),
        'w_branch': nrm(ks[18], (DEPTH, N_BRANCH, BRANCH_W, D_MODEL), BRANCH_W ** -0.5),
        'w_out': nrm(ks[19], (DEPTH, D_MODEL, D_MODEL), D_MODEL ** -0.5),
        'norm_ffn': 1.0 + nrm(ks[20], (DEPTH, D_MODEL), 0.02),
        'w_ffn_gate': nrm(ks[21], (DEPTH, D_MODEL, D_FF), D_MODEL ** -0.5),
        'w_ffn_up': nrm(ks[22], (DEPTH, D_MODEL, D_FF), D_MODEL ** -0.5),
        'w_ffn_down': nrm(ks[23], (DEPTH, D_FF, D_MODEL), D_FF ** -0.5),
        'norm_final': 1.0 + nrm(ks[24], (D_MODEL,), 0.02),
    }

def first_block(x, norm_mix, w_in, b_gate, diff_lq1, diff_lk1, diff_lq2, diff_lk2, diff_subln,
              lru_conv_w, lru_conv_b, lru_wa, lru_ba, lru_wx, lru_bx, lru_lambda,
              fox_b_f, swa_sinks, w_branch, w_out, norm_ffn, w_ffn_gate, w_ffn_up, w_ffn_down,
              norm_final):
    B, S, _ = x.shape
    slopes_a = alibi_slopes(A_HEADS)
    slopes_d = alibi_slopes(D_HEADS)
    split_points = []
    acc = 0
    for size in IN_SIZES[:-1]:
        acc += size
        split_points.append(acc)

    h = x
    for l in range(DEPTH):
        u = rms_norm(h, norm_mix[l])
        z = u @ w_in[l]
        (aq, ak, av, bxin, bgate, cq, ck, cv, cf, dq, dk, dv, gz) = jnp.split(z, split_points, axis=-1)

        lam_init = 0.8 - 0.6 * math.exp(-0.3 * l)
        lam = (jnp.exp(jnp.sum(diff_lq1[l].astype(jnp.float32) * diff_lk1[l].astype(jnp.float32)))
               - jnp.exp(jnp.sum(diff_lq2[l].astype(jnp.float32) * diff_lk2[l].astype(jnp.float32)))
               + lam_init)
        ya = diff_attention(aq.reshape(B, S, A_HEADS, 2, A_HD), ak.reshape(B, S, A_HEADS, 2, A_HD),
                            av.reshape(B, S, A_HEADS, 2 * A_HD), lam, slopes_a)
        ya = (rms_norm(ya, diff_subln[l]) * (1.0 - lam_init)).reshape(B, S, BRANCH_W)

        yb = rg_lru_branch(bxin, bgate, lru_conv_w[l], lru_conv_b[l], lru_wa[l], lru_ba[l],
                           lru_wx[l], lru_bx[l], lru_lambda[l])

        logf = jax.nn.log_sigmoid((cf + fox_b_f[l]).astype(jnp.float32))
        yc = forgetting_attention(cq.reshape(B, S, C_HEADS, C_HD), ck.reshape(B, S, C_HEADS, C_HD),
                                  cv.reshape(B, S, C_HEADS, C_HD), logf)

        yd = sliding_window_sink_attention(dq.reshape(B, S, D_KV, D_GROUP, D_HD),
                                           dk.reshape(B, S, D_KV, D_HD), dv.reshape(B, S, D_KV, D_HD),
                                           swa_sinks[l], slopes_d)

        gates = jax.nn.sigmoid(gz + b_gate[l]).reshape(B, S, N_BRANCH, D_MODEL)
        branches = (ya, yb, yc, yd)
        mixed = gates[:, :, 0] * (branches[0] @ w_branch[l, 0])
        for n in range(1, N_BRANCH):
            mixed = mixed + gates[:, :, n] * (branches[n] @ w_branch[l, n])
        h = h + mixed @ w_out[l]

        v = rms_norm(h, norm_ffn[l])
        h = h + (jax.nn.silu(v @ w_ffn_gate[l]) * (v @ w_ffn_up[l])) @ w_ffn_down[l]

    return rms_norm(h, norm_final)


BLK = 128
EPS = 1e-6
NEG = -1e30
TINY = 1e-30
FORCE = 1e4

A_DILATIONS = (1, 4, 16)
A_WINDOWS = (128, 512, 2048)
A_GROUPS = 3
A_HD_2 = 128
B_HEADS = 16
B_KV = 2
B_REP = B_HEADS // B_KV
B_HD = 64
CMP_LEN = 32
CMP_STRIDE = 16
CMP_HIDDEN = 128
SLC_LEN = 64
N_SEL = 16
WIN = 512
N_BRANCH_2 = 2
X_HEADS = 4
X_HD = 128
N_MEM = 256
PEER_HEADS = 8
PEER_DK = 256
N_KEYS = 128
N_EXPERTS = N_KEYS * N_KEYS
PEER_TOPK = 16
PEER_V_SCALE = 0.25

A_QKV_COLS = 3 * A_GROUPS * A_HEADS * A_HD_2
B_Q_COLS = B_HEADS * B_HD
B_KV_COLS = 3 * 2 * B_KV * B_HD
B_GATE_COLS = B_HEADS * 3
MERGE_COLS = N_BRANCH_2 * D_MODEL
IN_COLS_2 = A_QKV_COLS + B_Q_COLS + B_KV_COLS + B_GATE_COLS + MERGE_COLS
SPLITS = [A_QKV_COLS, A_QKV_COLS + B_Q_COLS, A_QKV_COLS + B_Q_COLS + B_KV_COLS, A_QKV_COLS + B_Q_COLS + B_KV_COLS + B_GATE_COLS]


def rmsnorm(x, g):
    xf = x.astype(jnp.float32)
    y = xf * lax.rsqrt(jnp.mean(xf * xf, axis=-1, keepdims=True) + EPS)
    return (y * g.astype(jnp.float32)).astype(x.dtype)

def alibi_slopes_2(n):
    return jnp.power(2.0, -8.0 * (jnp.arange(n, dtype=jnp.float32) + 1.0) / n)

def masked_probs(s, ok):
    s = jnp.where(ok, s, NEG)
    m = jnp.max(s, axis=-1, keepdims=True)
    p = jnp.where(ok, jnp.exp(s - m), 0.0)
    return p / jnp.maximum(jnp.sum(p, axis=-1, keepdims=True), TINY)

def dilated_window_attn(q, k, v, slopes, dil, steps):
    B, T, H, hd = q.shape
    L = T // dil
    Lp = -(-L // BLK) * BLK
    nb = Lp // BLK
    N = B * dil

    def strided(a):
        a = a.reshape(B, L, dil, H, hd).transpose(0, 2, 3, 1, 4).reshape(N, H, L, hd)
        return jnp.pad(a, ((0, 0), (0, 0), (0, Lp - L), (0, 0))).reshape(N, H, nb, BLK, hd)

    qb, kb, vb = strided(q), strided(k), strided(v)

    def with_prev(a):
        prev = jnp.concatenate([jnp.zeros_like(a[:, :, :1]), a[:, :, :-1]], axis=2)
        return jnp.concatenate([prev, a], axis=3)

    k2, v2 = with_prev(kb), with_prev(vb)
    s = jnp.einsum('nhbqd,nhbkd->nhbqk', qb, k2).astype(jnp.float32) * (hd ** -0.5)
    rel = jnp.arange(BLK)[:, None] + BLK - jnp.arange(2 * BLK)[None, :]
    ok = (rel >= 0) & (rel <= steps)
    ok = ok[None] & ((jnp.arange(nb)[:, None, None] > 0) | (jnp.arange(2 * BLK)[None, None, :] >= BLK))
    s = s - slopes.astype(jnp.float32)[:, None, None, None] * (rel * dil).astype(jnp.float32)
    s = jnp.where(ok, s, NEG)
    m = jnp.max(s, axis=-1, keepdims=True)
    p = jnp.exp(s - m)
    den = jnp.sum(p, axis=-1, keepdims=True)
    o = jnp.einsum('nhbqk,nhbkd->nhbqd', p, v2) / den
    lse = (m + jnp.log(den))[..., 0]
    o = o.reshape(N, H, Lp, hd)[:, :, :L].reshape(B, dil, H, L, hd).transpose(0, 3, 1, 2, 4).reshape(B, T, H, hd)
    lse = lse.reshape(N, H, Lp)[:, :, :L].reshape(B, dil, H, L).transpose(0, 3, 1, 2).reshape(B, T, H)
    return o, lse

def dilated_attention(qkv):
    B, T = qkv.shape[:2]
    slopes = alibi_slopes_2(A_GROUPS * A_HEADS).reshape(A_GROUPS, A_HEADS)
    outs, lses = [], []
    for g in range(A_GROUPS):
        o, l = dilated_window_attn(qkv[:, :, 0, g], qkv[:, :, 1, g], qkv[:, :, 2, g], slopes[g],
                                   A_DILATIONS[g], A_WINDOWS[g] // A_DILATIONS[g])
        outs.append(o)
        lses.append(l)
    w = jax.nn.softmax(jnp.stack(lses), axis=0)
    o = jnp.einsum('gbth,gbthd->bthd', w, jnp.stack(outs))
    return o.reshape(B, T, A_HEADS * A_HD_2)

def nsa_attention(q, kv, gates, w_ck1, w_ck2, pe_k, w_cv1, w_cv2, pe_v):
    B, T = q.shape[:2]
    scale = B_HD ** -0.5
    slopes = alibi_slopes_2(B_HEADS).reshape(B_KV, B_REP)[:, :, None, None]
    qg = q.reshape(B, T, B_KV, B_REP, B_HD).transpose(0, 2, 3, 1, 4)
    gg = gates.reshape(B, T, B_KV, B_REP, 3).transpose(0, 2, 3, 1, 4)
    kvg = kv.transpose(2, 3, 0, 4, 1, 5)
    k_c, v_c, k_s, v_s, k_w, v_w = kvg[0, 0], kvg[0, 1], kvg[1, 0], kvg[1, 1], kvg[2, 0], kvg[2, 1]

    n_cmp = (T - CMP_LEN) // CMP_STRIDE + 1
    c_idx = jnp.arange(n_cmp)[:, None] * CMP_STRIDE + jnp.arange(CMP_LEN)[None, :]

    def compress(a, pe, w1, w2):
        blocks = (a[:, :, c_idx] + pe).reshape(B, B_KV, n_cmp, CMP_LEN * B_HD)
        return jax.nn.gelu(blocks @ w1) @ w2

    kc = compress(k_c, pe_k, w_ck1, w_ck2)
    vc = compress(v_c, pe_v, w_cv1, w_cv2)
    c_end = c_idx[:, -1]
    n_slc = T // SLC_LEN
    c_start = jnp.arange(n_cmp)[:, None] * CMP_STRIDE
    s_start = jnp.arange(n_slc)[None, :] * SLC_LEN
    overlap = jnp.clip(jnp.minimum(c_start + CMP_LEN, s_start + SLC_LEN) - jnp.maximum(c_start, s_start),
                       0, None).astype(jnp.float32) / CMP_LEN
    ks_blk = k_s.reshape(B, B_KV, n_slc, SLC_LEN, B_HD)
    vs_blk = v_s.reshape(B, B_KV, n_slc, SLC_LEN, B_HD)
    nsel = min(N_SEL, n_slc)
    bi = jnp.arange(B)[:, None, None, None]
    gi = jnp.arange(B_KV)[None, :, None, None]
    kw_pad = jnp.pad(k_w, ((0, 0), (0, 0), (WIN, 0), (0, 0)))
    vw_pad = jnp.pad(v_w, ((0, 0), (0, 0), (WIN, 0), (0, 0)))
    j_slc = jnp.arange(n_slc)
    w_off = jnp.arange(BLK + WIN) - WIN

    def block(b):
        t0 = b * BLK
        t = t0 + jnp.arange(BLK)
        qb = lax.dynamic_slice_in_dim(qg, t0, BLK, axis=3)
        gb = lax.dynamic_slice_in_dim(gg, t0, BLK, axis=3)
        dist = t[:, None] - c_end[None, :]
        s = jnp.einsum('bgrqd,bgcd->bgrqc', qb, kc).astype(jnp.float32) * scale - slopes * dist.astype(jnp.float32)
        p_c = masked_probs(s, dist >= 0)
        o_c = jnp.einsum('bgrqc,bgcd->bgrqd', p_c, vc)
        imp = jnp.einsum('bgrqc,cj->bgqj', p_c, overlap)
        cur = (t // SLC_LEN)[:, None]
        forced = (j_slc == 0) | (j_slc == cur) | (j_slc == cur - 1)
        score = jnp.where(forced, FORCE, jnp.where(j_slc <= cur, imp, NEG))
        top_s, top_i = lax.top_k(score, nsel)
        ks = ks_blk[bi, gi, top_i].reshape(B, B_KV, BLK, nsel * SLC_LEN, B_HD)
        vs = vs_blk[bi, gi, top_i].reshape(B, B_KV, BLK, nsel * SLC_LEN, B_HD)
        pos = (top_i[..., None] * SLC_LEN + jnp.arange(SLC_LEN)).reshape(B, B_KV, BLK, nsel * SLC_LEN)
        d_s = t[:, None] - pos
        ok_s = (d_s >= 0) & jnp.repeat(top_s > NEG / 2, SLC_LEN, axis=-1)
        s = jnp.einsum('bgrqd,bgqkd->bgrqk', qb, ks).astype(jnp.float32) * scale - slopes * d_s[:, :, None].astype(jnp.float32)
        p_s = masked_probs(s, ok_s[:, :, None])
        o_s = jnp.einsum('bgrqk,bgqkd->bgrqd', p_s, vs)
        kw = lax.dynamic_slice_in_dim(kw_pad, t0, BLK + WIN, axis=2)
        vw = lax.dynamic_slice_in_dim(vw_pad, t0, BLK + WIN, axis=2)
        pos_w = t0 + w_off
        d_w = t[:, None] - pos_w[None, :]
        ok_w = (d_w >= 0) & (d_w < WIN) & (pos_w >= 0)[None, :]
        s = jnp.einsum('bgrqd,bgkd->bgrqk', qb, kw).astype(jnp.float32) * scale - slopes * d_w.astype(jnp.float32)
        p_w = masked_probs(s, ok_w)
        o_w = jnp.einsum('bgrqk,bgkd->bgrqd', p_w, vw)
        return gb[..., 0:1] * o_c + gb[..., 1:2] * o_s + gb[..., 2:3] * o_w

    out = lax.map(block, jnp.arange(T // BLK))
    return out.transpose(1, 0, 4, 2, 3, 5).reshape(B, T, B_HEADS * B_HD)

def memory_cross_attention(hn, mn, w_q, w_kv, w_o):
    B, T, _ = hn.shape
    q = (hn @ w_q).reshape(B, T, X_HEADS, X_HD)
    kv = (mn @ w_kv).reshape(B, mn.shape[1], 2, X_HEADS, X_HD)
    s = jnp.einsum('bthd,bmhd->bhtm', q, kv[:, :, 0]).astype(jnp.float32) * (X_HD ** -0.5)
    p = jax.nn.softmax(s, axis=-1)
    o = jnp.einsum('bhtm,bmhd->bthd', p, kv[:, :, 1]).reshape(B, T, X_HEADS * X_HD)
    return o @ w_o

def peer(xn, w_pq, sub_k1, sub_k2, u_tab, v_tab):
    B, T, D = xn.shape
    half = PEER_DK // 2
    q = (xn @ w_pq).reshape(B, T, PEER_HEADS, PEER_DK)
    s1 = jnp.einsum('bthd,kd->bthk', q[..., :half], sub_k1).astype(jnp.float32)
    s2 = jnp.einsum('bthd,kd->bthk', q[..., half:], sub_k2).astype(jnp.float32)
    v1, i1 = lax.top_k(s1, PEER_TOPK)
    v2, i2 = lax.top_k(s2, PEER_TOPK)
    cand = (v1[..., :, None] + v2[..., None, :]).reshape(B, T, PEER_HEADS, PEER_TOPK * PEER_TOPK)
    vs, ci = lax.top_k(cand, PEER_TOPK)
    e1 = jnp.take_along_axis(i1, ci // PEER_TOPK, axis=-1)
    e2 = jnp.take_along_axis(i2, ci % PEER_TOPK, axis=-1)
    eid = e1 * N_KEYS + e2
    g = jax.nn.softmax(vs, axis=-1)
    n_chunks = (B * T) // BLK
    xf = xn.reshape(n_chunks, BLK, D)
    ef = eid.reshape(n_chunks, BLK, PEER_HEADS * PEER_TOPK)
    gf = g.reshape(n_chunks, BLK, PEER_HEADS * PEER_TOPK)

    def chunk(args):
        xb, eb, gb = args
        a = jax.nn.gelu(jnp.einsum('nd,ned->ne', xb, u_tab[eb]))
        return jnp.einsum('ne,ned->nd', a * gb, v_tab[eb])

    return lax.map(chunk, (xf, ef, gf)).reshape(B, T, D)

def second_inputs(seed: int = 0) -> dict:
    key = jax.random.key(seed)
    ks = jax.random.split(key, 25)
    L, D = DEPTH, D_MODEL

    def nrm(k, shape, scale):
        return jax.random.normal(k, shape, jnp.float32) * scale

    def gain(k, shape):
        return 1.0 + 0.01 * jax.random.normal(k, shape, jnp.float32)

    return {
        'x': nrm(ks[0], (BATCH, SEQ, D), 1.0),
        'mem': nrm(ks[1], (BATCH, N_MEM, D), 1.0),
        'norm_mix': gain(ks[2], (L, D)),
        'w_in': nrm(ks[3], (L, D, IN_COLS_2), D ** -0.5),
        'w_cmp_k1': nrm(ks[4], (L, CMP_LEN * B_HD, CMP_HIDDEN), (CMP_LEN * B_HD) ** -0.5),
        'w_cmp_k2': nrm(ks[5], (L, CMP_HIDDEN, B_HD), CMP_HIDDEN ** -0.5),
        'pe_cmp_k': nrm(ks[6], (L, CMP_LEN, B_HD), 0.1),
        'w_cmp_v1': nrm(ks[7], (L, CMP_LEN * B_HD, CMP_HIDDEN), (CMP_LEN * B_HD) ** -0.5),
        'w_cmp_v2': nrm(ks[8], (L, CMP_HIDDEN, B_HD), CMP_HIDDEN ** -0.5),
        'pe_cmp_v': nrm(ks[9], (L, CMP_LEN, B_HD), 0.1),
        'w_up_a': nrm(ks[10], (L, A_HEADS * A_HD_2, D), (A_HEADS * A_HD_2) ** -0.5),
        'w_up_b': nrm(ks[11], (L, B_HEADS * B_HD, D), (B_HEADS * B_HD) ** -0.5),
        'w_out': nrm(ks[12], (L, D, D), D ** -0.5),
        'norm_x': gain(ks[13], (L, D)),
        'norm_mem': gain(ks[14], (L, D)),
        'w_xq': nrm(ks[15], (L, D, X_HEADS * X_HD), D ** -0.5),
        'w_xkv': nrm(ks[16], (L, D, 2 * X_HEADS * X_HD), D ** -0.5),
        'w_xo': nrm(ks[17], (L, X_HEADS * X_HD, D), (X_HEADS * X_HD) ** -0.5),
        'norm_ffn': gain(ks[18], (L, D)),
        'w_pq': nrm(ks[19], (L, D, PEER_HEADS * PEER_DK), D ** -0.5),
        'sub_keys1': nrm(ks[20], (L, N_KEYS, PEER_DK // 2), (PEER_DK // 2) ** -0.5),
        'sub_keys2': nrm(ks[21], (L, N_KEYS, PEER_DK // 2), (PEER_DK // 2) ** -0.5),
        'expert_u': nrm(ks[22], (L, N_EXPERTS, D), D ** -0.5),
        'expert_v': nrm(ks[23], (L, N_EXPERTS, D), PEER_V_SCALE),
        'norm_final': gain(ks[24], (D,)),
    }

def second_block(x, mem, norm_mix, w_in, w_cmp_k1, w_cmp_k2, pe_cmp_k, w_cmp_v1, w_cmp_v2, pe_cmp_v,
              w_up_a, w_up_b, w_out, norm_x, norm_mem, w_xq, w_xkv, w_xo, norm_ffn, w_pq,
              sub_keys1, sub_keys2, expert_u, expert_v, norm_final):
    B, T, D = x.shape
    h = x
    for l in range(DEPTH):
        n = rmsnorm(h, norm_mix[l])
        proj = n @ w_in[l]
        a_qkv, b_q, b_kv, b_gate, m_gate = jnp.split(proj, SPLITS, axis=-1)
        y_a = dilated_attention(a_qkv.reshape(B, T, 3, A_GROUPS, A_HEADS, A_HD_2))
        y_b = nsa_attention(b_q.reshape(B, T, B_HEADS, B_HD),
                            b_kv.reshape(B, T, 3, 2, B_KV, B_HD),
                            jax.nn.sigmoid(b_gate.reshape(B, T, B_HEADS, 3)),
                            w_cmp_k1[l], w_cmp_k2[l], pe_cmp_k[l], w_cmp_v1[l], w_cmp_v2[l], pe_cmp_v[l])
        gates = jax.nn.sigmoid(m_gate.reshape(B, T, N_BRANCH_2, D))
        mix = gates[:, :, 0] * (y_a @ w_up_a[l]) + gates[:, :, 1] * (y_b @ w_up_b[l])
        h = h + mix @ w_out[l]
        h = h + memory_cross_attention(rmsnorm(h, norm_x[l]), rmsnorm(mem, norm_mem[l]), w_xq[l], w_xkv[l], w_xo[l])
        h = h + peer(rmsnorm(h, norm_ffn[l]), w_pq[l], sub_keys1[l], sub_keys2[l], expert_u[l], expert_v[l])
    return rmsnorm(h, norm_final).astype(x.dtype)


def setup_inputs(seed=0):
    out = dict(first_inputs(seed))
    for name, value in second_inputs(seed + 1).items():
        if name != "x":
            out[name + "_2"] = value
    return out


def reference(
    x, norm_mix, w_in, b_gate, diff_lq1, diff_lk1, diff_lq2, diff_lk2, diff_subln, lru_conv_w,
    lru_conv_b, lru_wa, lru_ba, lru_wx, lru_bx, lru_lambda, fox_b_f, swa_sinks, w_branch, w_out,
    norm_ffn, w_ffn_gate, w_ffn_up, w_ffn_down, norm_final, mem_2, norm_mix_2, w_in_2,
    w_cmp_k1_2, w_cmp_k2_2, pe_cmp_k_2, w_cmp_v1_2, w_cmp_v2_2, pe_cmp_v_2, w_up_a_2, w_up_b_2,
    w_out_2, norm_x_2, norm_mem_2, w_xq_2, w_xkv_2, w_xo_2, norm_ffn_2, w_pq_2, sub_keys1_2,
    sub_keys2_2, expert_u_2, expert_v_2, norm_final_2,
):
    x = first_block(
        x, norm_mix, w_in, b_gate, diff_lq1, diff_lk1, diff_lq2, diff_lk2, diff_subln,
        lru_conv_w, lru_conv_b, lru_wa, lru_ba, lru_wx, lru_bx, lru_lambda, fox_b_f, swa_sinks,
        w_branch, w_out, norm_ffn, w_ffn_gate, w_ffn_up, w_ffn_down, norm_final,
    )
    return second_block(
        x, mem_2, norm_mix_2, w_in_2, w_cmp_k1_2, w_cmp_k2_2, pe_cmp_k_2, w_cmp_v1_2,
        w_cmp_v2_2, pe_cmp_v_2, w_up_a_2, w_up_b_2, w_out_2, norm_x_2, norm_mem_2, w_xq_2,
        w_xkv_2, w_xo_2, norm_ffn_2, w_pq_2, sub_keys1_2, sub_keys2_2, expert_u_2, expert_v_2,
        norm_final_2,
    )


_drawn_inputs = setup_inputs


def setup_inputs(seed=0):
    import zlib

    import numpy as np

    out = dict(_drawn_inputs(seed))
    spreads = {}
    factors = {'b_gate': 5.916,
     'diff_lk1': 2.735,
     'diff_lq2': 2.823,
     'diff_subln': 3.683,
     'lru_ba': 8.0,
     'lru_bx': 8.0,
     'swa_sinks': 8.0,
     'norm_ffn': 2.813,
     'norm_mix_2': 6.435,
     'pe_cmp_k_2': 8.0,
     'norm_x_2': 8.0,
     'norm_mem_2': 8.0,
     'norm_ffn_2': 34.68,
     'norm_final_2': 32.313}
    for name, (base, spread) in spreads.items():
        noise = np.random.default_rng([zlib.crc32(name.encode()), seed]).standard_normal(out[name].shape)
        drawn = base * np.exp(spread * noise) if base else spread * noise
        out[name] = jnp.asarray(drawn.astype(out[name].dtype))
    for name, factor in factors.items():
        out[name] = (out[name] * factor).astype(out[name].dtype)
    return out
```

```python
from contextlib import ExitStack, contextmanager
from collections import defaultdict
import math

import numpy as np
import concourse.bass as bass
from concourse import mybir

F32 = mybir.dt.float32
F32R = mybir.dt.float32r
I32 = mybir.dt.int32
U32 = mybir.dt.uint32
ALU = mybir.AluOpType
ACT = mybir.ActivationFunctionType
AX = mybir.AxisListType

P = 128
D = 2048
T = 256
KC = D // P
DFF = 5632
FT = DFF // P
NEG = -1e30
EPS = 1e-6
LAM_INIT = 0.8 - 0.6 * math.exp(-0.0)
RING = 4
BRANCHES = 4
N_KEYS = 128
TOPK = 16
HALF = N_KEYS // 2
C_CMP = 15

PARAMS = {}
_at = 0
for _name, _w in (
    ("norm_mix", KC), ("norm_ffn", KC), ("norm_final", KC), ("norm_mix_2", KC), ("norm_x_2", KC),
    ("norm_mem_2", KC), ("norm_ffn_2", KC), ("norm_final_2", KC), ("b_gate", 64), ("conv_w", 16),
    ("conv_b", 4), ("ba", 4), ("bx", 4), ("lambda", 4), ("fox_b_f", 4), ("sinks", 8), ("subln", 128),
    ("lq1", 64), ("lk1", 64), ("lq2", 64), ("lk2", 64), ("pe_k", 32), ("pe_v", 32), ("slopes", 40),
    ("w_cf", KC * 4),
):
    PARAMS[_name] = (_at, _w)
    _at += _w
N_PARAMS = _at
SLOPE_A, SLOPE_D, SLOPE_DIL, SLOPE_B = 0, 4, 12, 24

A_Q, A_K, A_V, B_X, B_G, C_Q, C_K, C_V, D_Q, D_K, D_V, GATES = 0, 4, 8, 12, 16, 20, 24, 28, 32, 36, 37, 38
Q2, K2, V2, BQ2, BKV2, GATES2 = 0, 12, 24, 36, 44, 50


def weight_stream():
    full = D
    s = []
    s.append(("lru", 1, [("w_in", B_X + ct + 4 * g, 0, full) for ct in range(4) for g in range(2)]))
    s.append(("diff", 2, [("w_in", b + hh, 2, full) for hh in range(2) for b in (A_Q, A_K, A_V)]))
    s.append(("fox", 2, [("w_in", b + hh, 2, full) for hh in range(2) for b in (C_Q, C_K, C_V)]))
    s.append(("swa", 1, [("w_in", b, 0, full) for b in (D_K, D_V, D_Q, D_Q + 1, D_Q + 2, D_Q + 3)]))
    s.append(("mix", KC // 2, [x for jj in range(2) for x in
              [("w_in", GATES + KC * n + jj, 2, full) for n in range(4)] + [("w_branch", jj, 2, full)]]))
    s.append(("out0", 1, [("w_out", k, 0, full) for k in range(2)]))
    s.append(("out", KC // 2 - 1, [("w_out", 2 + k, 2, full) for k in range(2)]))
    s.append(("ffn", FT // 2, [(w, k, 2, full) for k in range(2) for w in ("w_ffn_gate", "w_ffn_up")]))
    s.append(("down0", 1, [("w_ffn_down", k, 0, full) for k in range(2)]))
    s.append(("down", FT // 2 - 1, [("w_ffn_down", 2 + k, 2, full) for k in range(2)]))
    s.append(("dil", 2, [("w_in_2", b + 4 * g + hh, 2, full) for hh in range(2) for g in range(3) for b in (Q2, K2, V2)]))
    s.append(("nsa_kv", 1, [("w_in_2", BKV2 + k, 0, full) for k in range(6)]))
    for g in range(2):
        s.append((f"nsa{g}", 2, [("w_in_2", BQ2 + 4 * g + pp, 2, full) for pp in range(2)]))
    s.append(("mix2", KC // 2, [x for jj in range(2) for x in
              [("w_in_2", GATES2 + KC * n + jj, 2, full) for n in range(2)] + [("w_up_2", jj, 2, 12 * P)]]))
    s.append(("out2_0", 1, [("w_out_2", k, 0, full) for k in range(2)]))
    s.append(("out2", KC // 2 - 1, [("w_out_2", 2 + k, 2, full) for k in range(2)]))
    s.append(("mem_kv", 4, [("w_xkv_2", 0, 1, full), ("w_xkv_2", 4, 1, full)]))
    s.append(("cross", 1, [("w_xq_2", k, 0, full) for k in range(4)]))
    s.append(("xo0", 1, [("w_xo_2", k, 0, full) for k in range(2)]))
    s.append(("xo", 1, [("w_xo_2", 2 + k, 0, full) for k in range(2)]))
    s.append(("pq", 8, [("w_pq_2", k, 2, full) for k in range(2)]))
    for half in range(2):
        e = half * HALF
        n = 2 if half else HALF // 8
        s.append((f"u{half}", HALF // n, [("expert_u_2", e + k, n, full) for k in range(n)]))
        s.append((f"v{half}_0", 1, [("expert_v_2", e + k, 0, full) for k in range(2)]))
        s.append((f"v{half}", HALF // 2 - 1, [("expert_v_2", e + 2 + k, 2, full) for k in range(2)]))
    return s


class Counts:

    def __init__(self, engine, sems, found):
        self.engine, self.sems, self.found = engine, sems, found
        self.n = defaultdict(int)
        self.turn, self.per, self.last = None, {}, None
        self.held = {}

    def at(self, key, more=0):
        v = self.n[key] + more
        per = self.per.get(key, 0)
        return v if self.turn is None or not per else self.turn * per + v

    def up(self, key):
        self.n[key] += 1
        self.last = key
        return self.sems[key], 1

    def next(self, key, unit=1):
        self.n["got " + key] += 1
        v = self.at("got " + key)
        return self.sems[key], v * unit

    def own(self):
        return self.sems[self.last], self.at(self.last)

    @contextmanager
    def loop(self, name, eng, turns):
        if self.engine == "PE":
            self.last = None
        if self.last is not None:
            eng.wait_ge(*self.own())
        if turns == 1:
            yield 0
            return
        start = dict(self.n)
        self.per, self.held, self.last = LOOP_COUNTS.get(self.engine + " " + name, {}), {}, None
        with eng.Fori(0, turns) as i:
            self.turn = i
            yield i
            if self.last is not None and self.engine != "PE":
                eng.wait_ge(*self.own())
        added = {k: v - start.get(k, 0) for k, v in self.n.items() if v != start.get(k, 0)}
        if added != self.per:
            self.found[self.engine + " " + name] = added
        for k, v in added.items():
            self.n[k] = start.get(k, 0) + turns * v
        self.turn, self.per, self.held = None, {}, {}


def hold(eng, sem, value):
    if not isinstance(value, int) or value > 0:
        eng.wait_ge(sem, value)


LOOP_COUNTS = {
    "PE diff": {"full_v7": 2, "full_a0": 4, "begun": 6, "full_a1": 2, "full_a2": 2, "full_v2": 2, "full_v3": 2, "got normed": 2, "full_v6": 2, "got a_y": 2},
    "PE fox": {"full_a0": 4, "begun": 6, "full_a1": 2, "full_a2": 2, "full_v2": 2, "got normed": 2, "full_v6": 2, "got cum_ready": 2},
    "PE mix": {"full_v7": 2, "full_a0": 2, "begun": 10, "full_a1": 2, "full_a2": 2, "full_a3": 2, "full_v6": 2, "full_v4": 2, "full_v5": 2},
    "PE out": {"begun": 2, "got xkl_ready": 2},
    "PE ffn": {"full_a0": 1, "begun": 4, "full_a1": 1, "full_v4": 1, "full_v5": 1},
    "PE down": {"begun": 2, "got xkl_ready": 2},
    "PE dil": {"full_a0": 9, "begun": 18, "full_a1": 9, "full_a2": 2, "full_v2": 2, "full_a3": 2, "full_v3": 2, "got normed": 2, "full_v6": 2, "full_a4": 2, "full_v4": 2},
    "PE nsa0": {"full_a7": 2, "full_v7": 2, "full_a0": 1, "begun": 2, "full_a1": 1, "full_a2": 2, "full_v2": 2, "full_a3": 2, "full_v3": 2, "got normed": 2, "full_v6": 4, "full_a4": 2, "full_v4": 2, "full_a5": 2, "full_v5": 2},
    "PE nsa1": {"full_a7": 2, "full_v7": 2, "full_a0": 1, "begun": 2, "full_a1": 1, "full_a2": 2, "full_v2": 2, "full_a3": 2, "full_v3": 2, "got normed": 2, "full_v6": 4, "full_a4": 2, "full_v4": 2, "full_a5": 2, "full_v5": 2},
    "PE mix2": {"full_a0": 2, "begun": 6, "full_a1": 2, "full_v4": 2, "full_v5": 2},
    "PE out2": {"begun": 2, "got xkl_ready": 2},
    "PE mem_kv": {"full_a0": 1, "begun": 2, "full_a1": 1},
    "PE pq": {"full_a0": 1, "begun": 2, "full_a1": 1, "full_v2": 1},
    "PE route0": {"full_v2": 1, "full_v3": 1, "full_v4": 1, "full_v5": 1, "got lr_ready": 4},
    "PE u0": {"full_a0": 4, "begun": 8, "full_a1": 4},
    "PE v0": {"begun": 2, "got xkl_ready": 2},
    "PE route1": {"full_a2": 1, "full_a3": 1, "got lr_ready": 2},
    "PE u1": {"full_a0": 1, "begun": 2, "full_a1": 1},
    "PE v1": {"begun": 2, "got xkl_ready": 2},
    "ACT diff": {"act": 6, "got land0": 2, "hi": 6, "got land1": 2, "got land2": 1, "free_a1": 2, "free_a2": 2, "got land3": 1, "free_a0": 4, "got scored": 2, "exped": 2, "got a_ms": 2, "a_sd": 2},
    "ACT fox": {"act": 2, "got land0": 2, "hi": 6, "got land1": 2, "got land2": 1, "free_a1": 2, "free_a2": 2, "got land3": 1, "free_a0": 4, "got scored": 2, "exped": 2},
    "ACT mix": {"got land0": 3, "hi": 10, "got land1": 3, "got land2": 2, "free_a1": 2, "free_a2": 2, "free_a3": 2, "got land3": 2, "free_a0": 2, "gate_ready": 2},
    "ACT out": {"got land0": 1, "hi": 2, "got land1": 1, "xkh_ready": 2},
    "ACT ffn": {"got land0": 1, "hi": 4, "got land1": 1, "got land2": 1, "free_a1": 1, "got land3": 1, "free_a0": 1, "gate_ready": 2},
    "ACT down": {"got land0": 1, "hi": 2, "got land1": 1, "xkh_ready": 2},
    "ACT dil": {"act": 10, "got land0": 5, "hi": 18, "got land1": 5, "got land2": 4, "free_a1": 9, "free_a2": 2, "free_a3": 2, "got land3": 4, "free_a0": 9, "got scored": 2, "exped": 2, "free_a4": 2},
    "ACT nsa0": {"act": 16, "got land0": 1, "hi": 2, "got land1": 1, "free_a1": 1, "free_a2": 2, "free_a3": 2, "free_a0": 1, "got scored": 2, "exped": 2, "free_a4": 2, "free_a7": 2, "free_a5": 2},
    "ACT nsa1": {"act": 16, "got land0": 1, "hi": 2, "got land1": 1, "free_a1": 1, "free_a2": 2, "free_a3": 2, "free_a0": 1, "got scored": 2, "exped": 2, "free_a4": 2, "free_a7": 2, "free_a5": 2},
    "ACT mix2": {"got land0": 2, "hi": 6, "got land1": 2, "got land2": 1, "free_a1": 2, "got land3": 1, "free_a0": 2, "gate_ready": 2},
    "ACT out2": {"got land0": 1, "hi": 2, "got land1": 1, "xkh_ready": 2},
    "ACT mem_kv": {"got land0": 1, "hi": 2, "got land1": 1, "free_a1": 1, "free_a0": 1},
    "ACT pq": {"got land0": 1, "hi": 2, "got land1": 1, "free_a1": 1, "free_a0": 1},
    "ACT route0": {"free_a2": 1, "free_a3": 1},
    "ACT u0": {"got land0": 2, "hi": 8, "got land1": 2, "got land2": 2, "free_a1": 4, "got land3": 2, "free_a0": 4},
    "ACT v0": {"got land0": 1, "hi": 2, "got land1": 1, "xkh_ready": 2},
    "ACT route1": {"free_a2": 1, "free_a3": 1},
    "ACT u1": {"got land0": 1, "hi": 2, "got land1": 1, "free_a1": 1, "free_a0": 1, "gate_ready": 2, "got gate_free": 2},
    "ACT v1": {"got land0": 1, "hi": 2, "got land1": 1, "xkh_ready": 2},
    "DVE diff": {"dve": 16, "free_v7": 2, "got land0": 2, "lo": 6, "got land1": 2, "got land2": 1, "got land3": 1, "y_ready": 2, "free_v2": 2, "free_v3": 2, "scored": 2, "got exped": 2, "normed": 2, "free_v6": 2, "a_ms": 2, "got a_sd": 2, "a_y": 2},
    "DVE fox": {"dve": 6, "got land0": 2, "lo": 6, "got land1": 2, "got land2": 1, "got land3": 1, "y_ready": 2, "free_v2": 2, "scored": 2, "got exped": 2, "normed": 2, "free_v6": 2, "cum_ready": 2},
    "DVE mix": {"dve": 6, "free_v7": 2, "got land0": 3, "lo": 10, "got land1": 3, "got land2": 2, "got land3": 2, "free_v6": 2, "got gate_ready": 2, "free_v4": 2, "free_v5": 2},
    "DVE out": {"got land0": 1, "lo": 2, "got land1": 1, "got xkh_ready": 2, "xkl_ready": 2},
    "DVE ffn": {"got land0": 1, "lo": 4, "got land1": 1, "got land2": 1, "got land3": 1, "got gate_ready": 2, "free_v4": 1, "free_v5": 1},
    "DVE down": {"got land0": 1, "lo": 2, "got land1": 1, "got xkh_ready": 2, "xkl_ready": 2},
    "DVE dil": {"dve": 10, "got land0": 5, "lo": 18, "got land1": 5, "got land2": 4, "got land3": 4, "y_ready": 2, "free_v2": 2, "free_v3": 2, "scored": 2, "got exped": 2, "normed": 2, "free_v6": 2, "free_v4": 2},
    "DVE nsa0": {"dve": 26, "free_v7": 2, "got land0": 1, "lo": 2, "got land1": 1, "y_ready": 2, "free_v2": 2, "free_v3": 2, "scored": 2, "got exped": 2, "normed": 2, "free_v6": 4, "free_v4": 2, "free_v5": 2},
    "DVE nsa1": {"dve": 26, "free_v7": 2, "got land0": 1, "lo": 2, "got land1": 1, "y_ready": 2, "free_v2": 2, "free_v3": 2, "scored": 2, "got exped": 2, "normed": 2, "free_v6": 4, "free_v4": 2, "free_v5": 2},
    "DVE mix2": {"dve": 2, "got land0": 2, "lo": 6, "got land1": 2, "got land2": 1, "got land3": 1, "got gate_ready": 2, "free_v4": 2, "free_v5": 2},
    "DVE out2": {"got land0": 1, "lo": 2, "got land1": 1, "got xkh_ready": 2, "xkl_ready": 2},
    "DVE mem_kv": {"got land0": 1, "lo": 2, "got land1": 1},
    "DVE pq": {"got land0": 1, "lo": 2, "got land1": 1, "free_v2": 1},
    "DVE route0": {"dve": 8, "free_v2": 1, "free_v3": 1, "free_v4": 1, "free_v5": 1, "lr_ready": 4},
    "DVE u0": {"dve": 58, "got land0": 2, "lo": 8, "got land1": 2, "got land2": 2, "got land3": 2},
    "DVE v0": {"got land0": 1, "lo": 2, "got land1": 1, "got xkh_ready": 2, "xkl_ready": 2},
    "DVE route1": {"dve": 4, "lr_ready": 2},
    "DVE u1": {"got land0": 1, "lo": 2, "got land1": 1, "got gate_ready": 2, "gate_free": 2},
    "DVE v1": {"got land0": 1, "lo": 2, "got land1": 1, "got xkh_ready": 2, "xkl_ready": 2},
}


def build(nc, dram, out):
    found = {}
    stream = weight_stream()
    names = [s[0] for s in stream]
    ctx = ExitStack()
    with ctx:
        S = {}

        def sem(*keys):
            for key in keys:
                S[key] = ctx.enter_context(nc.semaphore(key))

        sem("params_in", "x_in", "mem_in", "gates_in", "small_in", "keys_in", "out_done", "table_ready")
        sem(*[f"land{s}" for s in range(RING)])
        sem("hi", "lo", "begun")
        for b in range(8):
            sem(f"full_a{b}", f"full_v{b}", f"free_a{b}", f"free_v{b}")
        sem("act", "dve", "pool")
        sem("xh_ready", "xl_ready", "sq_ready", "tmp_ready", "h_ready", "src_ready", "rs_var", "rs_std")
        sem("scored", "exped", "normed", "gate_ready", "gate_free", "conv_ready", "small_hi", "small_lo")
        sem("lru_gates", "lru_la", "lru_exp", "lru_m", "lru_s", "lsm_a", "lsm_b", "lsm_c", "cum_ready")
        sem("a_ss", "a_ms", "a_sd", "a_y", "sink_m", "sink_e", "cmp_in", "cmp_hid", "cmp_s", "cmp_e", "kv_ready")
        sem("top_m", "top_e", "idx_ready", "lr_ready", "lr_used", "g_stored", "w1_free", "lam_a", "lam_b", "masks_free", "out_ready", "y_ready", "xkh_ready", "xkl_ready", "kv2_ready")

        def sb(name, shape, dt=F32):
            return ctx.enter_context(nc.sbuf_tensor(name, shape, dt))

        ps = ctx.enter_context(nc.psum_tensor("ps", [P, 8, 512], F32))
        hT = sb("hT", [P, KC, T])
        xh = sb("xh", [P, KC, T], F32R)
        xl = sb("xl", [P, KC, T], F32R)
        raw = sb("raw", [P, RING, D])
        wh = sb("wh", [P, 2, D], F32R)
        wl = sb("wl", [P, 2, D], F32R)
        par = sb("par", [P, N_PARAMS])
        ident = sb("ident", [P, P])
        ones = sb("ones", [P, P])
        nd_causal = sb("nd_causal", [P, 2, T])
        nd_cmp = sb("nd_cmp", [P, 2, C_CMP])
        ok_cmp = sb("ok_cmp", [P, 2, C_CMP])
        iota = sb("iota", [P, P])
        iota_hi = sb("iota_hi", [P, P])
        xkh = sb("xkh", [P, 2, T], F32R)
        xkl = sb("xkl", [P, 2, T], F32R)
        rstd = sb("rstd", [P, T])
        small = sb("small", [P, 64])
        nmax = sb("nmax", [P, 8])
        ssum = sb("ssum", [P, 8])
        rinv = sb("rinv", [P, 8])
        arena0 = (nc.sbuf_base + 63) // 64 * 64
        arena_bytes = (nc.sbuf_usable_end - arena0) // 64 * 64 - 64

        def at(name, kb, shape, dt=F32):
            size = int(np.prod(shape[1:])) * 4
            assert kb * 1024 + size <= arena_bytes, (name, kb, size, arena_bytes)
            return nc.alloc_sbuf_tensor_at(name, shape, dt, offset=arena0 + int(kb * 1024))

        yh = at("yh", 0, [P, 16, T], F32R)
        yl = at("yl", 16, [P, 16, T], F32R)
        tmp = at("tmp", 32, [P, KC, T])
        xc = at("xc", 32, [P, 4, T])
        gg = at("gg", 36, [P, 4, T])
        rr = at("rr", 40, [P, 4, T])
        ii = at("ii", 44, [P, 4, T])
        wab = at("wab", 48, [P, 2, 4, P])
        aa = at("aa", 52, [P, 4, T])
        tt = at("tt", 56, [P, 4, T])
        xpad = at("xpad", 69, [P, T + 4])
        pr = at("pr", 32, [P, 4, 2, T])
        pt = at("pt", 40, [P, 4, 512])
        qs = at("qs", 48, [P, 3, T])
        ks = at("ks", 51, [P, 3, T])
        vs = at("vs", 54, [P, 6, 2, P])
        nd2 = at("nd2", 60, [P, 3, 2, T])
        triu = at("triu", 66, [P, 2, T])
        gln = at("gln", 68, [P, P])
        mscr = at("mscr", 71, [P, P])
        ysb = at("ysb", 69, [P, 2, P])
        cumq = at("cumq", 70.25, [P, 32])
        small_w = at("small_w", 71, [P, KC * 48])
        dist_i = at("dist_i", 66, [P, 2, T], I32)
        dist_m = at("dist_m", 68, [P, 2, T], I32)
        mask_f = at("mask_f", 70, [P, 2, T])
        w1 = at("w1", 32, [P, 32, P])
        small_h = at("small_h", 76, [P, KC * 48], F32R)
        small_l = at("small_l", 79, [P, KC * 48], F32R)
        xw = at("xw", 48, [P, 32, C_CMP])
        kcv = at("kcv", 64, [P, 2, T])
        kd = at("kd", 60, [P, 2, 2, T])
        kcd = at("kcd", 66, [P, 2, 16])
        vcd = at("vcd", 66.5, [P, 2, 64])
        w2 = at("w2", 74, [P, 2, P])
        hid_c = at("hid_c", 66.25, [P, 2, 16])
        sc = at("sc", 67, [P, 2, 2, 16])
        pc = at("pc", 56, [P, 2, 2, P])
        ptc = at("ptc", 58, [P, 2, T])
        bg2 = at("bg2", 75, [P, 2, 48])
        mixT = at("mixT", 32, [P, KC, T])
        gt = at("gt", 48, [P, 8, T])
        mtmp = at("mtmp", 56, [P, T])
        hidT = at("hidT", 0, [P, FT, T])
        gt2 = at("gt2", 48, [P, 2, T])
        memT = at("memT", 0, [P, KC, T])
        kx = at("kx", 56, [P, 4, T])
        vx = at("vx", 60, [P, 4, 2, P])
        yx = at("yx", 64, [P, 4, T])
        ag = at("ag", 0, [P, HALF, T])
        e1t = at("e1t", 64, [P, T])
        e2t = at("e2t", 65, [P, T])
        gtt = at("gtt", 66, [P, T])
        oh_l = at("oh_l", 67, [P, 2, 8, P])
        oh_r = at("oh_r", 75, [P, 2, 8, HALF])
        gt3 = at("gt3", 79, [P, 2, T])
        keysT = at("keysT", 82, [P, 2, P])
        qt = at("qt", 80, [P, 2, T])
        svs = at("svs", 48, [P, 8, 4 * P])
        sv = at("sv", 78, [P, 4, P])
        sv2 = at("sv2", 64, [P, 4, P])
        vtop = at("vtop", 66, [P, 4, TOPK])
        itop = at("itop", 66.25, [P, 4, TOPK], U32)
        itf = at("itf", 66.5, [P, 4, TOPK])
        ctop = at("ctop", 66.75, [P, 2, TOPK])
        cidx = at("cidx", 67, [P, 2, TOPK], U32)
        cij = at("cij", 67.25, [P, 2, 2, TOPK], U32)
        cijf = at("cijf", 67.75, [P, 2, 2, TOPK])
        cand = at("cand", 69, [P, 2, 256])
        cand2 = at("cand2", 71, [P, 2, 256])
        eqb = at("eqb", 73, [P, 2, 256])
        etab = at("etab", 75, [P, 3, 2, P])

        def p_col(name, j=0, n=1):
            o, w = PARAMS[name]
            return par[:, o + j:o + j + n]

        def p_dyn(name, j):
            o, w = PARAMS[name]
            return par[:, bass.ds(j + o, 1)]

        def one(ap3):
            return ap3.rearrange("p o t -> p (o t)")

        def dyn(t, j):
            return t[:, j, :] if isinstance(j, int) else one(t[:, bass.ds(j, 1), :])

        route_base = []
        block = ctx.enter_context(nc.Block())

        @block.sync
        def _(sp):
            k = Counts("SP", S, found)
            sp.dma_start(par[:], dram["params"]).then_inc(S["params_in"], 16)
            sp.dma_start(hT[:], dram["x"]).then_inc(S["x_in"], 16)
            sp.dma_start(wab[:], dram["w_ab"]).then_inc(S["gates_in"], 16)
            sp.dma_start(keysT[:], dram["sub_keys"]).then_inc(S["keys_in"], 16)
            sent, holder, before = 0, {}, None
            for name, turns, chunks in stream:
                n = len(chunks)
                last = {s: max((j for j in range(n) if j % RING == s), default=None) for s in range(RING)}

                def send(i, j, ordinal, prior):
                    tensor, first, step, width = chunks[j]
                    s = j % RING
                    if prior is not None:
                        sp.wait_ge(S["hi"], prior)
                        sp.wait_ge(S["lo"], prior)
                    src = dram[tensor]
                    idx = first + (step * i if step else 0)
                    src = src[idx] if isinstance(idx, int) else src[bass.ds(idx, 1)].rearrange("o p w -> (o p) w")
                    sp.dma_start(raw[:, s, 0:width], src).then_inc(S[f"land{s}"], 16)

                if turns == 1:
                    for j in range(n):
                        s = j % RING
                        send(0, j, sent + j, holder[s] + 1 if s in holder else None)
                        holder[s] = sent + j
                else:
                    back = []
                    for j in range(n):
                        s = j % RING
                        d = [RING] if j >= RING else [n - last[s] + j]
                        if j < RING:
                            d.append(sent + j - holder[s])
                        back.append(min(d))
                    with sp.Fori(0, turns) as i:
                        for j in range(n):
                            send(i, j, None, i * n + (sent + j - back[j] + 1))
                    for s in range(RING):
                        if last[s] is not None:
                            holder[s] = sent + (turns - 1) * n + last[s]
                sent += turns * n
            sp.wait_ge(S["out_ready"], 1)
            sp.dma_start(out, tmp[:]).then_inc(S["out_done"], 16)
            sp.wait_ge(S["out_done"], 16)

        @block.gpsimd
        def _(pool):
            k = Counts("Pool", S, found)
            g = nc.gpsimd

            def select(t, fill, base, pattern, mult, op=ALU.is_ge):
                pool.wait_ge(*k.own())
                g.affine_select(out=t, in_=t, compare_op=op, fill=fill, base=base, pattern=pattern,
                                channel_multiplier=mult).then_inc(*k.up("pool"))

            g.memset(ident[:], 1.0).then_inc(*k.up("pool"))
            select(ident[:], 0.0, 0, [[-1, P]], 1, ALU.is_equal)
            g.memset(ones[:], 1.0).then_inc(*k.up("pool"))
            g.iota(iota[:], [[1, P]], base=0, channel_multiplier=0,
                   allow_small_or_imprecise_dtypes=True).then_inc(*k.up("pool"))
            g.iota(iota_hi[:], [[1, P]], base=HALF, channel_multiplier=0,
                   allow_small_or_imprecise_dtypes=True).then_inc(*k.up("pool"))
            dist = [[-P, 2], [1, T]]
            g.iota(nd_causal[:], dist, base=0, channel_multiplier=-1,
                   allow_small_or_imprecise_dtypes=True).then_inc(*k.up("pool"))
            select(nd_causal[:], NEG, 0, [[P, 2], [-1, T]], 1)
            g.iota(nd_cmp[:], [[-P, 2], [16, C_CMP]], base=31, channel_multiplier=-1,
                   allow_small_or_imprecise_dtypes=True).then_inc(*k.up("pool"))
            select(nd_cmp[:], NEG, -31, [[P, 2], [-16, C_CMP]], 1)
            g.memset(ok_cmp[:], 1.0).then_inc(*k.up("pool"))
            select(ok_cmp[:], 0.0, -31, [[P, 2], [-16, C_CMP]], 1)
            g.iota(nd2[:, 0], dist, base=0, channel_multiplier=-1,
                   allow_small_or_imprecise_dtypes=True).then_inc(*k.up("pool"))
            select(nd2[:, 0], NEG, 0, [[P, 2], [-1, T]], 1)
            select(nd2[:, 0], NEG, 127, [[-P, 2], [1, T]], -1)
            g.memset(nd2[:, 1], 0.0).then_inc(*k.up("pool"))
            select(nd2[:, 1], NEG, 0, [[P, 2], [-1, T]], 1)
            g.memset(triu[:], 1.0).then_inc(*k.up("pool"))
            select(triu[:], 0.0, 0, [[-P, 2], [1, T]], -1)
            pool.wait_ge(*k.own())
            g.memset(rstd[:, 0:1], 0.0).then_inc(S["table_ready"], 1)
            pool.wait_ge(S["masks_free"], 1)
            for j in range(3):
                g.iota(nd2[:, j], dist, base=0, channel_multiplier=-1,
                       allow_small_or_imprecise_dtypes=True).then_inc(*k.up("pool"))
                select(nd2[:, j], NEG, 0, [[P, 2], [-1, T]], 1)
            select(nd2[:, 0], NEG, P, [[-P, 2], [1, T]], -1)
            pool.wait_ge(*k.own())
            g.iota(dist_i[:], [[P, 2], [-1, T]], base=0, channel_multiplier=1).then_inc(S["table_ready"], 1)

            loads = [("nsa_kv", 1, small_w, dram["w_bgate"], "small_in"), ("nsa_kv", 1, w1, dram["w_cmp1"][0], "small_in"),
                     ("nsa_kv", 1, w2, dram["w_cmp2"], "small_in"), ("nsa_kv", 2, w1, dram["w_cmp1"][1], "small_in"),
                     ("mem", 3, memT, dram["mem"], "mem_in")]
            for phase, free, dst, src, landed in loads:
                pool.wait_ge(S["w1_free"], free)
                g.dma_start(dst[:], src).then_inc(S[landed], 16)

        @block.tensor
        def _(pe):
            k = Counts("PE", S, found)
            mm = nc.tensor.matmul

            def reserve(*banks):
                for b in banks:
                    for e in "av":
                        key = f"full_{e}{b}"
                        if k.held.get(key) != k.n[key]:
                            hold(pe, S[f"free_{e}{b}"], k.at(key))
                            k.held[key] = k.n[key]

            def chunk():
                pe.wait_ge(S["hi"], k.at("begun", 1))
                pe.wait_ge(S["lo"], k.at("begun", 1))

            def begin(ins, first):
                if first:
                    ins.then_inc(*k.up("begun"))

            def tile_T(j, b, reader):
                reserve(b)
                chunk()
                for kc in range(KC):
                    c = slice(kc * P, (kc + 1) * P)
                    begin(mm(ps[:, b, 0:T], wh[:, j % 2, c], xh[:, kc, :], start=kc == 0, stop=False), kc == 0)
                    mm(ps[:, b, 0:T], wh[:, j % 2, c], xl[:, kc, :], start=False, stop=False)
                    m = mm(ps[:, b, 0:T], wl[:, j % 2, c], xh[:, kc, :], start=False, stop=kc == KC - 1)
                m.then_inc(*k.up(f"full_{reader}{b}"))

            def tile_N(j, b, reader):
                reserve(b)
                chunk()
                for tq in range(2):
                    o = ps[:, b, tq * P:(tq + 1) * P]
                    for kc in range(KC):
                        c, t = slice(kc * P, (kc + 1) * P), slice(tq * P, (tq + 1) * P)
                        begin(mm(o, xh[:, kc, t], wh[:, j % 2, c], start=kc == 0, stop=False), tq + kc == 0)
                        mm(o, xh[:, kc, t], wl[:, j % 2, c], start=False, stop=False)
                        m = mm(o, xl[:, kc, t], wh[:, j % 2, c], start=False, stop=kc == KC - 1)
                m.then_inc(*k.up(f"full_{reader}{b}"))

            def part_T(j, b, k0, nk, y0, first):
                reserve(b)
                for n in range(nk):
                    c = slice((k0 + n) * P, (k0 + n + 1) * P)
                    begin(mm(ps[:, b, 0:T], wh[:, j % 2, c], yh[:, y0 + n, :], start=n == 0, stop=False),
                          first and n == 0)
                    mm(ps[:, b, 0:T], wh[:, j % 2, c], yl[:, y0 + n, :], start=False, stop=False)
                    m = mm(ps[:, b, 0:T], wl[:, j % 2, c], yh[:, y0 + n, :], start=False, stop=n == nk - 1)
                m.then_inc(*k.up(f"full_v{b}"))

            def rows(j, first, last):
                chunk()
                pe.wait_ge(*k.next("xkl_ready"))
                for t in range(KC):
                    o = ps[:, t // 2, (t % 2) * T:(t % 2 + 1) * T]
                    c = slice(t * P, (t + 1) * P)
                    begin(mm(o, wh[:, j % 2, c], xkh[:, j % 2, :], start=first and t % 2 == 0, stop=False,
                             skip_group_check=True), t == 0)
                    mm(o, wh[:, j % 2, c], xkl[:, j % 2, :], start=False, stop=False, skip_group_check=True)
                    m = mm(o, wl[:, j % 2, c], xkh[:, j % 2, :], start=False, stop=last,
                           skip_group_check=True)
                    if last and t % 2 == 1:
                        m.then_inc(*k.up(f"full_v{t // 2}"))

            def residual(name, turns, peel_last=False):
                reserve(*range(8))
                rows(0, True, False)
                rows(1, False, False)
                if turns > 2:
                    with k.loop(name, pe, turns - 2):
                        rows(0, False, False)
                        rows(1, False, False)
                rows(0, False, False)
                rows(1, False, True)

            def sum_squares():
                reserve(7)
                for q in range(4):
                    pe.wait_ge(*k.next("sq_ready"))
                    for kc in range(4 * q, 4 * q + 4):
                        m = mm(ps[:, 7, 0:T], ones[:], tmp[:, kc, :], start=kc == 0, stop=kc == KC - 1)
                m.then_inc(*k.up("full_v7"))

            def normed_x():
                for q in range(4):
                    pe.wait_ge(*k.next("xl_ready"))

            def small_tile(b, width, reader):
                reserve(b)
                pe.wait_ge(*k.next("small_lo"))
                for tq in range(2):
                    o = ps[:, b, tq * 64:tq * 64 + width]
                    t = slice(tq * P, (tq + 1) * P)
                    for kc in range(KC):
                        c = slice(kc * width, (kc + 1) * width)
                        mm(o, xh[:, kc, t], small_h[:, c], start=kc == 0, stop=False)
                        mm(o, xh[:, kc, t], small_l[:, c], start=False, stop=False)
                        m = mm(o, xl[:, kc, t], small_h[:, c], start=False, stop=kc == KC - 1)
                m.then_inc(*k.up(f"full_{reader}{b}"))

            def staged(*banks):
                reserve(*banks)

            def qk(b, q, key, lo=0, hi=P, more=None):
                reserve(b)
                for i in range(2):
                    o = ps[:, b, i * T:(i + 1) * T]
                    m = mm(o, q[lo:hi, i * P:(i + 1) * P], key[lo:hi, :], start=True, stop=more is None)
                    if more is not None:
                        m = more(o)
                m.then_inc(*k.up(f"full_v{b}"))

            BLOCKS = ((0, 0), (1, 0), (1, 1), (0, 1))

            def turn_probs(maps, n_blocks=3):
                for m in maps:
                    reserve(2 + m)
                    for n, (i, kt) in enumerate(BLOCKS[:n_blocks]):
                        ins = nc.tensor.transpose(ps[:, 2 + m, n * P:(n + 1) * P],
                                                  pr[:, m, i, kt * P:(kt + 1) * P], ident[:])
                    ins.then_inc(*k.up(f"full_a{2 + m}"))

            def pv_T(o, v, m, first, last):
                mm(o, v(0), pt[:, m, 0:T], start=first, stop=False, skip_group_check=True)
                return mm(o[:, P:T], v(1), pt[:, m, T:T + P], start=False, stop=last, skip_group_check=True)

            pe.wait_ge(S["table_ready"], 1)
            sum_squares()
            normed_x()

            for ct in range(4):
                tile_T(2 * ct, 0, "v")
                tile_T(2 * ct + 1, 1, "a")
                pe.wait_ge(*k.next("conv_ready"))
                if ct == 0:
                    pe.wait_ge(S["gates_in"], 16)
                for gate in range(2):
                    reserve(2 + gate)
                    mm(ps[:, 2 + gate, 0:T], wab[:, gate, ct, :], xc[:, ct, :], start=True,
                       stop=True).then_inc(*k.up(f"full_a{2 + gate}"))

            def diff_finish(hh):
                pe.wait_ge(*k.next("normed"))
                turn_probs([0])
                staged(2)
                reserve(6)
                v = vs[:, hh]
                mm(ps[:, 6, 0:P], pt[:, 0, 0:P], v[:, 0, :], start=True, stop=True)
                mm(ps[:, 6, P:T], pt[:, 0, P:T], v[:, 0, :], start=True, stop=False)
                mm(ps[:, 6, P:T], pt[:, 0, T:T + P], v[:, 1, :], start=False,
                   stop=True).then_inc(*k.up("full_v6"))
                pe.wait_ge(*k.next("a_y"))
                reserve(7)
                for i in range(2):
                    m = nc.tensor.transpose(ps[:, 7, i * P:(i + 1) * P], ysb[:, i, :], ident[:])
                m.then_inc(*k.up("full_v7"))

            with k.loop("diff", pe, 2):
                for hh in range(2):
                    tile_T(3 * hh, 0, "a")
                    tile_T(3 * hh + 1, 1, "a")
                    tile_N(3 * hh + 2, 0, "a")
                    if hh == 1:
                        diff_finish(0)
                    staged(0, 1)
                    for m in range(2):
                        qk(2 + m, qs[:, 0], ks[:, 0], 64 * m, 64 * m + 64)
                diff_finish(1)

            small_tile(7, 4, "v")
            pe.wait_ge(*k.next("lsm_c"))
            reserve(7)
            for i in range(2):
                for st in range(2):
                    m = mm(ps[:, 7, 4 * i:4 * i + 4], triu[:, st, i * P:(i + 1) * P],
                           cumq[:, 8 + 4 * st:12 + 4 * st], start=st == 0, stop=st == 1)
            m.then_inc(*k.up("full_v7"))

            def fox_finish(hh):
                pe.wait_ge(*k.next("normed"))
                turn_probs([0])
                staged(2)
                reserve(6)
                pv_T(ps[:, 6, 0:T], lambda kt: vs[:, hh, kt, :], 0, True, True).then_inc(*k.up("full_v6"))

            with k.loop("fox", pe, 2):
                for hh in range(2):
                    tile_T(3 * hh, 0, "a")
                    tile_T(3 * hh + 1, 1, "a")
                    tile_N(3 * hh + 2, 0, "a")
                    if hh == 1:
                        fox_finish(0)
                    staged(0, 1)
                    pe.wait_ge(*k.next("cum_ready"))

                    def less_cum(o):
                        for st in range(2):
                            m = mm(o, cumq[:, 16 + st:17 + st].to_broadcast([P, P]), triu[:, st, :],
                                   start=False, stop=st == 1)
                        return m
                    qk(2, qs[:, 0], ks[:, 0], more=less_cum)
                fox_finish(1)

            tile_T(0, 0, "a")
            tile_N(1, 1, "a")

            def swa_finish(g):
                pe.wait_ge(*k.next("normed"))
                turn_probs([0, 1])
                staged(2, 3)
                reserve(6)
                for hh in range(2):
                    m = pv_T(ps[64 * hh:64 * hh + 64, 6, 0:T], lambda kt: vs[:, 0, kt, 64 * g:64 * g + 64],
                             hh, True, True)
                m.then_inc(*k.up("full_v6"))

            for pair in range(4):
                tile_T(2 + pair, pair % 2, "a")
                if pair:
                    swa_finish((pair - 1) // 2)
                staged(0, 1)
                for hh in range(2):
                    qk(2 + hh, qs[:, 0], ks[:, 1 + pair // 2], 64 * hh, 64 * hh + 64)
            swa_finish(1)

            for _ in range(16):
                k.n["got y_ready"] += 1
            pe.wait_ge(S["y_ready"], k.n["got y_ready"])
            with k.loop("mix", pe, KC // 2):
                for jj in range(2):
                    for n in range(4):
                        tile_T(5 * jj + n, n, "a")
                    chunk()
                    for n in range(4):
                        part_T(5 * jj + 4, 4 + n, 4 * n, 4, 4 * n, n == 0)

            residual("out", KC // 2)
            sum_squares()
            normed_x()
            with k.loop("ffn", pe, FT // 2):
                for f in range(2):
                    reserve(4 + f)
                    tile_T(2 * f, f, "a")
                    tile_T(2 * f + 1, 4 + f, "v")
            residual("down", FT // 2)
            sum_squares()

            sum_squares()
            normed_x()

            def dil_finish(hh):
                pe.wait_ge(*k.next("normed"))
                turn_probs([0, 1, 2])
                staged(2, 3, 4)
                reserve(6)
                for g in range(3):
                    m = pv_T(ps[:, 6, 0:T], lambda kt: vs[:, 3 * hh + g, kt, :], g, g == 0, g == 2)
                m.then_inc(*k.up("full_v6"))

            with k.loop("dil", pe, 2):
                for hh in range(2):
                    for g in range(3):
                        c = 9 * hh + 3 * g
                        tile_T(c, c % 2, "a")
                        tile_T(c + 1, (c + 1) % 2, "a")
                        tile_N(c + 2, c % 2, "a")
                        if hh == 1 and g == 0:
                            dil_finish(0)
                        staged(0, 1)
                        qk(2 + g, qs[:, g], ks[:, g])
                dil_finish(1)

            for j, kind in enumerate("TTTNTN"):
                (tile_T if kind == "T" else tile_N)(j, j % 2, "a")
            small_tile(7, 48, "a")
            for kv in range(2):
                pe.wait_ge(*k.next("cmp_in"))
                pe.wait_ge(S["small_in"], 48 if kv == 0 else 64)
                reserve(5, 6)
                for g in range(2):
                    o = ps[:, 5 + g, 0:C_CMP]
                    for i in range(32):
                        m = mm(o, w1[64 * g:64 * g + 64, i, :], xw[64 * g:64 * g + 64, i, :],
                               start=i == 0, stop=i == 31)
                    m.then_inc(*k.up(f"full_a{5 + g}"))
                pe.wait_ge(*k.next("cmp_hid"))
                reserve(7)
                for g in range(2):
                    if kv == 0:
                        m = mm(ps[:, 7, g * 16:g * 16 + C_CMP], w2[:, 0, :], hid_c[:, g, 0:C_CMP],
                               start=True, stop=True)
                    else:
                        m = mm(ps[0:C_CMP, 7, g * 64:g * 64 + 64], hid_c[:, g, 0:C_CMP], w2[:, 1, 0:64],
                               start=True, stop=True)
                m.then_inc(*k.up("full_v7"))

            def nsa_finish(g):
                pe.wait_ge(*k.next("normed"))
                turn_probs([0, 1, 2, 3])
                reserve(7)
                for hh in range(2):
                    for i in range(2):
                        m = nc.tensor.transpose(ps[:, 7, hh * T + i * P:hh * T + (i + 1) * P],
                                                pc[:, hh, i, :], ident[:])
                m.then_inc(*k.up("full_a7"))
                staged(2, 3, 4, 5, 7)
                reserve(6)
                for hh in range(2):
                    o = ps[64 * hh:64 * hh + 64, 6, 0:T]
                    for br in range(2):
                        pv_T(o, lambda kt: vs[:, br, kt, 64 * g:64 * g + 64], 2 * hh + br, br == 0, False)
                    m = mm(o, vcd[0:C_CMP, g, :], ptc[0:C_CMP, hh, :], start=False, stop=True,
                           skip_group_check=True)
                m.then_inc(*k.up("full_v6"))

            pe.wait_ge(*k.next("kv2_ready"))
            for g in range(2):
                with k.loop(f"nsa{g}", pe, 2):
                    for pp in range(2):
                        tile_T(pp, pp, "a")
                        if pp == 1:
                            nsa_finish(g)
                        staged(0, 1)
                        for hh in range(2):
                            for br in range(2):
                                qk(2 + 2 * hh + br, qs[:, 0], kd[:, br, g], 64 * hh, 64 * hh + 64)
                        reserve(6, 7)
                        for hh in range(2):
                            for i in range(2):
                                m = mm(ps[:, 6 + hh, i * 16:i * 16 + C_CMP], qs[64 * hh:64 * hh + 64, 0, i * P:(i + 1) * P],
                                       kcd[64 * hh:64 * hh + 64, g, 0:C_CMP], start=True, stop=True)
                            m.then_inc(*k.up(f"full_v{6 + hh}"))
                    nsa_finish(g)

            for _ in range(12):
                k.n["got y_ready"] += 1
            pe.wait_ge(S["y_ready"], k.n["got y_ready"])
            with k.loop("mix2", pe, KC // 2):
                for jj in range(2):
                    for n in range(2):
                        tile_T(3 * jj + n, n, "a")
                    chunk()
                    part_T(3 * jj + 2, 4, 0, 4, 0, True)
                    part_T(3 * jj + 2, 5, 4, 8, 4, False)

            residual("out2", KC // 2)
            sum_squares()
            normed_x()
            with k.loop("mem_kv", pe, 4):
                tile_T(0, 0, "a")
                tile_N(1, 1, "a")
            sum_squares()
            normed_x()

            def cross_finish(h):
                pe.wait_ge(*k.next("normed"))
                turn_probs([0], 4)
                staged(2)
                reserve(6)
                o = ps[:, 6, 0:T]
                mm(o, vx[:, h, 0, :], pt[:, 0, 0:T], start=True, stop=False, skip_group_check=True)
                mm(o[:, P:T], vx[:, h, 1, :], pt[:, 0, T:T + P], start=False, stop=False, skip_group_check=True)
                mm(o[:, 0:P], vx[:, h, 1, :], pt[:, 0, T + P:2 * T], start=False, stop=True,
                   skip_group_check=True).then_inc(*k.up("full_v6"))

            for h in range(4):
                tile_T(h, h % 2, "a")
                if h:
                    cross_finish(h - 1)
                staged(0, 1)
                qk(2, qs[:, 0], kx[:, h])
            cross_finish(3)
            residual("xo", 2)
            def route(b):
                reserve(b)
                for s in range(8):
                    m = mm(ps[:, b, s * HALF:(s + 1) * HALF], oh_l[:, b % 2, s, :], oh_r[:, b % 2, s, :],
                           start=True, stop=True)
                return m

            sum_squares()
            normed_x()
            pe.wait_ge(S["keys_in"], 16)
            with k.loop("pq", pe, 8):
                tile_T(0, 0, "a")
                tile_T(1, 1, "a")
                staged(0, 1)
                reserve(2)
                for i in range(2):
                    for side in range(2):
                        c = (2 * i + side) * P
                        m = mm(ps[:, 2, c:c + P], qt[:, side, i * P:(i + 1) * P], keysT[:, side, :],
                               start=True, stop=True)
                m.then_inc(*k.up("full_v2"))
            with k.loop("u0", pe, 8):
                for j in range(HALF // 8):
                    tile_T(j, j % 2, "a")
            pe.wait_ge(*k.next("idx_ready"))
            for n in range(3):
                reserve(3 + n)
                for i in range(2):
                    m = nc.tensor.transpose(ps[:, 3 + n, i * P:(i + 1) * P], etab[:, n, i, :], ident[:])
                m.then_inc(*k.up(f"full_v{3 + n}"))
            with k.loop("route0", pe, 8):
                for b in range(4):
                    pe.wait_ge(*k.next("lr_ready"))
                    route(2 + b).then_inc(*k.up(f"full_v{2 + b}"))
            residual("v0", HALF // 2)
            route_base.extend([k.at("full_a2"), k.at("full_a3")])
            with k.loop("route1", pe, 16):
                for b in range(2):
                    pe.wait_ge(*k.next("lr_ready"))
                    route(2 + b).then_inc(*k.up(f"full_a{2 + b}"))
            with k.loop("u1", pe, HALF // 2):
                for b in range(2):
                    tile_T(b, b, "a")
            residual("v1", HALF // 2)
            sum_squares()

        @block.scalar
        def _(act):
            k = Counts("ACT", S, found)
            f = nc.scalar.activation

            def own():
                act.wait_ge(*k.own())

            def take(b):
                act.wait_ge(S[f"full_a{b}"], k.at(f"free_a{b}", 1))

            def split(j, width=D):
                act.wait_ge(*k.next(f"land{j % RING}", 16))
                hold(act, S["begun"], k.at("hi"))
                f(wh[:, j % 2, 0:width], raw[:, j % RING, 0:width], ACT.Copy).then_inc(*k.up("hi"))

            def xsplit(j, src, n):
                hold(act, S["begun"], k.at("hi", -1))
                f(xkh[:, j % 2, :], dyn(src, n), ACT.Copy).then_inc(*k.up("xkh_ready"))

            def residual(src, name, turns, more=True):
                act.wait_ge(*k.next("src_ready"))
                xsplit(0, src, 0)
                split(1)
                xsplit(1, src, 1)
                split(0)
                xsplit(0, src, 2)
                if turns > 2:
                    with k.loop(name, act, turns - 2) as i:
                        split(1)
                        xsplit(1, src, i * 2 + 3)
                        split(0)
                        xsplit(0, src, i * 2 + 4)
                split(1)
                xsplit(1, src, 2 * turns - 1)
                if more:
                    split(0)

            def norm(src, arrived=None, parts=True):
                if arrived is None:
                    act.wait_ge(*k.next("h_ready"))
                else:
                    act.wait_ge(*arrived)
                for q in range(4):
                    c = slice(4 * q, 4 * q + 4)
                    f(tmp[:, c, :], src[:, c, :], ACT.Square).then_inc(*k.up("sq_ready"))
                act.wait_ge(*k.next("rs_var"))
                f(rstd[:], rstd[:], ACT.Sqrt).then_inc(*k.up("rs_std"))
                if parts:
                    for q in range(4):
                        c = slice(4 * q, 4 * q + 4)
                        act.wait_ge(*k.next("tmp_ready"))
                        f(xh[:, c, :], tmp[:, c, :], ACT.Copy).then_inc(*k.up("xh_ready"))

            def evac(b, dst, scale=None):
                take(b)
                src = ps[:, b, 0:T]
                if scale is None:
                    f(dst, src, ACT.Copy).then_inc(*k.up(f"free_a{b}"))
                else:
                    f(dst, src, ACT.Copy, scale=scale).then_inc(*k.up(f"free_a{b}"))

            def flat(t):
                return t.rearrange("p a b -> p (a b)")

            def exps(maps, joint=False):
                for m in maps:
                    for i in range(2):
                        bias = nmax[:, i:i + 1] if joint else nmax[:, 2 * m + i:2 * m + i + 1]
                        ins = f(pr[:, m, i, :], pr[:, m, i, :], ACT.Exp, bias=bias,
                                accum_out=ssum[:, 2 * m + i:2 * m + i + 1])
                        last = m == maps[-1] and i == 1
                        ins.then_inc(*k.up("exped" if last else "act"))

            def probs_out(maps, n_blocks=3):
                for m in maps:
                    take(2 + m)
                    w = n_blocks * P
                    f(pt[:, m, 0:w], ps[:, 2 + m, 0:w], ACT.Copy).then_inc(*k.up(f"free_a{2 + m}"))

            act.wait_ge(S["params_in"], 16)
            act.wait_ge(S["table_ready"], 1)
            f(small[:, 4:8], p_col("lambda", 0, 4), ACT.Abs).then_inc(*k.up("act"))
            own()
            f(small[:, 4:8], small[:, 4:8], ACT.Exp, scale=-1.0).then_inc(*k.up("lam_a"))
            act.wait_ge(*k.next("lam_b"))
            f(small[:, 4:8], small[:, 4:8], ACT.Ln).then_inc(*k.up("lam_a"))
            act.wait_ge(*k.next("lam_b"))
            f(small[:, 50:52], small[:, 48:50], ACT.Exp).then_inc(*k.up("lam_a"))
            norm(hT, (S["x_in"], 16))
            split(0)

            for ct in range(4):
                split(2 * ct + 1)
                if ct < 3:
                    split(2 * ct + 2)
                else:
                    split(0)
                take(1)
                f(gg[:, ct, :], ps[:, 1, 0:T], ACT.Gelu_apprx_tanh).then_inc(*k.up("free_a1"))
                for b, dst, bias in ((2, rr, "ba"), (3, ii, "bx")):
                    take(b)
                    f(dst[:, ct, :], ps[:, b, 0:T], ACT.Sigmoid, bias=p_col(bias, ct)).then_inc(*k.up(f"free_a{b}"))
            act.wait_ge(*k.next("lam_b"))
            own()
            for ct in range(4):
                f(aa[:, ct, :], rr[:, ct, :], ACT.Exp, scale=small[:, ct:ct + 1]).then_inc(*k.up("act"))
            for ct in range(4):
                f(tt[:, ct, :], rr[:, ct, :], ACT.Tanh, scale=small[:, 8 + ct:9 + ct])\
                    .then_inc(*k.up("lru_exp" if ct == 3 else "act"))
            act.wait_ge(*k.next("lru_m"))
            f(rr[:], rr[:], ACT.Sqrt).then_inc(*k.up("lru_s"))

            def diff_out():
                probs_out([0])
                act.wait_ge(*k.next("a_ms"))
                f(small[:, 54:56], small[:, 54:56], ACT.Sqrt).then_inc(*k.up("a_sd"))

            with k.loop("diff", act, 2):
                for hh in range(2):
                    split(3 * hh + 1)
                    evac(0, qs[:, 0], 64.0 ** -0.5)
                    split(3 * hh + 2)
                    evac(1, ks[:, 0])
                    split((3 * hh + 3) % 6)
                    evac(0, flat(vs[:, hh]))
                    if hh == 1:
                        diff_out()
                    act.wait_ge(*k.next("scored"))
                    exps([0, 1])
                diff_out()

            f(small_h[:, 0:4 * KC], p_col("w_cf", 0, 4 * KC), ACT.Copy).then_inc(*k.up("small_hi"))
            act.wait_ge(*k.next("lsm_a"))
            f(small[:, 24:32], small[:, 16:24], ACT.Abs).then_inc(*k.up("act"))
            own()
            f(small[:, 24:32], small[:, 24:32], ACT.Exp, scale=-1.0).then_inc(*k.up("lsm_b"))
            act.wait_ge(*k.next("lsm_a"))
            f(small[:, 24:32], small[:, 24:32], ACT.Ln).then_inc(*k.up("lsm_b"))

            with k.loop("fox", act, 2):
                for hh in range(2):
                    split(3 * hh + 1)
                    evac(0, qs[:, 0], 128.0 ** -0.5)
                    split(3 * hh + 2)
                    evac(1, ks[:, 0])
                    split((3 * hh + 3) % 6)
                    evac(0, flat(vs[:, hh]))
                    if hh == 1:
                        probs_out([0])
                    act.wait_ge(*k.next("scored"))
                    exps([0])
                probs_out([0])

            split(1)
            take(0)
            own()
            for g in range(2):
                for h in range(2):
                    last = f(ks[64 * h:64 * h + 64, 1 + g, :], ps[64 * g:64 * g + 64, 0, 0:T], ACT.Copy)
                    last.then_inc(*k.up("free_a0" if g + h == 2 else "act"))
            split(2)
            evac(1, flat(vs[:, 0]))
            for pair in range(4):
                split((3 + pair) % 6)
                evac(pair % 2, qs[:, 0], 64.0 ** -0.5)
                if pair:
                    probs_out([0, 1])
                act.wait_ge(*k.next("scored"))
                for m in range(2):
                    for i in range(2):
                        f(small[:, 40 + 2 * m + i:41 + 2 * m + i], p_col("sinks", 2 * pair + m), ACT.Exp,
                          bias=nmax[:, 2 * m + i:2 * m + i + 1]).then_inc(*k.up("act"))
                exps([0, 1])
            probs_out([0, 1])

            with k.loop("mix", act, KC // 2) as i:
                for jj in range(2):
                    for n in range(4):
                        split((5 * jj + n + 1) % 10)
                        take(n)
                        f(gt[:, 4 * jj + n, :], ps[:, n, 0:T], ACT.Sigmoid,
                          bias=p_dyn("b_gate", i * 2 + (KC * n + jj))).then_inc(*k.up(f"free_a{n}"))
                    own()
                    f(small[:, 60:61], ones[:, 0:1], ACT.Copy).then_inc(*k.up("gate_ready"))
                    split((5 * jj + 5) % 10)
            residual(mixT, "out", KC // 2)
            norm(hT)
            with k.loop("ffn", act, FT // 2):
                for n in range(2):
                    split(2 * n + 1)
                    take(n)
                    f(gt2[:, n, :], ps[:, n, 0:T], ACT.Silu).then_inc(*k.up(f"free_a{n}"))
                    own()
                    f(small[:, 60:61], ones[:, 0:1], ACT.Copy).then_inc(*k.up("gate_ready"))
                    split((2 * n + 2) % 4)
            residual(hidT, "down", FT // 2)
            norm(hT, parts=False)

            norm(hT)
            with k.loop("dil", act, 2):
                for hh in range(2):
                    for g in range(3):
                        c = 9 * hh + 3 * g
                        split(c + 1)
                        evac(c % 2, qs[:, g], 128.0 ** -0.5)
                        split(c + 2)
                        evac((c + 1) % 2, ks[:, g])
                        split((c + 3) % 18)
                        evac(c % 2, flat(vs[:, 3 * hh + g]))
                        if hh == 1 and g == 0:
                            probs_out([0, 1, 2])
                    act.wait_ge(*k.next("scored"))
                    exps([0, 1, 2], joint=True)
                probs_out([0, 1, 2])

            def spread(b, dst):
                take(b)
                for g in range(2):
                    for h in range(2):
                        last = f(dst[64 * h:64 * h + 64, g, :], ps[64 * g:64 * g + 64, b, 0:T], ACT.Copy)
                        last.then_inc(*k.up(f"free_a{b}" if g + h == 2 else "act"))

            split(1)
            evac(0, kcv[:, 0])
            split(2)
            evac(1, kcv[:, 1])
            split(3)
            spread(0, kd[:, 0])
            split(4)
            evac(1, flat(vs[:, 0]))
            split(5)
            spread(0, kd[:, 1])
            split(0)
            evac(1, flat(vs[:, 1]))
            own()
            f(small[:, 60:61], ones[:, 0:1], ACT.Copy).then_inc(*k.up("kv_ready"))
            act.wait_ge(S["small_in"], 48)
            f(small_h[:], small_w[:], ACT.Copy).then_inc(*k.up("small_hi"))
            take(7)
            f(bg2[:], ps[:, 7, 0:P].rearrange("p (i c) -> p i c", i=2)[:, :, 0:48],
              ACT.Sigmoid).then_inc(*k.up("free_a7"))
            own()
            for kv in range(2):
                for g in range(2):
                    take(5 + g)
                    f(hid_c[:, g, 0:C_CMP], ps[:, 5 + g, 0:C_CMP],
                      ACT.Gelu_apprx_tanh).then_inc(*k.up(f"free_a{5 + g}"))
                own()
                f(small[:, 60:61], ones[:, 0:1], ACT.Copy).then_inc(*k.up("cmp_hid"))
                if kv == 0:
                    act.wait_ge(*k.next("cmp_s"))

            def nsa_out():
                probs_out([0, 1, 2, 3])
                take(7)
                f(flat(ptc[0:C_CMP, :, :]), ps[0:C_CMP, 7, :], ACT.Copy).then_inc(*k.up("free_a7"))

            for g in range(2):
                with k.loop(f"nsa{g}", act, 2):
                    for pp in range(2):
                        split((pp + 1) % 2)
                        evac(pp, qs[:, 0], 64.0 ** -0.5)
                        if pp == 1:
                            nsa_out()
                        act.wait_ge(*k.next("scored"))
                        f(sc[:, :, :, 0:C_CMP], sc[:, :, :, 0:C_CMP], ACT.Exp).then_inc(*k.up("act"))
                        exps([0, 1, 2, 3])
                    nsa_out()

            with k.loop("mix2", act, KC // 2):
                for jj in range(2):
                    for n in range(2):
                        split((3 * jj + n + 1) % 6, 12 * P if n == 1 else D)
                        take(n)
                        f(gt[:, 4 * jj + n, :], ps[:, n, 0:T], ACT.Sigmoid).then_inc(*k.up(f"free_a{n}"))
                    own()
                    f(small[:, 60:61], ones[:, 0:1], ACT.Copy).then_inc(*k.up("gate_ready"))
                    split((3 * jj + 3) % 6)
            residual(mixT, "out2", KC // 2)
            act.wait_ge(*k.next("h_ready"))
            norm(memT, (S["mem_in"], 16))
            with k.loop("mem_kv", act, 4) as h:
                split(1)
                evac(0, dyn(kx, h))
                split(0)
                evac(1, vx[:, bass.ds(h, 1), :, :].rearrange("p o a b -> p (o a b)"))
            norm(hT)
            for h in range(4):
                split((h + 1) % 4)
                evac(h % 2, qs[:, 0], 128.0 ** -0.5)
                if h:
                    probs_out([0], 4)
                act.wait_ge(*k.next("scored"))
                exps([0])
            probs_out([0], 4)
            residual(yx, "xo", 2)
            norm(hT)
            with k.loop("pq", act, 8):
                split(1)
                evac(0, qt[:, 0])
                split(0)
                evac(1, qt[:, 1])
            with k.loop("u0", act, 8) as i:
                for j in range(HALF // 8):
                    split((j + 1) % 8)
                    take(j % 2)
                    f(dyn(ag, i * 8 + j), ps[:, j % 2, 0:T], ACT.Gelu_apprx_tanh).then_inc(*k.up(f"free_a{j % 2}"))
            act.wait_ge(*k.next("top_m"))
            f(etab[:, 2], etab[:, 2], ACT.Exp).then_inc(*k.up("top_e"))
            residual(ag, "v0", HALF // 2)
            act.wait_ge(*k.next("h_ready"))
            with k.loop("route1", act, 16) as i:
                for b in range(2):
                    take(2 + b)
                    f(ag[:, :, bass.ds(i * 16 + 8 * b, 8)], ps[:, 2 + b, :].rearrange("p (s e) -> p e s", s=8),
                      ACT.Copy).then_inc(*k.up(f"free_a{2 + b}"))
            own()
            f(small[:, 60:61], ones[:, 0:1], ACT.Copy).then_inc(*k.up("g_stored"))
            with k.loop("u1", act, HALF // 2):
                for b in range(2):
                    split((b + 1) % 2)
                    take(b)
                    act.wait_ge(*k.next("gate_free"))
                    f(gt3[:, b, :], ps[:, b, 0:T], ACT.Gelu_apprx_tanh).then_inc(*k.up(f"free_a{b}"))
                    own()
                    f(small[:, 60:61], ones[:, 0:1], ACT.Copy).then_inc(*k.up("gate_ready"))
            residual(ag, "v1", HALF // 2, more=False)
            norm(hT, parts=False)
        @block.vector
        def _(dve):
            k = Counts("DVE", S, found)
            v = nc.vector

            def own():
                dve.wait_ge(*k.own())

            def take(b):
                dve.wait_ge(S[f"full_v{b}"], k.at(f"free_v{b}", 1))

            def flag(key):
                own()
                v.memset(small[:, 63:64], 0.0).then_inc(*k.up(key))

            def step(ins):
                ins.then_inc(*k.up("dve"))
                own()

            def split(j, width=D):
                dve.wait_ge(*k.next(f"land{j % RING}", 16))
                dve.wait_ge(S["hi"], k.at("lo", 1))
                w = slice(0, width)
                v.tensor_tensor(wl[:, j % 2, w], raw[:, j % RING, w], wh[:, j % 2, w].bitcast(F32),
                                ALU.subtract).then_inc(*k.up("lo"))

            def xsplit(j, src, n):
                dve.wait_ge(*k.next("xkh_ready"))
                v.tensor_tensor(xkl[:, j % 2, :], dyn(src, n), xkh[:, j % 2, :].bitcast(F32),
                                ALU.subtract).then_inc(*k.up("xkl_ready"))

            def residual(src, name, turns, more=True):
                flag("src_ready")
                xsplit(0, src, 0)
                split(1)
                xsplit(1, src, 1)
                split(0)
                xsplit(0, src, 2)
                if turns > 2:
                    with k.loop(name, dve, turns - 2) as i:
                        split(1)
                        xsplit(1, src, i * 2 + 3)
                        split(0)
                        xsplit(0, src, i * 2 + 4)
                split(1)
                xsplit(1, src, 2 * turns - 1)
                if more:
                    split(0)
                for b in range(8):
                    take(b)
                    h = hT[:, 2 * b:2 * b + 2, :]
                    v.tensor_tensor(h, h, ps[:, b, :].rearrange("p (a t) -> p a t", a=2),
                                    ALU.add).then_inc(*k.up(f"free_v{b}"))
                flag("h_ready")

            def norm(src, gain, dst=None):
                take(7)
                v.tensor_scalar(rstd[:], ps[:, 7, 0:T], 1.0 / D, EPS, ALU.mult, ALU.add)\
                    .then_inc(*k.up("free_v7"))
                flag("rs_var")
                dve.wait_ge(*k.next("rs_std"))
                step(v.reciprocal(rstd[:], rstd[:]))
                for q in range(4):
                    for kc in range(4 * q, 4 * q + 4):
                        o = tmp if dst is None else dst
                        v.scalar_tensor_tensor(o[:, kc, :], src[:, kc, :], p_col(gain, kc), rstd[:],
                                               ALU.mult, ALU.mult).then_inc(*k.up("dve"))
                    if dst is None:
                        flag("tmp_ready")
                if dst is None:
                    for q in range(4):
                        c = slice(4 * q, 4 * q + 4)
                        dve.wait_ge(*k.next("xh_ready"))
                        v.tensor_tensor(xl[:, c, :], tmp[:, c, :], xh[:, c, :].bitcast(F32),
                                        ALU.subtract).then_inc(*k.up("xl_ready"))

            def slope(i):
                return p_col("slopes", i) if isinstance(i, int) else p_dyn("slopes", i)

            def score(m, mask, slope_col):
                take(2 + m)
                v.scalar_tensor_tensor(pr[:, m], mask, slope_col, ps[:, 2 + m, :].rearrange("p (i s) -> p i s", i=2),
                                       ALU.mult, ALU.add).then_inc(*k.up(f"free_v{2 + m}"))

            def maxima(n):
                own()
                v.tensor_reduce(nmax[:, 0:2 * n], pr[:, 0:n].rearrange("p m i s -> p (m i) s"), AX.X, ALU.max,
                                negate=True)

            def bring_max(n, key="scored"):
                own()
                v.tensor_reduce(nmax[:, 0:2 * n], pr[:, 0:n].rearrange("p m i s -> p (m i) s"), AX.X, ALU.max,
                                negate=True).then_inc(*k.up(key))

            def normalise(n, key="normed"):
                rows = pr[:, 0:n].rearrange("p m i s -> p (m i) s")
                v.tensor_tensor(rows, rows, rinv[:, 0:2 * n].unsqueeze(2).to_broadcast([P, 2 * n, T]),
                                ALU.mult).then_inc(*k.up(key))

            def take_y(b, n, lo=0):
                take(b)
                src = ps[:, b, 0:T]
                step(v.tensor_copy(dyn(yh, n), src))
                v.tensor_tensor(dyn(yl, n), src, dyn(yh, n).bitcast(F32), ALU.subtract).then_inc(*k.up(f"free_v{b}"))
                flag("y_ready")

            dve.wait_ge(S["params_in"], 16)
            dve.wait_ge(S["table_ready"], 1)
            dve.wait_ge(*k.next("lam_a"))
            step(v.tensor_scalar(small[:, 4:8], small[:, 4:8], 1.0, None, ALU.add))
            flag("lam_b")
            for j in range(2):
                step(v.tensor_tensor_reduce(gln[:, 0:64], p_col(f"lq{j + 1}", 0, 64), p_col(f"lk{j + 1}", 0, 64),
                                            1.0, 0.0, ALU.mult, ALU.add, small[:, 48 + j:49 + j]))
            flag("lam_b")
            dve.wait_ge(*k.next("lam_a"))
            step(v.tensor_scalar(small[:, 0:4], p_col("lambda", 0, 4), -1.0, 0.0, ALU.mult, ALU.max))
            step(v.tensor_tensor(small[:, 0:4], small[:, 0:4], small[:, 4:8], ALU.add))
            step(v.tensor_scalar(small[:, 8:12], small[:, 0:4], 8.0, None, ALU.mult))
            step(v.tensor_scalar(small[:, 0:4], small[:, 0:4], -8.0, None, ALU.mult))
            flag("lam_b")
            dve.wait_ge(*k.next("lam_a"))
            step(v.tensor_tensor(small[:, 52:53], small[:, 51:52], small[:, 50:51], ALU.subtract))
            step(v.tensor_scalar(small[:, 52:53], small[:, 52:53], -LAM_INIT, None, ALU.add))
            step(v.tensor_scalar(gln[:], p_col("subln", 0, P), 1.0 - LAM_INIT, None, ALU.mult))
            norm(hT, "norm_mix")
            split(0)

            step(v.memset(xpad[:], 0.0))
            for ct in range(4):
                split(2 * ct + 1)
                take(0)
                v.tensor_copy(xpad[:, 3:3 + T], ps[:, 0, 0:T]).then_inc(*k.up("free_v0"))
                own()
                x3 = [xpad[:, j:j + T] for j in range(4)]
                step(v.tensor_scalar(xc[:, ct, :], x3[3], p_col("conv_w", 12 + ct), p_col("conv_b", ct),
                                     ALU.mult, ALU.add))
                for j in (2, 1):
                    step(v.scalar_tensor_tensor(xc[:, ct, :], x3[j], p_col("conv_w", 4 * j + ct), xc[:, ct, :],
                                                ALU.mult, ALU.add))
                v.scalar_tensor_tensor(xc[:, ct, :], x3[0], p_col("conv_w", ct), xc[:, ct, :],
                                       ALU.mult, ALU.add).then_inc(*k.up("conv_ready"))
                own()
                split((2 * ct + 2) % 8)
            dve.wait_ge(*k.next("lru_exp"))
            step(v.tensor_tensor(ii[:], ii[:], xc[:], ALU.mult))
            step(v.tensor_tensor(rr[:], aa[:], aa[:], ALU.mult))
            v.scalar_tensor_tensor(rr[:], rr[:], 1.0, tt[:], ALU.add, ALU.mult).then_inc(*k.up("lru_m"))
            dve.wait_ge(*k.next("lru_s"))
            step(v.tensor_tensor(ii[:], ii[:], rr[:], ALU.mult))
            for ct in range(4):
                v.tensor_tensor_scan(xc[:, ct, :], aa[:, ct, :], ii[:, ct, :], 0.0, ALU.mult,
                                     ALU.add).then_inc(*k.up("dve"))
            own()
            step(v.tensor_tensor(tt[:], gg[:], xc[:], ALU.mult))
            step(v.tensor_copy(yh[:, 4:8, :], tt[:]))
            step(v.tensor_tensor(yl[:, 4:8, :], tt[:], yh[:, 4:8, :].bitcast(F32), ALU.subtract))
            for ct in range(4):
                flag("y_ready")

            def diff_end(h):
                take(6)
                v.tensor_copy(ysb[:], ps[:, 6, 0:T].rearrange("p (i e) -> p i e", i=2)).then_inc(*k.up("free_v6"))
                own()
                for i in range(2):
                    step(v.tensor_tensor_reduce(mscr[:], ysb[:, i, :], ysb[:, i, :], 1.0, 0.0, ALU.mult,
                                                ALU.add, small[:, 54 + i:55 + i]))
                v.tensor_scalar(small[:, 54:56], small[:, 54:56], 1.0 / P, EPS, ALU.mult,
                                ALU.add).then_inc(*k.up("a_ms"))
                dve.wait_ge(*k.next("a_sd"))
                step(v.reciprocal(small[:, 56:58], small[:, 54:56]))
                for i in range(2):
                    v.scalar_tensor_tensor(ysb[:, i, :], ysb[:, i, :], small[:, 56 + i:57 + i], gln[:],
                                           ALU.mult, ALU.mult).then_inc(*k.up("dve" if i == 0 else "a_y"))
                take_y(7, h)

            with k.loop("diff", dve, 2) as t:
                for hh in range(2):
                    split(3 * hh + 1)
                    split(3 * hh + 2)
                    split((3 * hh + 3) % 6)
                    if hh == 1:
                        diff_end(t * 2)
                    for m in range(2):
                        score(m, nd_causal[:], slope(t * 2 + (SLOPE_A + hh)))
                    bring_max(2)
                    dve.wait_ge(*k.next("exped"))
                    step(v.reciprocal(rinv[:, 0:4], ssum[:, 0:4]))
                    step(v.tensor_scalar(rinv[:, 2:4], rinv[:, 2:4], small[:, 52:53], None, ALU.mult))
                    normalise(2, "dve")
                    own()
                    v.tensor_tensor(pr[:, 0], pr[:, 0], pr[:, 1], ALU.add).then_inc(*k.up("normed"))
                diff_end(t * 2 + 1)

            dve.wait_ge(*k.next("small_hi"))
            v.tensor_tensor(small_l[:, 0:4 * KC], p_col("w_cf", 0, 4 * KC), small_h[:, 0:4 * KC].bitcast(F32),
                            ALU.subtract).then_inc(*k.up("small_lo"))
            take(7)
            v.tensor_tensor(small[:, 16:24].rearrange("p (i h) -> p i h", i=2),
                            ps[:, 7, 0:P].rearrange("p (i c) -> p i c", i=2)[:, :, 0:4],
                            p_col("fox_b_f", 0, 4).unsqueeze(1).to_broadcast([P, 2, 4]),
                            ALU.add).then_inc(*k.up("free_v7"))
            flag("lsm_a")
            dve.wait_ge(*k.next("lsm_b"))
            step(v.tensor_scalar(small[:, 24:32], small[:, 24:32], 1.0, None, ALU.add))
            flag("lsm_a")
            dve.wait_ge(*k.next("lsm_b"))
            step(v.tensor_scalar(small[:, 16:24], small[:, 16:24], 0.0, None, ALU.min))
            v.tensor_tensor(cumq[:, 8:16], small[:, 16:24], small[:, 24:32], ALU.subtract)\
                .then_inc(*k.up("lsm_c"))
            take(7)
            v.tensor_copy(cumq[:, 0:8], ps[:, 7, 0:8]).then_inc(*k.up("free_v7"))
            own()

            with k.loop("fox", dve, 2) as t:
                for hh in range(2):
                    h = t * 2 + hh
                    lf = cumq[:, 8:16].rearrange("p (s h) -> p h s", s=2)[:, bass.ds(h, 1), :]
                    v.tensor_scalar(cumq[:, 16:18], lf.rearrange("p o s -> p (o s)"), -1.0, None, ALU.mult)\
                        .then_inc(*k.up("cum_ready"))
                    split(3 * hh + 1)
                    split(3 * hh + 2)
                    split((3 * hh + 3) % 6)
                    if hh == 1:
                        take_y(6, t * 2 + 8)
                    take(2)
                    for i in range(2):
                        cq = cumq[:, bass.ds(h + 4 * i, 1)]
                        v.scalar_tensor_tensor(pr[:, 0, i, :], ps[:, 2, i * T:(i + 1) * T], cq, nd2[:, 1, i, :],
                                               ALU.add, ALU.add).then_inc(*k.up("free_v2" if i else "dve"))
                    bring_max(1)
                    dve.wait_ge(*k.next("exped"))
                    step(v.reciprocal(rinv[:, 0:2], ssum[:, 0:2]))
                    normalise(1)
                    own()
                take_y(6, t * 2 + 9)

            step(v.tensor_scalar(small[:, 12:20], p_col("sinks", 0, 8), -1.0, None, ALU.mult))
            split(1)
            split(2)
            for pair in range(4):
                split((3 + pair) % 6)
                if pair:
                    take_y(6, 12 + pair - 1)
                for m in range(2):
                    score(m, nd2[:, 0], slope(SLOPE_D + 2 * pair + m))
                bring_max(2, "dve")
                own()
                for m in range(2):
                    c = slice(2 * m, 2 * m + 2)
                    v.tensor_scalar(nmax[:, c], nmax[:, c], small[:, 12 + 2 * pair + m:13 + 2 * pair + m], None,
                                    ALU.min).then_inc(*k.up("scored" if m else "dve"))
                dve.wait_ge(*k.next("exped"))
                step(v.tensor_tensor(rinv[:, 0:4], ssum[:, 0:4], small[:, 40:44], ALU.add))
                step(v.reciprocal(rinv[:, 0:4], rinv[:, 0:4]))
                normalise(2)
                own()
            take_y(6, 15)
            flag("masks_free")

            def mixed(j, jj, n_gates, banks):
                dve.wait_ge(*k.next("gate_ready"))
                for n in range(n_gates):
                    take(banks[n])
                    o = dyn(mixT, j) if n == 0 else mtmp[:]
                    v.tensor_tensor(o, gt[:, 4 * jj + n, :], ps[:, banks[n], 0:T],
                                    ALU.mult).then_inc(*k.up(f"free_v{banks[n]}"))
                    own()
                    if n:
                        step(v.tensor_tensor(dyn(mixT, j), dyn(mixT, j), mtmp[:], ALU.add))

            with k.loop("mix", dve, KC // 2) as i:
                for jj in range(2):
                    for n in range(5):
                        split((5 * jj + n + 1) % 10)
                    mixed(i * 2 + jj, jj, 4, (4, 5, 6, 7))
            residual(mixT, "out", KC // 2)
            norm(hT, "norm_ffn")
            with k.loop("ffn", dve, FT // 2) as i:
                for n in range(2):
                    split(2 * n + 1)
                    split((2 * n + 2) % 4)
                    dve.wait_ge(*k.next("gate_ready"))
                    take(4 + n)
                    v.tensor_tensor(dyn(hidT, i * 2 + n), gt2[:, n, :], ps[:, 4 + n, 0:T],
                                    ALU.mult).then_inc(*k.up(f"free_v{4 + n}"))
            residual(hidT, "down", FT // 2)
            norm(hT, "norm_final", hT)
            flag("h_ready")

            norm(hT, "norm_mix_2")
            dve.wait_ge(S["table_ready"], 2)
            for j, dil in ((1, 4), (2, 16)):
                step(v.tensor_scalar(dist_m[:], dist_i[:], dil - 1, None, ALU.bitwise_and))
                step(v.tensor_scalar(mask_f[:], dist_m[:], 0.0, None, ALU.is_equal))
                step(v.tensor_scalar(mask_f[:], mask_f[:], -NEG, NEG, ALU.mult, ALU.add))
                step(v.tensor_tensor(nd2[:, j], nd2[:, j], mask_f[:], ALU.add))

            with k.loop("dil", dve, 2) as t:
                for hh in range(2):
                    for g in range(3):
                        for n in range(3):
                            split((9 * hh + 3 * g + n + 1) % 18)
                        if hh == 1 and g == 0:
                            take_y(6, t * 2)
                        score(g, nd2[:, g], slope(t * 2 + (SLOPE_DIL + 4 * g + hh)))
                    own()
                    v.tensor_reduce(nmax[:, 0:2], pr[:, 0:3].rearrange("p m i s -> p i m s"), AX.XY, ALU.max,
                                    negate=True).then_inc(*k.up("scored"))
                    dve.wait_ge(*k.next("exped"))
                    step(v.tensor_reduce(rinv[:, 0:2], ssum[:, 0:6].rearrange("p (m i) -> p i m", m=3), AX.X,
                                         ALU.add))
                    step(v.reciprocal(rinv[:, 0:2], rinv[:, 0:2]))
                    for m in range(3):
                        v.tensor_tensor(pr[:, m], pr[:, m], rinv[:, 0:2].unsqueeze(2).to_broadcast([P, 2, T]),
                                        ALU.mult).then_inc(*k.up("normed" if m == 2 else "dve"))
                    own()
                take_y(6, t * 2 + 1)

            flag("w1_free")
            for j in range(6):
                split((j + 1) % 6)
            dve.wait_ge(*k.next("small_hi"))
            v.tensor_tensor(small_l[:], small_w[:], small_h[:].bitcast(F32),
                            ALU.subtract).then_inc(*k.up("small_lo"))
            dve.wait_ge(*k.next("kv_ready"))
            for kv, pe_name in ((0, "pe_k"), (1, "pe_v")):
                src = kcv[:, kv].rearrange("p (c b) -> p b c", b=16)
                for a in range(2):
                    v.tensor_tensor(xw[:, 16 * a:16 * a + 16, :], src[:, :, a:a + C_CMP],
                                    p_col(pe_name, 16 * a, 16).unsqueeze(2).to_broadcast([P, 16, C_CMP]),
                                    ALU.add).then_inc(*k.up("cmp_in" if a else "dve"))
                take(7)
                if kv == 0:
                    v.tensor_copy(kcd[:, :, 0:C_CMP],
                                  ps[:, 7, 0:32].rearrange("p (g c) -> p g c", g=2)[:, :, 0:C_CMP])\
                        .then_inc(*k.up("free_v7"))
                    flag("w1_free")
                    flag("cmp_s")
                else:
                    v.tensor_copy(vcd[0:C_CMP, :, :],
                                  ps[0:C_CMP, 7, 0:P].rearrange("p (g c) -> p g c", g=2))\
                        .then_inc(*k.up("free_v7"))
                    own()
            step(v.memset(pc[:], 0.0))
            flag("kv2_ready")

            def softmax_cmp(h0, hh_off):
                s4 = sc[:, :, :, 0:C_CMP]
                ok = ok_cmp[:].unsqueeze(1).to_broadcast([P, 2, 2, C_CMP])
                step(v.tensor_tensor(s4, s4, ok, ALU.mult))
                step(v.tensor_reduce(small[:, 44:48].rearrange("p (a b) -> p a b", a=2), s4, AX.X, ALU.add))
                step(v.tensor_scalar(small[:, 44:48], small[:, 44:48], 1e-30, None, ALU.max))
                step(v.reciprocal(small[:, 44:48], small[:, 44:48]))

            for g in range(2):
                with k.loop(f"nsa{g}", dve, 2) as t:
                    for pp in range(2):
                        split((pp + 1) % 2)
                        if pp == 1:
                            take_y(6, t * 2 + (4 + 4 * g))
                        head = [t * 4 + (8 * g + 2 * pp + hh) for hh in range(2)]
                        for hh in range(2):
                            for br in range(2):
                                score(2 * hh + br, nd_causal[:], slope(head[hh] + SLOPE_B))
                        for hh in range(2):
                            take(6 + hh)
                            v.scalar_tensor_tensor(
                                sc[:, hh, :, 0:C_CMP], nd_cmp[:], slope(head[hh] + SLOPE_B),
                                ps[:, 6 + hh, 0:32].rearrange("p (i c) -> p i c", i=2)[:, :, 0:C_CMP],
                                ALU.mult, ALU.add).then_inc(*k.up(f"free_v{6 + hh}"))
                        own()
                        s4 = sc[:, :, :, 0:C_CMP]
                        m4 = small[:, 40:44].rearrange("p (a b) -> p a b", a=2)
                        step(v.tensor_reduce(m4, s4, AX.X, ALU.max))
                        step(v.tensor_tensor(s4, s4, m4.unsqueeze(3).to_broadcast([P, 2, 2, C_CMP]),
                                             ALU.subtract))
                        bring_max(4)
                        dve.wait_ge(*k.next("exped"))
                        step(v.reciprocal(rinv[:], ssum[:]))
                        softmax_cmp(0, 0)
                        gates = bg2[:].rearrange("p i (h b) -> p h b i", b=3)
                        for hh in range(2):
                            r4 = rinv[:, 4 * hh:4 * hh + 4].rearrange("p (b i) -> p b i", b=2)
                            gh = gates[:, bass.ds(head[hh], 1), :, :].rearrange("p o b i -> p (o b) i")
                            step(v.tensor_tensor(r4, r4, gh[:, 1:3, :], ALU.mult))
                            c2 = small[:, 44 + 2 * hh:46 + 2 * hh]
                            step(v.tensor_tensor(c2, c2, gh[:, 0, :], ALU.mult))
                        step(v.tensor_tensor(
                            pc[:, :, :, 0:C_CMP], s4,
                            small[:, 44:48].rearrange("p (a b) -> p a b", a=2).unsqueeze(3)
                            .to_broadcast([P, 2, 2, C_CMP]), ALU.mult))
                        normalise(4)
                        own()
                    take_y(6, t * 2 + (5 + 4 * g))

            with k.loop("mix2", dve, KC // 2) as i:
                for jj in range(2):
                    for n in range(3):
                        split((3 * jj + n + 1) % 6, 12 * P if n == 1 else D)
                    mixed(i * 2 + jj, jj, 2, (4, 5))
            flag("w1_free")
            residual(mixT, "out2", KC // 2)
            norm(memT, "norm_mem_2")
            with k.loop("mem_kv", dve, 4):
                split(1)
                split(0)
            flag("h_ready")
            norm(hT, "norm_x_2")
            for h in range(4):
                split((h + 1) % 4)
                if h:
                    take(6)
                    v.tensor_copy(yx[:, h - 1, :], ps[:, 6, 0:T]).then_inc(*k.up("free_v6"))
                take(2)
                v.tensor_copy(pr[:, 0], ps[:, 2, :].rearrange("p (i s) -> p i s", i=2)).then_inc(*k.up("free_v2"))
                bring_max(1)
                dve.wait_ge(*k.next("exped"))
                step(v.reciprocal(rinv[:, 0:2], ssum[:, 0:2]))
                normalise(1)
                own()
            take(6)
            v.tensor_copy(yx[:, 3, :], ps[:, 6, 0:T]).then_inc(*k.up("free_v6"))
            residual(yx, "xo", 2)
            flag("w1_free")
            norm(hT, "norm_ffn_2")
            with k.loop("pq", dve, 8) as h:
                split(1)
                split(0)
                take(2)
                v.tensor_copy(dyn(svs, h), ps[:, 2, :]).then_inc(*k.up("free_v2"))

            def own_then_max():
                own()
                v.memset(small[:, 62:63], 0.0).then_inc(*k.up("dve"))

            def first8(rows, vals, n):
                own_then_max()
                for r in range(n):
                    v.max(vals[:, r, 0:8], rows[:, r, :]).then_inc(*k.up("dve"))
                own()

            def without8(rows, scratch, vals, idx, n):
                own_then_max()
                for r in range(n):
                    v.max_index(idx[:, r, 0:8], vals[:, r, 0:8], rows[:, r, :]).then_inc(*k.up("dve"))
                    v.match_replace(scratch[:, r, :], vals[:, r, 0:8], rows[:, r, :], -3e38).then_inc(*k.up("dve"))
                own()

            def next8(scratch, vals, idx, n):
                own_then_max()
                for r in range(n):
                    v.max(vals[:, r, 8:16], scratch[:, r, :]).then_inc(*k.up("dve"))
                own_then_max()
                for r in range(n):
                    v.max_index(idx[:, r, 8:16], vals[:, r, 8:16], scratch[:, r, :]).then_inc(*k.up("dve"))
                own()

            def pairs(a, b, op, out):
                for i in range(2):
                    v.tensor_tensor(out[:, i, :].rearrange("p (s t) -> p s t", s=TOPK),
                                    a(i).unsqueeze(2).to_broadcast([P, TOPK, TOPK]),
                                    b(i).unsqueeze(1).to_broadcast([P, TOPK, TOPK]), op).then_inc(*k.up("dve"))
                own()

            def numbers(side, h):
                pairs(lambda i: cijf[:, side, i, :], lambda i: iota[:, 0:TOPK], ALU.is_equal, eqb)
                for i in range(2):
                    e = eqb[:, i, :].rearrange("p (s t) -> p s t", s=TOPK)
                    v.tensor_tensor(e, e, itf[:, 2 * i + side, :].unsqueeze(1).to_broadcast([P, TOPK, TOPK]),
                                    ALU.mult).then_inc(*k.up("dve"))
                own()
                for i in range(2):
                    v.tensor_reduce(etab[:, side, i, bass.ds(h * TOPK, TOPK)],
                                    eqb[:, i, :].rearrange("p (s t) -> p s t", s=TOPK), AX.X, ALU.add)\
                        .then_inc(*k.up("dve"))
                own()

            def search(part, h):
                if part == 0:
                    v.tensor_copy(sv[:].rearrange("p r c -> p (r c)"), dyn(svs, h)).then_inc(*k.up("dve"))
                    first8(sv, vtop, 4)
                elif part == 1:
                    without8(sv, sv2, vtop, itop, 4)
                elif part == 2:
                    next8(sv2, vtop, itop, 4)
                elif part == 3:
                    v.tensor_copy(itf[:], itop[:]).then_inc(*k.up("dve"))
                    pairs(lambda i: vtop[:, 2 * i, :], lambda i: vtop[:, 2 * i + 1, :], ALU.add, cand)
                    first8(cand, ctop, 2)
                elif part == 4:
                    without8(cand, cand2, ctop, cidx, 2)
                elif part == 5:
                    next8(cand2, ctop, cidx, 2)
                    v.tensor_tensor(etab[:, 2, :, bass.ds(h * TOPK, TOPK)], ctop[:],
                                    ctop[:, :, 0:1].to_broadcast([P, 2, TOPK]), ALU.subtract).then_inc(*k.up("dve"))
                    v.tensor_scalar(cij[:, 0], cidx[:], 4, None, ALU.logical_shift_right).then_inc(*k.up("dve"))
                    v.tensor_scalar(cij[:, 1], cidx[:], 15, None, ALU.bitwise_and).then_inc(*k.up("dve"))
                    own()
                    step(v.tensor_copy(cijf[:], cij[:]))
                else:
                    numbers(part - 6, h)

            def one_hots(keys, n, b, done):
                tok = bass.ds(n, 8)
                v.tensor_tensor(oh_r[:, b], keys[:, 0:HALF].unsqueeze(1).to_broadcast([P, 8, HALF]),
                                e1t[:, tok].unsqueeze(2).to_broadcast([P, 8, HALF]), ALU.is_equal)\
                    .then_inc(*k.up("dve"))
                v.tensor_tensor(oh_l[:, b], iota[:].unsqueeze(1).to_broadcast([P, 8, P]),
                                e2t[:, tok].unsqueeze(2).to_broadcast([P, 8, P]), ALU.is_equal)\
                    .then_inc(*k.up("dve"))
                own()
                v.tensor_tensor(oh_r[:, b], oh_r[:, b], gtt[:, tok].unsqueeze(2).to_broadcast([P, 8, HALF]),
                                ALU.mult).then_inc(*k.up(done))

            with k.loop("u0", dve, 8) as h:
                for j in range(HALF // 8):
                    split((j + 1) % 8)
                    search(j, h)
            flag("top_m")
            dve.wait_ge(*k.next("top_e"))
            weights = etab[:, 2].rearrange("p i (h s) -> p (i h) s", s=TOPK)
            step(v.tensor_reduce(small[:, 20:36], weights, AX.X, ALU.add))
            step(v.reciprocal(small[:, 20:36], small[:, 20:36]))
            step(v.tensor_tensor(weights, weights, small[:, 20:36].unsqueeze(2).to_broadcast([P, 16, TOPK]),
                                 ALU.mult))
            flag("idx_ready")
            for n, dst in enumerate((e1t, e2t, gtt)):
                take(3 + n)
                v.tensor_copy(dst[:], ps[:, 3 + n, 0:T]).then_inc(*k.up(f"free_v{3 + n}"))
                own()
            with k.loop("route0", dve, 8) as i:
                def weigh(b):
                    take(2 + b)
                    a = ag[:, :, bass.ds(i * 32 + 8 * b, 8)]
                    v.tensor_tensor(a, a, ps[:, 2 + b, :].rearrange("p (s e) -> p e s", s=8), ALU.mult)\
                        .then_inc(*k.up(f"free_v{2 + b}"))

                for b in range(4):
                    one_hots(iota, i * 32 + 8 * b, b % 2, "lr_ready")
                    if b:
                        weigh(b - 1)
                weigh(3)
            residual(ag, "v0", HALF // 2)
            flag("gate_free")
            flag("gate_free")
            with k.loop("route1", dve, 16) as i:
                for b in range(2):
                    dve.wait_ge(S[f"free_a{2 + b}"], i + route_base[b])
                    one_hots(iota_hi, i * 16 + 8 * b, b, "lr_ready")
            dve.wait_ge(*k.next("g_stored"))
            with k.loop("u1", dve, HALF // 2) as i:
                for b in range(2):
                    split((b + 1) % 2)
                    dve.wait_ge(*k.next("gate_ready"))
                    a = dyn(ag, i * 2 + b)
                    v.tensor_tensor(a, a, gt3[:, b, :], ALU.mult).then_inc(*k.up("gate_free"))
            residual(ag, "v1", HALF // 2, more=False)
            norm(hT, "norm_final_2", tmp)
            flag("out_ready")
    return found


def _tiles(w):
    w = np.asarray(w)
    n = w.shape[1] // P
    return np.ascontiguousarray(w.reshape(w.shape[0] // P, P, n, P).transpose(2, 1, 0, 3)).reshape(n, P, w.shape[0])


def _feature_major(a):
    return np.ascontiguousarray(np.asarray(a).reshape(T, KC, P).transpose(2, 1, 0))


def layout(x):
    x = {k: np.asarray(v) for k, v in x.items()}
    w_in, w_in2 = x["w_in"][0], x["w_in_2"][0]
    cf, bg = 4096, 6400
    arrays = {
        "x": _feature_major(x["x"][0]),
        "mem": _feature_major(x["mem_2"][0]),
        "w_in": _tiles(np.concatenate([w_in[:, :cf], w_in[:, cf + 4:]], axis=1)),
        "w_branch": np.ascontiguousarray(
            x["w_branch"][0].reshape(BRANCHES, 4, P, KC, P).transpose(3, 2, 0, 1, 4)).reshape(KC, P, D),
        "w_out": x["w_out"][0].reshape(KC, P, D),
        "w_ffn_gate": _tiles(x["w_ffn_gate"][0]),
        "w_ffn_up": _tiles(x["w_ffn_up"][0]),
        "w_ffn_down": x["w_ffn_down"][0].reshape(FT, P, D),
        "w_in_2": _tiles(np.concatenate([w_in2[:, :bg], w_in2[:, bg + 48:]], axis=1)),
        "w_up_2": _tiles(np.concatenate([x["w_up_a_2"][0], x["w_up_b_2"][0]], axis=0)),
        "w_out_2": x["w_out_2"][0].reshape(KC, P, D),
        "w_xq_2": _tiles(x["w_xq_2"][0]),
        "w_xkv_2": _tiles(x["w_xkv_2"][0]),
        "w_xo_2": x["w_xo_2"][0].reshape(4, P, D),
        "w_pq_2": _tiles(x["w_pq_2"][0]),
        "expert_u_2": np.ascontiguousarray(
            x["expert_u_2"][0].reshape(N_KEYS, P, KC, P).transpose(0, 3, 2, 1)).reshape(N_KEYS, P, D),
        "expert_v_2": x["expert_v_2"][0].reshape(N_KEYS, P, D),
        "sub_keys": np.ascontiguousarray(np.stack([x["sub_keys1_2"][0].T, x["sub_keys2_2"][0].T], axis=1)),
    }
    blocks = np.zeros((P, 2, 4, P), np.float32)
    for g, name in enumerate(("lru_wa", "lru_wx")):
        for n in range(8):
            o = 64 * (n % 2)
            blocks[o:o + 64, g, n // 2, o:o + 64] = x[name][0, n]
    arrays["w_ab"] = blocks
    arrays["w_bgate"] = np.ascontiguousarray(w_in2[:, bg:bg + 48].reshape(KC, P, 48).transpose(1, 0, 2)).reshape(P, -1)
    cmp1 = np.stack([x["w_cmp_k1_2"][0], x["w_cmp_v1_2"][0]]).reshape(2, 32, 64, P).transpose(0, 2, 1, 3)
    arrays["w_cmp1"] = np.concatenate([cmp1, cmp1], axis=1)
    cmp2 = np.stack([x["w_cmp_k2_2"][0], x["w_cmp_v2_2"][0]], axis=1)
    arrays["w_cmp2"] = np.concatenate([cmp2, cmp2], axis=2)

    def col(v):
        return v.reshape(-1, P).T

    def row(v):
        return np.broadcast_to(v.reshape(1, -1), (P, v.size))

    def alibi(n):
        return (2.0 ** (-8.0 * np.arange(1, n + 1) / n)).astype(np.float32)

    def pe_cols(v):
        return np.concatenate([v.T, v.T], axis=0)

    parts = {
        "norm_mix": col(x["norm_mix"][0]), "norm_ffn": col(x["norm_ffn"][0]), "norm_final": col(x["norm_final"]),
        "norm_mix_2": col(x["norm_mix_2"][0]), "norm_x_2": col(x["norm_x_2"][0]),
        "norm_mem_2": col(x["norm_mem_2"][0]), "norm_ffn_2": col(x["norm_ffn_2"][0]),
        "norm_final_2": col(x["norm_final_2"]), "b_gate": col(x["b_gate"][0]),
        "conv_w": col(x["lru_conv_w"][0].reshape(-1)), "conv_b": col(x["lru_conv_b"][0]), "ba": col(x["lru_ba"][0]),
        "bx": col(x["lru_bx"][0]), "lambda": col(x["lru_lambda"][0]), "fox_b_f": row(x["fox_b_f"][0]),
        "sinks": row(x["swa_sinks"][0]), "subln": row(x["diff_subln"][0]), "lq1": row(x["diff_lq1"][0]),
        "lk1": row(x["diff_lk1"][0]), "lq2": row(x["diff_lq2"][0]), "lk2": row(x["diff_lk2"][0]),
        "pe_k": pe_cols(x["pe_cmp_k_2"][0]), "pe_v": pe_cols(x["pe_cmp_v_2"][0]),
        "slopes": row(np.concatenate([alibi(4), alibi(8), alibi(12), alibi(16)])),
        "w_cf": w_in[:, cf:cf + 4].reshape(KC, P, 4).transpose(1, 0, 2).reshape(P, -1),
    }
    arrays["params"] = np.concatenate([parts[name] for name in PARAMS], axis=1)
    return arrays


def kernel(**inputs):
    import concourse.bacc as bacc
    from concourse.bass_utils import run_bass_kernel_spmd

    arrays = {f"in_{name}": np.ascontiguousarray(a) for name, a in layout(inputs).items()}
    nc = bacc.Bacc("TRN2", target_bir_lowering=False, num_devices=1)
    dram = {name[3:]: nc.dram_tensor(name, a.shape, F32, kind="ExternalInput").ap() for name, a in arrays.items()}
    out = nc.dram_tensor("out", (P, KC, T), F32, kind="ExternalOutput").ap()
    wrong = build(nc, dram, out)
    assert not wrong, wrong
    r = run_bass_kernel_spmd(nc, [arrays], core_ids=[0])
    return np.ascontiguousarray(r.results[0]["out"].transpose(2, 1, 0)).reshape(1, T, D)
```

```python
from contextlib import ExitStack, contextmanager
from collections import defaultdict
import math

import numpy as np
import concourse.bass as bass
from concourse import mybir

F32 = mybir.dt.float32
BF16 = mybir.dt.bfloat16
F32R = mybir.dt.float32r
I32 = mybir.dt.int32
U32 = mybir.dt.uint32
ALU = mybir.AluOpType
ACT = mybir.ActivationFunctionType
AX = mybir.AxisListType

P = 128
D = 2048
T = 256
KC = D // P
DFF = 5632
FT = DFF // P
NEG = -1e30
EPS = 1e-6
LAM_INIT = 0.8 - 0.6 * math.exp(-0.0)
RING = 4
BRANCHES = 4
N_KEYS = 128
TOPK = 16
HALF = N_KEYS // 2
C_CMP = 15

PARAMS = {}
_at = 0
for _name, _w in (
    ("norm_mix", KC), ("norm_ffn", KC), ("norm_final", KC), ("norm_mix_2", KC), ("norm_x_2", KC),
    ("norm_mem_2", KC), ("norm_ffn_2", KC), ("norm_final_2", KC), ("b_gate", 64), ("conv_w", 16),
    ("conv_b", 4), ("ba", 4), ("bx", 4), ("lambda", 4), ("fox_b_f", 4), ("sinks", 8), ("subln", 128),
    ("lq1", 64), ("lk1", 64), ("lq2", 64), ("lk2", 64), ("pe_k", 32), ("pe_v", 32), ("slopes", 40),
    ("w_cf", KC * 4),
):
    PARAMS[_name] = (_at, _w)
    _at += _w
N_PARAMS = _at
SLOPE_A, SLOPE_D, SLOPE_DIL, SLOPE_B = 0, 4, 12, 24

A_Q, A_K, A_V, B_X, B_G, C_Q, C_K, C_V, D_Q, D_K, D_V, GATES = 0, 4, 8, 12, 16, 20, 24, 28, 32, 36, 37, 38
Q2, K2, V2, BQ2, BKV2, GATES2 = 0, 12, 24, 36, 44, 50


def weight_stream():
    full = D
    s = []
    s.append(("lru", 1, [("w_in", B_X + ct + 4 * g, 0, full) for ct in range(4) for g in range(2)]))
    s.append(("diff", 1, [("w_in", b + h, 0, full) for h in range(4) for b in (A_Q, A_K, A_V)]))
    s.append(("fox", 1, [("w_in", b + h, 0, full) for h in range(4) for b in (C_Q, C_K, C_V)]))
    s.append(("swa", 1, [("w_in", b, 0, full) for b in (D_K, D_V, D_Q, D_Q + 1, D_Q + 2, D_Q + 3)]))
    s.append(("mix", KC // 2, [x for jj in range(2) for x in
              [("w_in", GATES + KC * n + jj, 2, full) for n in range(4)] + [("w_branch", jj, 2, full)]]))
    s.append(("out0", 1, [("w_out", k, 0, full) for k in range(2)]))
    s.append(("out", KC // 2 - 1, [("w_out", 2 + k, 2, full) for k in range(2)]))
    s.append(("ffn", FT // 2, [(w, k, 2, full) for k in range(2) for w in ("w_ffn_gate", "w_ffn_up")]))
    s.append(("down0", 1, [("w_ffn_down", k, 0, full) for k in range(2)]))
    s.append(("down", FT // 2 - 1, [("w_ffn_down", 2 + k, 2, full) for k in range(2)]))
    s.append(("dil", 1, [("w_in_2", b + 4 * g + h, 0, full) for h in range(4) for g in range(3) for b in (Q2, K2, V2)]))
    s.append(("nsa_kv", 1, [("w_in_2", BKV2 + k, 0, full) for k in range(6)]))
    s.append(("nsa", 1, [("w_in_2", BQ2 + pair, 0, full) for pair in range(8)]))
    s.append(("mix2", KC // 2, [x for jj in range(2) for x in
              [("w_in_2", GATES2 + KC * n + jj, 2, full) for n in range(2)] + [("w_up_2", jj, 2, 12 * P)]]))
    s.append(("out2_0", 1, [("w_out_2", k, 0, full) for k in range(2)]))
    s.append(("out2", KC // 2 - 1, [("w_out_2", 2 + k, 2, full) for k in range(2)]))
    s.append(("mem_kv", 4, [("w_xkv_2", 0, 1, full), ("w_xkv_2", 4, 1, full)]))
    s.append(("cross", 1, [("w_xq_2", k, 0, full) for k in range(4)]))
    s.append(("xo0", 1, [("w_xo_2", k, 0, full) for k in range(2)]))
    s.append(("xo", 1, [("w_xo_2", 2 + k, 0, full) for k in range(2)]))
    s.append(("pq", 8, [("w_pq_2", k, 2, full) for k in range(2)]))
    for half in range(2):
        e = half * HALF
        n = 2 if half else HALF // 8
        s.append((f"u{half}", HALF // n, [("expert_u_2", e + k, n, full) for k in range(n)]))
        s.append((f"v{half}_0", 1, [("expert_v_2", e + k, 0, full) for k in range(2)]))
        s.append((f"v{half}", HALF // 2 - 1, [("expert_v_2", e + 2 + k, 2, full) for k in range(2)]))
    return s


class Counts:

    def __init__(self, engine, sems, found):
        self.engine, self.sems, self.found = engine, sems, found
        self.n = defaultdict(int)
        self.turn, self.per, self.last = None, {}, None
        self.held = {}

    def at(self, key, more=0):
        v = self.n[key] + more
        per = self.per.get(key, 0)
        return v if self.turn is None or not per else self.turn * per + v

    def up(self, key):
        self.n[key] += 1
        self.last = key
        return self.sems[key], 1

    def next(self, key, unit=1):
        self.n["got " + key] += 1
        v = self.at("got " + key)
        return self.sems[key], v * unit

    def own(self):
        return self.sems[self.last], self.at(self.last)

    @contextmanager
    def loop(self, name, eng, turns):
        if self.engine == "PE":
            self.last = None
        if self.last is not None:
            eng.wait_ge(*self.own())
        if turns == 1:
            yield 0
            return
        start = dict(self.n)
        self.per, self.held, self.last = LOOP_COUNTS.get(self.engine + " " + name, {}), {}, None
        with eng.Fori(0, turns) as i:
            self.turn = i
            yield i
            if self.last is not None and self.engine != "PE":
                eng.wait_ge(*self.own())
        added = {k: v - start.get(k, 0) for k, v in self.n.items() if v != start.get(k, 0)}
        if added != self.per:
            self.found[self.engine + " " + name] = added
        for k, v in added.items():
            self.n[k] = start.get(k, 0) + turns * v
        self.turn, self.per, self.held = None, {}, {}


def hold(eng, sem, value):
    if not isinstance(value, int) or value > 0:
        eng.wait_ge(sem, value)


LOOP_COUNTS = {
    "PE mix": {"full_v7": 2, "full_a0": 2, "begun": 10, "full_a1": 2, "full_a2": 2, "full_a3": 2, "full_v6": 2, "full_v4": 2, "full_v5": 2},
    "PE out": {"begun": 2, "got xkl_ready": 2},
    "PE ffn": {"full_a0": 1, "begun": 4, "full_a1": 1, "full_v4": 1, "full_v5": 1},
    "PE down": {"begun": 2, "got xkl_ready": 2},
    "PE mix2": {"full_a0": 2, "begun": 6, "full_a1": 2, "full_v4": 2, "full_v5": 2},
    "PE out2": {"begun": 2, "got xkl_ready": 2},
    "PE mem_kv": {"full_a0": 1, "begun": 2, "full_a1": 1},
    "PE pq": {"full_a0": 1, "begun": 2, "full_a1": 1, "full_v2": 1},
    "PE route0": {"full_v2": 2, "full_v3": 2, "full_v4": 2, "full_v5": 2, "got oh_ready": 16, "got lr_ready": 16},
    "PE u0": {"full_a0": 4, "begun": 8, "full_a1": 4},
    "PE v0": {"begun": 2, "got xkl_ready": 2},
    "PE route1": {"full_a2": 2, "full_a3": 2, "full_a4": 2, "full_a5": 2, "got oh_ready": 16, "got lr_ready": 16},
    "PE u1": {"full_a0": 1, "begun": 2, "full_a1": 1},
    "PE v1": {"begun": 2, "got xkl_ready": 2},
    "ACT mix": {"got land0": 3, "hi": 10, "got land1": 3, "got land2": 2, "free_a1": 2, "free_a2": 2, "free_a3": 2, "got land3": 2, "free_a0": 2, "gate_ready": 2},
    "ACT out": {"got land0": 1, "hi": 2, "got land1": 1, "xkh_ready": 2},
    "ACT ffn": {"got land0": 1, "hi": 4, "got land1": 1, "got land2": 1, "free_a1": 1, "got land3": 1, "free_a0": 1, "gate_ready": 2},
    "ACT down": {"got land0": 1, "hi": 2, "got land1": 1, "xkh_ready": 2},
    "ACT mix2": {"got land0": 2, "hi": 6, "got land1": 2, "got land2": 1, "free_a1": 2, "got land3": 1, "free_a0": 2, "gate_ready": 2},
    "ACT out2": {"got land0": 1, "hi": 2, "got land1": 1, "xkh_ready": 2},
    "ACT mem_kv": {"got land0": 1, "hi": 2, "got land1": 1, "free_a1": 1, "free_a0": 1},
    "ACT pq": {"got land0": 1, "hi": 2, "got land1": 1, "free_a1": 1, "free_a0": 1},
    "ACT route0": {"free_a2": 1, "free_a3": 1},
    "ACT u0": {"got land0": 2, "hi": 8, "got land1": 2, "got land2": 2, "free_a1": 4, "got land3": 2, "free_a0": 4},
    "ACT v0": {"got land0": 1, "hi": 2, "got land1": 1, "xkh_ready": 2},
    "ACT route1": {"free_a2": 2, "free_a3": 2, "free_a4": 2, "free_a5": 2},
    "ACT u1": {"got land0": 1, "hi": 2, "got land1": 1, "free_a1": 1, "free_a0": 1, "gate_ready": 2, "got gate_free": 2},
    "ACT v1": {"got land0": 1, "hi": 2, "got land1": 1, "xkh_ready": 2},
    "DVE mix": {"dve": 6, "free_v7": 2, "got land0": 3, "lo": 10, "got land1": 3, "got land2": 2, "got land3": 2, "free_v6": 2, "got gate_ready": 2, "free_v4": 2, "free_v5": 2},
    "DVE out": {"got land0": 1, "lo": 2, "got land1": 1, "got xkh_ready": 2, "xkl_ready": 2},
    "DVE ffn": {"got land0": 1, "lo": 4, "got land1": 1, "got land2": 1, "got land3": 1, "got gate_ready": 2, "free_v4": 1, "free_v5": 1},
    "DVE down": {"got land0": 1, "lo": 2, "got land1": 1, "got xkh_ready": 2, "xkl_ready": 2},
    "DVE mix2": {"dve": 2, "got land0": 2, "lo": 6, "got land1": 2, "got land2": 1, "got land3": 1, "got gate_ready": 2, "free_v4": 2, "free_v5": 2},
    "DVE out2": {"got land0": 1, "lo": 2, "got land1": 1, "got xkh_ready": 2, "xkl_ready": 2},
    "DVE mem_kv": {"got land0": 1, "lo": 2, "got land1": 1},
    "DVE pq": {"got land0": 1, "lo": 2, "got land1": 1, "free_v2": 1},
    "DVE route0": {"free_v2": 2, "free_v3": 2, "free_v4": 2, "free_v5": 2, "er_ready": 8, "oh_ready": 16},
    "DVE u0": {"dve": 58, "got land0": 2, "lo": 8, "got land1": 2, "got land2": 2, "got land3": 2},
    "DVE v0": {"got land0": 1, "lo": 2, "got land1": 1, "got xkh_ready": 2, "xkl_ready": 2},
    "DVE route1": {"er_ready": 8, "oh_ready": 16},
    "DVE u1": {"got land0": 1, "lo": 2, "got land1": 1, "got gate_ready": 2, "gate_free": 2},
    "DVE v1": {"got land0": 1, "lo": 2, "got land1": 1, "got xkh_ready": 2, "xkl_ready": 2},
    "Pool route0": {"got er_ready": 8, "lr_ready": 16},
    "Pool route1": {"got er_ready": 8, "lr_ready": 16},
}


def build(nc, dram, out):
    found = {}
    stream = weight_stream()
    names = [s[0] for s in stream]
    ctx = ExitStack()
    with ctx:
        S = {}

        def sem(*keys):
            for key in keys:
                S[key] = ctx.enter_context(nc.semaphore(key))

        sem("params_in", "x_in0", "x_in1", "x_in2", "x_in3", "mem_in", "gates_in", "small_in", "keys_in", "mem_normed", "wk_in", "wv_in", "out_done", "table_ready")
        sem(*[f"land{s}" for s in range(RING)])
        sem("hi", "lo", "begun")
        for b in range(8):
            sem(f"full_a{b}", f"full_v{b}", f"free_a{b}", f"free_v{b}")
        sem("act", "dve", "pool")
        sem("xh_ready", "xl_ready", "sq_ready", "tmp_ready", "h_ready", "src_ready", "rs_var", "rs_std")
        sem("scored", "exped", "normed", "gate_ready", "gate_free", "conv_ready", "small_hi", "small_lo")
        sem("lru_exp", "lru_m", "lru_s", "lsm_a", "lsm_b", "lsm_c", "cum_ready")
        sem("a_ms", "a_sd", "a_y", "cmp_in", "cmp_hid", "cmp_s", "kv_ready")
        sem("top_m", "top_e", "idx_ready", "lr_ready", "er_ready", "oh_ready", "g_stored", "w1_free", "lam_a", "lam_b", "masks_free", "out_ready", "y_ready", "xkh_ready", "xkl_ready", "kv2_ready")

        def sb(name, shape, dt=F32):
            return ctx.enter_context(nc.sbuf_tensor(name, shape, dt))

        ps = ctx.enter_context(nc.psum_tensor("ps", [P, 8, 512], F32))
        hT = sb("hT", [P, KC, T])
        xh = sb("xh", [P, KC, T], F32R)
        xl = sb("xl", [P, KC, T], F32R)
        raw = sb("raw", [P, RING, D])
        wh = sb("wh", [P, 2, D], F32R)
        wl = sb("wl", [P, 2, D], F32R)
        par = sb("par", [P, N_PARAMS])
        ident = sb("ident", [P, P])
        ones = sb("ones", [P, P])
        nd_causal = sb("nd_causal", [P, 2, T])
        nd_cmp = sb("nd_cmp", [P, 2, C_CMP])
        ok_cmp = sb("ok_cmp", [P, 2, C_CMP])
        iota = sb("iota", [P, P])
        iota_hi = sb("iota_hi", [P, P])
        xkh = sb("xkh", [P, 2, T], F32R)
        xkl = sb("xkl", [P, 2, T], F32R)
        rstd = sb("rstd", [P, T])
        small = sb("small", [P, 64])
        nmax = sb("nmax", [P, 8])
        ssum = sb("ssum", [P, 8])
        rinv = sb("rinv", [P, 8])
        arena0 = (nc.sbuf_base + 63) // 64 * 64
        arena_bytes = (nc.sbuf_usable_end - arena0) // 64 * 64 - 64

        def at(name, kb, shape, dt=F32):
            size = int(np.prod(shape[1:])) * (2 if dt == BF16 else 4)
            assert kb * 1024 + size <= arena_bytes, (name, kb, size, arena_bytes)
            return nc.alloc_sbuf_tensor_at(name, shape, dt, offset=arena0 + int(kb * 1024))

        yh = at("yh", 0, [P, 16, T], F32R)
        yl = at("yl", 16, [P, 16, T], F32R)
        tmp = at("tmp", 32, [P, KC, T])
        xc = at("xc", 32, [P, 4, T])
        gg = at("gg", 36, [P, 4, T])
        rr = at("rr", 40, [P, 4, T])
        ii = at("ii", 44, [P, 4, T])
        wab = at("wab", 48, [P, 2, 4, P])
        aa = at("aa", 52, [P, 4, T])
        tt = at("tt", 56, [P, 4, T])
        xpad = at("xpad", 69, [P, T + 4])
        pr = at("pr", 32, [P, 4, 2, T])
        pt = at("pt", 40, [P, 4, 512])
        qs = at("qs", 48, [P, 3, T])
        ks = at("ks", 51, [P, 3, T])
        vs = at("vs", 54, [P, 6, 2, P])
        nd2 = at("nd2", 60, [P, 3, 2, T])
        triu = at("triu", 66, [P, 2, T])
        gln = at("gln", 68, [P, P])
        mscr = at("mscr", 71, [P, P])
        ysb = at("ysb", 69, [P, 2, P])
        cumq = at("cumq", 70.25, [P, 32])
        small_w = at("small_w", 71, [P, KC * 48])
        dist_i = at("dist_i", 66, [P, 2, T], I32)
        dist_m = at("dist_m", 68, [P, 2, T], I32)
        mask_f = at("mask_f", 76, [P, 2, T])
        w1 = at("w1", 32, [P, 32, P])
        small_h = at("small_h", 76, [P, KC * 48], F32R)
        small_l = at("small_l", 79, [P, KC * 48], F32R)
        w1v = [at(f"w1v{q}", (12, 28, 50, 56)[q], [P, 8, P]) for q in range(4)]
        narrow = at("narrow", 69, [P, T])
        xw = at("xw", 48, [P, 32, C_CMP])
        kcv = at("kcv", 64, [P, 2, T])
        kd = at("kd", 60, [P, 2, 2, T])
        kcd = at("kcd", 66, [P, 2, 16])
        vcd = at("vcd", 66.5, [P, 2, 64])
        w2 = at("w2", 74, [P, 2, P])
        hid_c = at("hid_c", 66.25, [P, 2, 16])
        sc = at("sc", 67, [P, 2, 2, 16])
        pc = at("pc", 56, [P, 2, 2, P])
        ptc = at("ptc", 58, [P, 2, T])
        bg2 = at("bg2", 75, [P, 2, 48])
        mixT = at("mixT", 32, [P, KC, T])
        gt = at("gt", 48, [P, 8, T])
        mtmp = at("mtmp", 56, [P, T])
        hidT = at("hidT", 0, [P, FT, T])
        gt2 = at("gt2", 48, [P, 2, T])
        memT = at("memT", 0, [P, KC, T])
        kx = at("kx", 56, [P, 4, T])
        vx = at("vx", 60, [P, 4, 2, P])
        yx = at("yx", 64, [P, 4, T])
        ag = at("ag", 0, [P, HALF, T])
        e1t = rstd
        e2t = at("e2t", 64, [P, T])
        gate_parts = at("gate_parts", 65, [P, 3, T], BF16)
        rest = at("rest", 66.5, [P, T])
        oh_l = at("oh_l", 68, [P, 2, 8, P], BF16)
        oh_r = at("oh_r", 72, [P, 2, 8, HALF], BF16)
        oh_g = at("oh_g", 74, [P, 2, 3, 8, HALF], BF16)
        gt3 = at("gt3", 79, [P, 2, T])
        keysT = at("keysT", 82, [P, 2, P])
        qt = at("qt", 80, [P, 2, T])
        svs = at("svs", 48, [P, 8, 4 * P])
        sv = at("sv", 78, [P, 4, P])
        sv2 = at("sv2", 64, [P, 4, P])
        vtop = at("vtop", 66, [P, 4, TOPK])
        itop = at("itop", 66.25, [P, 4, TOPK], U32)
        itf = at("itf", 66.5, [P, 4, TOPK])
        ctop = at("ctop", 66.75, [P, 2, TOPK])
        cidx = at("cidx", 67, [P, 2, TOPK], U32)
        cij = at("cij", 67.25, [P, 2, 2, TOPK], U32)
        cijf = at("cijf", 67.75, [P, 2, 2, TOPK])
        cand = at("cand", 69, [P, 2, 256])
        cand2 = at("cand2", 71, [P, 2, 256])
        eqb = at("eqb", 73, [P, 2, 256])
        etab = at("etab", 75, [P, 3, 2, P])

        def p_col(name, j=0, n=1):
            o, w = PARAMS[name]
            return par[:, o + j:o + j + n]

        def p_dyn(name, j):
            o, w = PARAMS[name]
            return par[:, bass.ds(j + o, 1)]

        def one(ap3):
            return ap3.rearrange("p o t -> p (o t)")

        def dyn(t, j):
            return t[:, j, :] if isinstance(j, int) else one(t[:, bass.ds(j, 1), :])

        route_base = []

        def routed(eng, half, i, b):
            bank = (b + 2) % 4
            eng.wait_ge(S[f"full_{'va'[half]}{2 + bank}"], i * 2 + (route_base[half][bank] + (b + 2) // 4))
        block = ctx.enter_context(nc.Block())

        @block.sync
        def _(sp):
            k = Counts("SP", S, found)
            sp.dma_start(par[:], dram["params"]).then_inc(S["params_in"], 16)
            for q in range(4):
                c = slice(4 * q, 4 * q + 4)
                sp.dma_start(hT[:, c, :], dram["x"][:, c, :]).then_inc(S[f"x_in{q}"], 16)
            sp.dma_start(wab[:], dram["w_ab"]).then_inc(S["gates_in"], 16)
            sp.dma_start(keysT[:], dram["sub_keys"]).then_inc(S["keys_in"], 16)
            sent, holder, before = 0, {}, None
            for name, turns, chunks in stream:
                n = len(chunks)
                last = {s: max((j for j in range(n) if j % RING == s), default=None) for s in range(RING)}

                def send(i, j, ordinal, prior):
                    tensor, first, step, width = chunks[j]
                    s = j % RING
                    if prior is not None:
                        sp.wait_ge(S["hi"], prior)
                        sp.wait_ge(S["lo"], prior)
                    src = dram[tensor]
                    idx = first + (step * i if step else 0)
                    src = src[idx] if isinstance(idx, int) else src[bass.ds(idx, 1)].rearrange("o p w -> (o p) w")
                    sp.dma_start(raw[:, s, 0:width], src).then_inc(S[f"land{s}"], 16)

                if turns == 1:
                    for j in range(n):
                        s = j % RING
                        send(0, j, sent + j, holder[s] + 1 if s in holder else None)
                        holder[s] = sent + j
                else:
                    back = []
                    for j in range(n):
                        s = j % RING
                        d = [RING] if j >= RING else [n - last[s] + j]
                        if j < RING:
                            d.append(sent + j - holder[s])
                        back.append(min(d))
                    with sp.Fori(0, turns) as i:
                        for j in range(n):
                            send(i, j, None, i * n + (sent + j - back[j] + 1))
                    for s in range(RING):
                        if last[s] is not None:
                            holder[s] = sent + (turns - 1) * n + last[s]
                sent += turns * n
            sp.wait_ge(S["out_ready"], 1)
            sp.dma_start(out, tmp[:]).then_inc(S["out_done"], 16)
            sp.wait_ge(S["out_done"], 16)

        @block.tensor
        def _(pe):
            k = Counts("PE", S, found)
            mm = nc.tensor.matmul
            fresh = []

            def reserve(*banks):
                for b in banks:
                    for e in "av":
                        key = f"full_{e}{b}"
                        if k.held.get(key) != k.n[key]:
                            hold(pe, S[f"free_{e}{b}"], k.at(key))
                            k.held[key] = k.n[key]

            def chunk():
                pe.wait_ge(S["hi"], k.at("begun", 1))
                pe.wait_ge(S["lo"], k.at("begun", 1))

            def begin(ins, first):
                if first:
                    ins.then_inc(*k.up("begun"))

            def quarter(kc):
                if fresh and kc % 4 == 0:
                    pe.wait_ge(*fresh[kc // 4])

            def tile_T(j, b, reader):
                reserve(b)
                chunk()
                for kc in range(KC):
                    quarter(kc)
                    c = slice(kc * P, (kc + 1) * P)
                    begin(mm(ps[:, b, 0:T], wh[:, j % 2, c], xh[:, kc, :], start=kc == 0, stop=False), kc == 0)
                    mm(ps[:, b, 0:T], wh[:, j % 2, c], xl[:, kc, :], start=False, stop=False)
                    m = mm(ps[:, b, 0:T], wl[:, j % 2, c], xh[:, kc, :], start=False, stop=kc == KC - 1)
                m.then_inc(*k.up(f"full_{reader}{b}"))
                fresh.clear()

            def tile_N(j, b, reader):
                reserve(b)
                chunk()
                for tq in range(2):
                    o = ps[:, b, tq * P:(tq + 1) * P]
                    for kc in range(KC):
                        c, t = slice(kc * P, (kc + 1) * P), slice(tq * P, (tq + 1) * P)
                        begin(mm(o, xh[:, kc, t], wh[:, j % 2, c], start=kc == 0, stop=False), tq + kc == 0)
                        mm(o, xh[:, kc, t], wl[:, j % 2, c], start=False, stop=False)
                        m = mm(o, xl[:, kc, t], wh[:, j % 2, c], start=False, stop=kc == KC - 1)
                m.then_inc(*k.up(f"full_{reader}{b}"))

            def part_T(j, b, k0, nk, y0, first):
                reserve(b)
                for n in range(nk):
                    c = slice((k0 + n) * P, (k0 + n + 1) * P)
                    begin(mm(ps[:, b, 0:T], wh[:, j % 2, c], yh[:, y0 + n, :], start=n == 0, stop=False),
                          first and n == 0)
                    mm(ps[:, b, 0:T], wh[:, j % 2, c], yl[:, y0 + n, :], start=False, stop=False)
                    m = mm(ps[:, b, 0:T], wl[:, j % 2, c], yh[:, y0 + n, :], start=False, stop=n == nk - 1)
                m.then_inc(*k.up(f"full_v{b}"))

            def rows(j, first, last):
                chunk()
                pe.wait_ge(*k.next("xkl_ready"))
                for t in range(KC):
                    o = ps[:, t // 2, (t % 2) * T:(t % 2 + 1) * T]
                    c = slice(t * P, (t + 1) * P)
                    begin(mm(o, wh[:, j % 2, c], xkh[:, j % 2, :], start=first and t % 2 == 0, stop=False,
                             skip_group_check=True), t == 0)
                    mm(o, wh[:, j % 2, c], xkl[:, j % 2, :], start=False, stop=False, skip_group_check=True)
                    m = mm(o, wl[:, j % 2, c], xkh[:, j % 2, :], start=False, stop=last,
                           skip_group_check=True)
                    if last and t % 2 == 1:
                        m.then_inc(*k.up(f"full_v{t // 2}"))

            def residual(name, turns, peel_last=False):
                reserve(*range(8))
                rows(0, True, False)
                rows(1, False, False)
                if turns > 2:
                    with k.loop(name, pe, turns - 2):
                        rows(0, False, False)
                        rows(1, False, False)
                rows(0, False, False)
                rows(1, False, True)

            def sum_squares():
                reserve(0)
                for q in range(4):
                    pe.wait_ge(*k.next("sq_ready"))
                    for kc in range(4 * q, 4 * q + 4):
                        m = mm(ps[:, 0, 0:T], ones[:], tmp[:, kc, :], start=kc == 0, stop=kc == KC - 1)
                m.then_inc(*k.up("full_v0"))

            def normed_x():
                fresh.extend([k.next("xl_ready") for q in range(4)])

            def small_tile(b, width, reader):
                reserve(b)
                pe.wait_ge(*k.next("small_lo"))
                for kc in range(KC):
                    c, o = slice(kc * width, (kc + 1) * width), ps[0:width, b, 0:T]
                    mm(o, small_h[:, c], xh[:, kc, :], start=kc == 0, stop=False)
                    mm(o, small_h[:, c], xl[:, kc, :], start=False, stop=False)
                    m = mm(o, small_l[:, c], xh[:, kc, :], start=False, stop=kc == KC - 1)
                m.then_inc(*k.up(f"full_a{b}"))
                reserve(b)
                for tq in range(2):
                    m = nc.tensor.transpose(ps[:, b, tq * 64:tq * 64 + width], narrow[0:width, tq * P:(tq + 1) * P],
                                            ident[0:width, 0:width])
                m.then_inc(*k.up(f"full_{reader}{b}"))

            def staged(*banks):
                reserve(*banks)

            def qk(b, q, key, lo=0, hi=P, more=None):
                reserve(b)
                for i in range(2):
                    o = ps[:, b, i * T:(i + 1) * T]
                    m = mm(o, q[lo:hi, i * P:(i + 1) * P], key[lo:hi, :], start=True, stop=more is None)
                    if more is not None:
                        m = more(o)
                m.then_inc(*k.up(f"full_v{b}"))

            BLOCKS = ((0, 0), (1, 0), (1, 1), (0, 1))

            def turn_probs(maps, n_blocks=3):
                for m in maps:
                    reserve(2 + m)
                    for n, (i, kt) in enumerate(BLOCKS[:n_blocks]):
                        ins = nc.tensor.transpose(ps[:, 2 + m, n * P:(n + 1) * P],
                                                  pr[:, m, i, kt * P:(kt + 1) * P], ident[:])
                    ins.then_inc(*k.up(f"full_a{2 + m}"))

            def pv_T(o, v, m, first, last):
                mm(o, v(0), pt[:, m, 0:T], start=first, stop=False, skip_group_check=True)
                return mm(o[:, P:T], v(1), pt[:, m, T:T + P], start=False, stop=last, skip_group_check=True)

            pe.wait_ge(S["table_ready"], 1)
            sum_squares()
            normed_x()

            for ct in range(4):
                tile_T(2 * ct, 0, "v")
                tile_T(2 * ct + 1, 1, "a")
                pe.wait_ge(*k.next("conv_ready"))
                if ct == 0:
                    pe.wait_ge(S["gates_in"], 16)
                for gate in range(2):
                    reserve(2 + gate)
                    mm(ps[:, 2 + gate, 0:T], wab[:, gate, ct, :], xc[:, ct, :], start=True,
                       stop=True).then_inc(*k.up(f"full_a{2 + gate}"))

            def diff_finish(hh):
                pe.wait_ge(*k.next("normed"))
                turn_probs([0])
                staged(2)
                reserve(6)
                v = vs[:, hh]
                mm(ps[:, 6, 0:P], pt[:, 0, 0:P], v[:, 0, :], start=True, stop=True)
                mm(ps[:, 6, P:T], pt[:, 0, P:T], v[:, 0, :], start=True, stop=False)
                mm(ps[:, 6, P:T], pt[:, 0, T:T + P], v[:, 1, :], start=False,
                   stop=True).then_inc(*k.up("full_v6"))
                pe.wait_ge(*k.next("a_y"))
                reserve(7)
                for i in range(2):
                    m = nc.tensor.transpose(ps[:, 7, i * P:(i + 1) * P], ysb[:, i, :], ident[:])
                m.then_inc(*k.up("full_v7"))

            for h in range(4):
                tile_T(3 * h, 0, "a")
                tile_T(3 * h + 1, 1, "a")
                tile_N(3 * h + 2, 0, "a")
                if h:
                    diff_finish((h - 1) % 2)
                staged(0, 1)
                for m in range(2):
                    qk(2 + m, qs[:, 0], ks[:, 0], 64 * m, 64 * m + 64)
            diff_finish(1)

            small_tile(7, 4, "v")
            pe.wait_ge(*k.next("lsm_c"))
            reserve(7)
            for i in range(2):
                for st in range(2):
                    m = mm(ps[:, 7, 4 * i:4 * i + 4], triu[:, st, i * P:(i + 1) * P],
                           cumq[:, 8 + 4 * st:12 + 4 * st], start=st == 0, stop=st == 1)
            m.then_inc(*k.up("full_v7"))

            def fox_finish(hh):
                pe.wait_ge(*k.next("normed"))
                turn_probs([0])
                staged(2)
                reserve(6)
                pv_T(ps[:, 6, 0:T], lambda kt: vs[:, hh, kt, :], 0, True, True).then_inc(*k.up("full_v6"))

            for h in range(4):
                tile_T(3 * h, 0, "a")
                tile_T(3 * h + 1, 1, "a")
                tile_N(3 * h + 2, 0, "a")
                if h:
                    fox_finish((h - 1) % 2)
                staged(0, 1)
                pe.wait_ge(*k.next("cum_ready"))

                def less_cum(o):
                    for st in range(2):
                        m = mm(o, cumq[:, 16 + st:17 + st].to_broadcast([P, P]), triu[:, st, :],
                               start=False, stop=st == 1)
                    return m
                qk(2, qs[:, 0], ks[:, 0], more=less_cum)
            fox_finish(1)

            tile_T(0, 0, "a")
            tile_N(1, 1, "a")

            def swa_finish(g):
                pe.wait_ge(*k.next("normed"))
                turn_probs([0, 1])
                staged(2, 3)
                reserve(6)
                for hh in range(2):
                    m = pv_T(ps[64 * hh:64 * hh + 64, 6, 0:T], lambda kt: vs[:, 0, kt, 64 * g:64 * g + 64],
                             hh, True, True)
                m.then_inc(*k.up("full_v6"))

            for pair in range(4):
                tile_T(2 + pair, pair % 2, "a")
                if pair:
                    swa_finish((pair - 1) // 2)
                staged(0, 1)
                for hh in range(2):
                    qk(2 + hh, qs[:, 0], ks[:, 1 + pair // 2], 64 * hh, 64 * hh + 64)
            swa_finish(1)

            for _ in range(16):
                k.n["got y_ready"] += 1
            pe.wait_ge(S["y_ready"], k.n["got y_ready"])
            with k.loop("mix", pe, KC // 2):
                for jj in range(2):
                    for n in range(4):
                        tile_T(5 * jj + n, n, "a")
                    chunk()
                    for n in range(4):
                        part_T(5 * jj + 4, 4 + n, 4 * n, 4, 4 * n, n == 0)

            residual("out", KC // 2)
            sum_squares()
            normed_x()
            with k.loop("ffn", pe, FT // 2):
                for f in range(2):
                    reserve(4 + f)
                    tile_T(2 * f, f, "a")
                    tile_T(2 * f + 1, 4 + f, "v")
            residual("down", FT // 2)
            sum_squares()

            sum_squares()
            normed_x()

            def dil_finish(hh):
                pe.wait_ge(*k.next("normed"))
                turn_probs([0, 1, 2])
                staged(2, 3, 4)
                reserve(6)
                for g in range(3):
                    m = pv_T(ps[:, 6, 0:T], lambda kt: vs[:, 3 * hh + g, kt, :], g, g == 0, g == 2)
                m.then_inc(*k.up("full_v6"))

            for h in range(4):
                for g in range(3):
                    c = 9 * h + 3 * g
                    tile_T(c, c % 2, "a")
                    tile_T(c + 1, (c + 1) % 2, "a")
                    tile_N(c + 2, c % 2, "a")
                    if h and g == 0:
                        dil_finish((h - 1) % 2)
                    staged(0, 1)
                    qk(2 + g, qs[:, g], ks[:, g])
            dil_finish(1)

            for j, kind in enumerate("TTTNTN"):
                (tile_T if kind == "T" else tile_N)(j, j % 2, "a")
            small_tile(7, 48, "a")
            for kv in range(2):
                pe.wait_ge(*k.next("cmp_in"))
                pe.wait_ge(*((S["wk_in"], 16) if kv == 0 else (S["wv_in"], 64)))
                if kv == 0:
                    pe.wait_ge(S["small_in"], 32)
                reserve(5, 6)
                for g in range(2):
                    o = ps[:, 5 + g, 0:C_CMP]
                    for i in range(32):
                        w = w1 if kv == 0 else w1v[i // 8]
                        m = mm(o, w[64 * g:64 * g + 64, i if kv == 0 else i % 8, :], xw[64 * g:64 * g + 64, i, :],
                               start=i == 0, stop=i == 31)
                    m.then_inc(*k.up(f"full_a{5 + g}"))
                pe.wait_ge(*k.next("cmp_hid"))
                reserve(7)
                for g in range(2):
                    if kv == 0:
                        m = mm(ps[:, 7, g * 16:g * 16 + C_CMP], w2[:, 0, :], hid_c[:, g, 0:C_CMP],
                               start=True, stop=True)
                    else:
                        m = mm(ps[0:C_CMP, 7, g * 64:g * 64 + 64], hid_c[:, g, 0:C_CMP], w2[:, 1, 0:64],
                               start=True, stop=True)
                m.then_inc(*k.up("full_v7"))

            def nsa_finish(g):
                pe.wait_ge(*k.next("normed"))
                turn_probs([0, 1, 2, 3])
                reserve(7)
                for hh in range(2):
                    for i in range(2):
                        m = nc.tensor.transpose(ps[:, 7, hh * T + i * P:hh * T + (i + 1) * P],
                                                pc[:, hh, i, :], ident[:])
                m.then_inc(*k.up("full_a7"))
                staged(2, 3, 4, 5, 7)
                reserve(6)
                for hh in range(2):
                    o = ps[64 * hh:64 * hh + 64, 6, 0:T]
                    for br in range(2):
                        pv_T(o, lambda kt: vs[:, br, kt, 64 * g:64 * g + 64], 2 * hh + br, br == 0, False)
                    m = mm(o, vcd[0:C_CMP, g, :], ptc[0:C_CMP, hh, :], start=False, stop=True,
                           skip_group_check=True)
                m.then_inc(*k.up("full_v6"))

            pe.wait_ge(*k.next("kv2_ready"))
            for pair in range(8):
                g = pair // 4
                tile_T(pair, pair % 2, "a")
                if pair:
                    nsa_finish((pair - 1) // 4)
                staged(0, 1)
                for hh in range(2):
                    for br in range(2):
                        qk(2 + 2 * hh + br, qs[:, 0], kd[:, br, g], 64 * hh, 64 * hh + 64)
                reserve(6, 7)
                for hh in range(2):
                    for i in range(2):
                        m = mm(ps[:, 6 + hh, i * 16:i * 16 + C_CMP], qs[64 * hh:64 * hh + 64, 0, i * P:(i + 1) * P],
                               kcd[64 * hh:64 * hh + 64, g, 0:C_CMP], start=True, stop=True)
                    m.then_inc(*k.up(f"full_v{6 + hh}"))
            nsa_finish(1)

            for _ in range(12):
                k.n["got y_ready"] += 1
            pe.wait_ge(S["y_ready"], k.n["got y_ready"])
            with k.loop("mix2", pe, KC // 2):
                for jj in range(2):
                    for n in range(2):
                        tile_T(3 * jj + n, n, "a")
                    chunk()
                    part_T(3 * jj + 2, 4, 0, 4, 0, True)
                    part_T(3 * jj + 2, 5, 4, 8, 4, False)

            residual("out2", KC // 2)
            sum_squares()
            normed_x()
            with k.loop("mem_kv", pe, 4):
                tile_T(0, 0, "a")
                tile_N(1, 1, "a")
            sum_squares()
            normed_x()

            def cross_finish(h):
                pe.wait_ge(*k.next("normed"))
                turn_probs([0], 4)
                staged(2)
                reserve(6)
                o = ps[:, 6, 0:T]
                mm(o, vx[:, h, 0, :], pt[:, 0, 0:T], start=True, stop=False, skip_group_check=True)
                mm(o[:, P:T], vx[:, h, 1, :], pt[:, 0, T:T + P], start=False, stop=False, skip_group_check=True)
                mm(o[:, 0:P], vx[:, h, 1, :], pt[:, 0, T + P:2 * T], start=False, stop=True,
                   skip_group_check=True).then_inc(*k.up("full_v6"))

            for h in range(4):
                tile_T(h, h % 2, "a")
                if h:
                    cross_finish(h - 1)
                staged(0, 1)
                qk(2, qs[:, 0], kx[:, h])
            cross_finish(3)
            residual("xo", 2)
            def route(b):
                reserve(b)
                for s in range(8):
                    o = ps[:, b, s * HALF:(s + 1) * HALF]
                    for part in range(3):
                        m = mm(o, oh_l[:, b % 2, s, :], oh_g[:, b % 2, part, s, :], start=part == 0, stop=part == 2)
                return m

            sum_squares()
            normed_x()
            pe.wait_ge(S["keys_in"], 16)
            with k.loop("pq", pe, 8):
                tile_T(0, 0, "a")
                tile_T(1, 1, "a")
                staged(0, 1)
                reserve(2)
                for i in range(2):
                    for side in range(2):
                        c = (2 * i + side) * P
                        m = mm(ps[:, 2, c:c + P], qt[:, side, i * P:(i + 1) * P], keysT[:, side, :],
                               start=True, stop=True)
                m.then_inc(*k.up("full_v2"))
            with k.loop("u0", pe, 8):
                for j in range(HALF // 8):
                    tile_T(j, j % 2, "a")
            pe.wait_ge(*k.next("idx_ready"))
            for n in range(3):
                reserve(3 + n)
                for i in range(2):
                    m = nc.tensor.transpose(ps[:, 3 + n, i * P:(i + 1) * P], etab[:, n, i, :], ident[:])
                m.then_inc(*k.up(f"full_v{3 + n}"))
            route_base.append([k.at(f"full_v{2 + b}") for b in range(4)])
            with k.loop("route0", pe, 4):
                for b in range(8):
                    for ready in ("oh_ready", "lr_ready"):
                        k.next(ready)
                        pe.wait_ge(*k.next(ready))
                    route(2 + b % 4).then_inc(*k.up(f"full_v{2 + b % 4}"))
            residual("v0", HALF // 2)
            route_base.append([k.at(f"full_a{2 + b}") for b in range(4)])
            with k.loop("route1", pe, 4):
                for b in range(8):
                    for ready in ("oh_ready", "lr_ready"):
                        k.next(ready)
                        pe.wait_ge(*k.next(ready))
                    route(2 + b % 4).then_inc(*k.up(f"full_a{2 + b % 4}"))
            with k.loop("u1", pe, HALF // 2):
                for b in range(2):
                    tile_T(b, b, "a")
            residual("v1", HALF // 2)
            sum_squares()

        @block.scalar
        def _(act):
            k = Counts("ACT", S, found)
            f = nc.scalar.activation

            def own():
                act.wait_ge(*k.own())

            def take(b):
                act.wait_ge(S[f"full_a{b}"], k.at(f"free_a{b}", 1))

            def split(j, width=D):
                act.wait_ge(*k.next(f"land{j % RING}", 16))
                hold(act, S["begun"], k.at("hi"))
                f(wh[:, j % 2, 0:width], raw[:, j % RING, 0:width], ACT.Copy).then_inc(*k.up("hi"))

            def xsplit(j, src, n):
                hold(act, S["begun"], k.at("hi", -1))
                f(xkh[:, j % 2, :], dyn(src, n), ACT.Copy).then_inc(*k.up("xkh_ready"))

            def residual(src, name, turns, more=True):
                act.wait_ge(*k.next("src_ready"))
                xsplit(0, src, 0)
                split(1)
                xsplit(1, src, 1)
                split(0)
                xsplit(0, src, 2)
                if turns > 2:
                    with k.loop(name, act, turns - 2) as i:
                        split(1)
                        xsplit(1, src, i * 2 + 3)
                        split(0)
                        xsplit(0, src, i * 2 + 4)
                split(1)
                xsplit(1, src, 2 * turns - 1)
                if more:
                    split(0)

            def norm(src, arrived=None, parts=True):
                for q in range(4):
                    c = slice(4 * q, 4 * q + 4)
                    if arrived is None:
                        act.wait_ge(*k.next("h_ready"))
                    elif q < len(arrived):
                        act.wait_ge(*arrived[q])
                    f(tmp[:, c, :], src[:, c, :], ACT.Square).then_inc(*k.up("sq_ready"))
                act.wait_ge(*k.next("rs_var"))
                f(rstd[:], rstd[:], ACT.Sqrt).then_inc(*k.up("rs_std"))
                if parts:
                    for q in range(4):
                        c = slice(4 * q, 4 * q + 4)
                        act.wait_ge(*k.next("tmp_ready"))
                        f(xh[:, c, :], tmp[:, c, :], ACT.Copy).then_inc(*k.up("xh_ready"))

            def evac(b, dst, scale=None):
                take(b)
                src = ps[:, b, 0:T]
                if scale is None:
                    f(dst, src, ACT.Copy).then_inc(*k.up(f"free_a{b}"))
                else:
                    f(dst, src, ACT.Copy, scale=scale).then_inc(*k.up(f"free_a{b}"))

            def flat(t):
                return t.rearrange("p a b -> p (a b)")

            def exps(maps, joint=False):
                for m in maps:
                    for i in range(2):
                        bias = nmax[:, i:i + 1] if joint else nmax[:, 2 * m + i:2 * m + i + 1]
                        ins = f(pr[:, m, i, :], pr[:, m, i, :], ACT.Exp, bias=bias,
                                accum_out=ssum[:, 2 * m + i:2 * m + i + 1])
                        last = m == maps[-1] and i == 1
                        ins.then_inc(*k.up("exped" if last else "act"))

            def probs_out(maps, n_blocks=3):
                for m in maps:
                    take(2 + m)
                    w = n_blocks * P
                    f(pt[:, m, 0:w], ps[:, 2 + m, 0:w], ACT.Copy).then_inc(*k.up(f"free_a{2 + m}"))

            act.wait_ge(S["params_in"], 16)
            act.wait_ge(S["table_ready"], 1)
            norm(hT, [(S[f"x_in{q}"], 16) for q in range(4)])
            split(0)
            f(small[:, 4:8], p_col("lambda", 0, 4), ACT.Abs).then_inc(*k.up("act"))
            own()
            f(small[:, 4:8], small[:, 4:8], ACT.Exp, scale=-1.0).then_inc(*k.up("lam_a"))
            act.wait_ge(*k.next("lam_b"))
            f(small[:, 4:8], small[:, 4:8], ACT.Ln).then_inc(*k.up("lam_a"))
            act.wait_ge(*k.next("lam_b"))
            f(small[:, 50:52], small[:, 48:50], ACT.Exp).then_inc(*k.up("lam_a"))

            for ct in range(4):
                split(2 * ct + 1)
                if ct < 3:
                    split(2 * ct + 2)
                else:
                    split(0)
                take(1)
                f(gg[:, ct, :], ps[:, 1, 0:T], ACT.Gelu_apprx_tanh).then_inc(*k.up("free_a1"))
                for b, dst, bias in ((2, rr, "ba"), (3, ii, "bx")):
                    take(b)
                    f(dst[:, ct, :], ps[:, b, 0:T], ACT.Sigmoid, bias=p_col(bias, ct)).then_inc(*k.up(f"free_a{b}"))
            act.wait_ge(*k.next("lam_b"))
            own()
            for ct in range(4):
                f(aa[:, ct, :], rr[:, ct, :], ACT.Exp, scale=small[:, ct:ct + 1]).then_inc(*k.up("act"))
            for ct in range(4):
                f(tt[:, ct, :], rr[:, ct, :], ACT.Tanh, scale=small[:, 8 + ct:9 + ct])\
                    .then_inc(*k.up("lru_exp" if ct == 3 else "act"))
            act.wait_ge(*k.next("lru_m"))
            f(rr[:], rr[:], ACT.Sqrt).then_inc(*k.up("lru_s"))

            def diff_out():
                probs_out([0])
                act.wait_ge(*k.next("a_ms"))
                f(small[:, 54:56], small[:, 54:56], ACT.Sqrt).then_inc(*k.up("a_sd"))

            for h in range(4):
                split(3 * h + 1)
                evac(0, qs[:, 0], 64.0 ** -0.5)
                split(3 * h + 2)
                evac(1, ks[:, 0])
                split((3 * h + 3) % 12)
                evac(0, flat(vs[:, h % 2]))
                if h:
                    diff_out()
                act.wait_ge(*k.next("scored"))
                exps([0, 1])
            diff_out()

            f(small_h[:, 0:4 * KC], p_col("w_cf", 0, 4 * KC), ACT.Copy).then_inc(*k.up("small_hi"))
            take(7)
            f(narrow[0:4, :], ps[0:4, 7, 0:T], ACT.Copy).then_inc(*k.up("free_a7"))
            act.wait_ge(*k.next("lsm_a"))
            f(small[:, 24:32], small[:, 16:24], ACT.Abs).then_inc(*k.up("act"))
            own()
            f(small[:, 24:32], small[:, 24:32], ACT.Exp, scale=-1.0).then_inc(*k.up("lsm_b"))
            act.wait_ge(*k.next("lsm_a"))
            f(small[:, 24:32], small[:, 24:32], ACT.Ln).then_inc(*k.up("lsm_b"))

            for h in range(4):
                split(3 * h + 1)
                evac(0, qs[:, 0], 128.0 ** -0.5)
                split(3 * h + 2)
                evac(1, ks[:, 0])
                split((3 * h + 3) % 12)
                evac(0, flat(vs[:, h % 2]))
                if h:
                    probs_out([0])
                act.wait_ge(*k.next("scored"))
                exps([0])
            probs_out([0])

            split(1)
            take(0)
            own()
            for g in range(2):
                for h in range(2):
                    last = f(ks[64 * h:64 * h + 64, 1 + g, :], ps[64 * g:64 * g + 64, 0, 0:T], ACT.Copy)
                    last.then_inc(*k.up("free_a0" if g + h == 2 else "act"))
            split(2)
            evac(1, flat(vs[:, 0]))
            for pair in range(4):
                split((3 + pair) % 6)
                evac(pair % 2, qs[:, 0], 64.0 ** -0.5)
                if pair:
                    probs_out([0, 1])
                act.wait_ge(*k.next("scored"))
                for m in range(2):
                    for i in range(2):
                        f(small[:, 40 + 2 * m + i:41 + 2 * m + i], p_col("sinks", 2 * pair + m), ACT.Exp,
                          bias=nmax[:, 2 * m + i:2 * m + i + 1]).then_inc(*k.up("act"))
                exps([0, 1])
            probs_out([0, 1])

            with k.loop("mix", act, KC // 2) as i:
                for jj in range(2):
                    for n in range(4):
                        split((5 * jj + n + 1) % 10)
                        take(n)
                        f(gt[:, 4 * jj + n, :], ps[:, n, 0:T], ACT.Sigmoid,
                          bias=p_dyn("b_gate", i * 2 + (KC * n + jj))).then_inc(*k.up(f"free_a{n}"))
                    own()
                    f(small[:, 60:61], ones[:, 0:1], ACT.Copy).then_inc(*k.up("gate_ready"))
                    split((5 * jj + 5) % 10)
            residual(mixT, "out", KC // 2)
            norm(hT)
            with k.loop("ffn", act, FT // 2):
                for n in range(2):
                    split(2 * n + 1)
                    take(n)
                    f(gt2[:, n, :], ps[:, n, 0:T], ACT.Silu).then_inc(*k.up(f"free_a{n}"))
                    own()
                    f(small[:, 60:61], ones[:, 0:1], ACT.Copy).then_inc(*k.up("gate_ready"))
                    split((2 * n + 2) % 4)
            residual(hidT, "down", FT // 2)
            norm(hT, parts=False)

            norm(hT)
            for h in range(4):
                for g in range(3):
                    c = 9 * h + 3 * g
                    split(c + 1)
                    evac(c % 2, qs[:, g], 128.0 ** -0.5)
                    split(c + 2)
                    evac((c + 1) % 2, ks[:, g])
                    split((c + 3) % 36)
                    evac(c % 2, flat(vs[:, 3 * (h % 2) + g]))
                    if h and g == 0:
                        probs_out([0, 1, 2])
                act.wait_ge(*k.next("scored"))
                exps([0, 1, 2], joint=True)
            probs_out([0, 1, 2])

            def spread(b, dst):
                take(b)
                for g in range(2):
                    for h in range(2):
                        last = f(dst[64 * h:64 * h + 64, g, :], ps[64 * g:64 * g + 64, b, 0:T], ACT.Copy)
                        last.then_inc(*k.up(f"free_a{b}" if g + h == 2 else "act"))

            split(1)
            evac(0, kcv[:, 0])
            split(2)
            evac(1, kcv[:, 1])
            split(3)
            spread(0, kd[:, 0])
            split(4)
            evac(1, flat(vs[:, 0]))
            split(5)
            spread(0, kd[:, 1])
            split(0)
            evac(1, flat(vs[:, 1]))
            own()
            f(small[:, 60:61], ones[:, 0:1], ACT.Copy).then_inc(*k.up("kv_ready"))
            act.wait_ge(S["small_in"], 32)
            f(small_h[:], small_w[:], ACT.Copy).then_inc(*k.up("small_hi"))
            take(7)
            f(narrow[0:48, :], ps[0:48, 7, 0:T], ACT.Copy).then_inc(*k.up("free_a7"))
            take(7)
            f(bg2[:], ps[:, 7, 0:P].rearrange("p (i c) -> p i c", i=2)[:, :, 0:48],
              ACT.Sigmoid).then_inc(*k.up("free_a7"))
            own()
            for kv in range(2):
                for g in range(2):
                    take(5 + g)
                    f(hid_c[:, g, 0:C_CMP], ps[:, 5 + g, 0:C_CMP],
                      ACT.Gelu_apprx_tanh).then_inc(*k.up(f"free_a{5 + g}"))
                own()
                f(small[:, 60:61], ones[:, 0:1], ACT.Copy).then_inc(*k.up("cmp_hid"))
                if kv == 0:
                    act.wait_ge(*k.next("cmp_s"))

            def nsa_out():
                probs_out([0, 1, 2, 3])
                take(7)
                f(flat(ptc[0:C_CMP, :, :]), ps[0:C_CMP, 7, :], ACT.Copy).then_inc(*k.up("free_a7"))

            for pair in range(8):
                split((pair + 1) % 8)
                evac(pair % 2, qs[:, 0], 64.0 ** -0.5)
                if pair:
                    nsa_out()
                act.wait_ge(*k.next("scored"))
                f(sc[:, :, :, 0:C_CMP], sc[:, :, :, 0:C_CMP], ACT.Exp).then_inc(*k.up("act"))
                exps([0, 1, 2, 3])
            nsa_out()

            with k.loop("mix2", act, KC // 2):
                for jj in range(2):
                    for n in range(2):
                        split((3 * jj + n + 1) % 6, 12 * P if n == 1 else D)
                        take(n)
                        f(gt[:, 4 * jj + n, :], ps[:, n, 0:T], ACT.Sigmoid).then_inc(*k.up(f"free_a{n}"))
                    own()
                    f(small[:, 60:61], ones[:, 0:1], ACT.Copy).then_inc(*k.up("gate_ready"))
                    split((3 * jj + 3) % 6)
            residual(mixT, "out2", KC // 2)
            for q in range(4):
                act.wait_ge(*k.next("h_ready"))
            norm(memT, [(S["mem_in"], 16)])
            with k.loop("mem_kv", act, 4) as h:
                split(1)
                evac(0, dyn(kx, h))
                split(0)
                evac(1, vx[:, bass.ds(h, 1), :, :].rearrange("p o a b -> p (o a b)"))
            norm(hT, [k.next("mem_normed")])
            for h in range(4):
                split((h + 1) % 4)
                evac(h % 2, qs[:, 0], 128.0 ** -0.5)
                if h:
                    probs_out([0], 4)
                act.wait_ge(*k.next("scored"))
                exps([0])
            probs_out([0], 4)
            residual(yx, "xo", 2)
            norm(hT)
            with k.loop("pq", act, 8):
                split(1)
                evac(0, qt[:, 0])
                split(0)
                evac(1, qt[:, 1])
            with k.loop("u0", act, 8) as i:
                for j in range(HALF // 8):
                    split((j + 1) % 8)
                    take(j % 2)
                    f(dyn(ag, i * 8 + j), ps[:, j % 2, 0:T], ACT.Gelu_apprx_tanh).then_inc(*k.up(f"free_a{j % 2}"))
            act.wait_ge(*k.next("top_m"))
            f(etab[:, 2], etab[:, 2], ACT.Exp).then_inc(*k.up("top_e"))
            residual(ag, "v0", HALF // 2)
            for q in range(4):
                act.wait_ge(*k.next("h_ready"))
            with k.loop("route1", act, 4) as i:
                for b in range(8):
                    take(2 + b % 4)
                    f(ag[:, :, bass.ds(i * 64 + 8 * b, 8)], ps[:, 2 + b % 4, :].rearrange("p (s e) -> p e s", s=8),
                      ACT.Copy).then_inc(*k.up(f"free_a{2 + b % 4}"))
            own()
            f(small[:, 60:61], ones[:, 0:1], ACT.Copy).then_inc(*k.up("g_stored"))
            with k.loop("u1", act, HALF // 2):
                for b in range(2):
                    split((b + 1) % 2)
                    take(b)
                    act.wait_ge(*k.next("gate_free"))
                    f(gt3[:, b, :], ps[:, b, 0:T], ACT.Gelu_apprx_tanh).then_inc(*k.up(f"free_a{b}"))
                    own()
                    f(small[:, 60:61], ones[:, 0:1], ACT.Copy).then_inc(*k.up("gate_ready"))
            residual(ag, "v1", HALF // 2, more=False)
            norm(hT, parts=False)
        @block.vector
        def _(dve):
            k = Counts("DVE", S, found)
            v = nc.vector

            def own():
                dve.wait_ge(*k.own())

            def take(b):
                dve.wait_ge(S[f"full_v{b}"], k.at(f"free_v{b}", 1))

            def flag(key):
                own()
                v.memset(small[:, 63:64], 0.0).then_inc(*k.up(key))

            def step(ins):
                ins.then_inc(*k.up("dve"))
                own()

            def split(j, width=D):
                dve.wait_ge(*k.next(f"land{j % RING}", 16))
                dve.wait_ge(S["hi"], k.at("lo", 1))
                w = slice(0, width)
                v.tensor_tensor(wl[:, j % 2, w], raw[:, j % RING, w], wh[:, j % 2, w].bitcast(F32),
                                ALU.subtract).then_inc(*k.up("lo"))

            def xsplit(j, src, n):
                dve.wait_ge(*k.next("xkh_ready"))
                v.tensor_tensor(xkl[:, j % 2, :], dyn(src, n), xkh[:, j % 2, :].bitcast(F32),
                                ALU.subtract).then_inc(*k.up("xkl_ready"))

            def residual(src, name, turns, more=True):
                flag("src_ready")
                xsplit(0, src, 0)
                split(1)
                xsplit(1, src, 1)
                split(0)
                xsplit(0, src, 2)
                if turns > 2:
                    with k.loop(name, dve, turns - 2) as i:
                        split(1)
                        xsplit(1, src, i * 2 + 3)
                        split(0)
                        xsplit(0, src, i * 2 + 4)
                split(1)
                xsplit(1, src, 2 * turns - 1)
                if more:
                    split(0)
                for b in range(8):
                    take(b)
                    h = hT[:, 2 * b:2 * b + 2, :]
                    v.tensor_tensor(h, h, ps[:, b, :].rearrange("p (a t) -> p a t", a=2),
                                    ALU.add).then_inc(*k.up(f"free_v{b}"))
                    if b % 2:
                        flag("h_ready")

            def norm(src, gain, dst=None):
                take(0)
                v.tensor_scalar(rstd[:], ps[:, 0, 0:T], 1.0 / D, EPS, ALU.mult, ALU.add)\
                    .then_inc(*k.up("free_v0"))
                flag("rs_var")
                dve.wait_ge(*k.next("rs_std"))
                step(v.reciprocal(rstd[:], rstd[:]))

                def lower(q):
                    c = slice(4 * q, 4 * q + 4)
                    dve.wait_ge(*k.next("xh_ready"))
                    v.tensor_tensor(xl[:, c, :], tmp[:, c, :], xh[:, c, :].bitcast(F32),
                                    ALU.subtract).then_inc(*k.up("xl_ready"))

                for q in range(4):
                    for kc in range(4 * q, 4 * q + 4):
                        o = tmp if dst is None else dst
                        v.scalar_tensor_tensor(o[:, kc, :], src[:, kc, :], p_col(gain, kc), rstd[:],
                                               ALU.mult, ALU.mult).then_inc(*k.up("dve"))
                    if dst is None:
                        flag("tmp_ready")
                        if q:
                            lower(q - 1)
                    elif dst is src:
                        flag("h_ready")
                if dst is None:
                    lower(3)

            def slope(i):
                return p_col("slopes", i) if isinstance(i, int) else p_dyn("slopes", i)

            def score(m, mask, slope_col):
                take(2 + m)
                v.scalar_tensor_tensor(pr[:, m], mask, slope_col, ps[:, 2 + m, :].rearrange("p (i s) -> p i s", i=2),
                                       ALU.mult, ALU.add).then_inc(*k.up(f"free_v{2 + m}"))

            def bring_max(n, key="scored"):
                own()
                v.tensor_reduce(nmax[:, 0:2 * n], pr[:, 0:n].rearrange("p m i s -> p (m i) s"), AX.X, ALU.max,
                                negate=True).then_inc(*k.up(key))

            def normalise(n, key="normed"):
                rows = pr[:, 0:n].rearrange("p m i s -> p (m i) s")
                v.tensor_tensor(rows, rows, rinv[:, 0:2 * n].unsqueeze(2).to_broadcast([P, 2 * n, T]),
                                ALU.mult).then_inc(*k.up(key))

            def take_y(b, n, lo=0):
                take(b)
                src = ps[:, b, 0:T]
                step(v.tensor_copy(dyn(yh, n), src))
                v.tensor_tensor(dyn(yl, n), src, dyn(yh, n).bitcast(F32), ALU.subtract).then_inc(*k.up(f"free_v{b}"))
                flag("y_ready")

            dve.wait_ge(S["params_in"], 16)
            dve.wait_ge(S["table_ready"], 1)
            norm(hT, "norm_mix")
            split(0)
            dve.wait_ge(*k.next("lam_a"))
            step(v.tensor_scalar(small[:, 4:8], small[:, 4:8], 1.0, None, ALU.add))
            flag("lam_b")
            for j in range(2):
                step(v.tensor_tensor_reduce(gln[:, 0:64], p_col(f"lq{j + 1}", 0, 64), p_col(f"lk{j + 1}", 0, 64),
                                            1.0, 0.0, ALU.mult, ALU.add, small[:, 48 + j:49 + j]))
            flag("lam_b")
            dve.wait_ge(*k.next("lam_a"))
            step(v.tensor_scalar(small[:, 0:4], p_col("lambda", 0, 4), -1.0, 0.0, ALU.mult, ALU.max))
            step(v.tensor_tensor(small[:, 0:4], small[:, 0:4], small[:, 4:8], ALU.add))
            step(v.tensor_scalar(small[:, 8:12], small[:, 0:4], 8.0, None, ALU.mult))
            step(v.tensor_scalar(small[:, 0:4], small[:, 0:4], -8.0, None, ALU.mult))
            flag("lam_b")
            dve.wait_ge(*k.next("lam_a"))
            step(v.tensor_tensor(small[:, 52:53], small[:, 51:52], small[:, 50:51], ALU.subtract))
            step(v.tensor_scalar(small[:, 52:53], small[:, 52:53], -LAM_INIT, None, ALU.add))
            step(v.tensor_scalar(gln[:], p_col("subln", 0, P), 1.0 - LAM_INIT, None, ALU.mult))

            step(v.memset(xpad[:], 0.0))
            for ct in range(4):
                split(2 * ct + 1)
                take(0)
                v.tensor_copy(xpad[:, 3:3 + T], ps[:, 0, 0:T]).then_inc(*k.up("free_v0"))
                own()
                x3 = [xpad[:, j:j + T] for j in range(4)]
                step(v.tensor_scalar(xc[:, ct, :], x3[3], p_col("conv_w", 12 + ct), p_col("conv_b", ct),
                                     ALU.mult, ALU.add))
                for j in (2, 1):
                    step(v.scalar_tensor_tensor(xc[:, ct, :], x3[j], p_col("conv_w", 4 * j + ct), xc[:, ct, :],
                                                ALU.mult, ALU.add))
                v.scalar_tensor_tensor(xc[:, ct, :], x3[0], p_col("conv_w", ct), xc[:, ct, :],
                                       ALU.mult, ALU.add).then_inc(*k.up("conv_ready"))
                own()
                split((2 * ct + 2) % 8)
            dve.wait_ge(*k.next("lru_exp"))
            step(v.tensor_tensor(ii[:], ii[:], xc[:], ALU.mult))
            step(v.tensor_tensor(rr[:], aa[:], aa[:], ALU.mult))
            v.scalar_tensor_tensor(rr[:], rr[:], 1.0, tt[:], ALU.add, ALU.mult).then_inc(*k.up("lru_m"))
            dve.wait_ge(*k.next("lru_s"))
            step(v.tensor_tensor(ii[:], ii[:], rr[:], ALU.mult))
            for ct in range(4):
                v.tensor_tensor_scan(xc[:, ct, :], aa[:, ct, :], ii[:, ct, :], 0.0, ALU.mult,
                                     ALU.add).then_inc(*k.up("dve"))
            own()
            step(v.tensor_tensor(tt[:], gg[:], xc[:], ALU.mult))
            step(v.tensor_copy(yh[:, 4:8, :], tt[:]))
            step(v.tensor_tensor(yl[:, 4:8, :], tt[:], yh[:, 4:8, :].bitcast(F32), ALU.subtract))
            for ct in range(4):
                flag("y_ready")

            def diff_end(h):
                take(6)
                v.tensor_copy(ysb[:], ps[:, 6, 0:T].rearrange("p (i e) -> p i e", i=2)).then_inc(*k.up("free_v6"))
                own()
                for i in range(2):
                    step(v.tensor_tensor_reduce(mscr[:], ysb[:, i, :], ysb[:, i, :], 1.0, 0.0, ALU.mult,
                                                ALU.add, small[:, 54 + i:55 + i]))
                v.tensor_scalar(small[:, 54:56], small[:, 54:56], 1.0 / P, EPS, ALU.mult,
                                ALU.add).then_inc(*k.up("a_ms"))
                dve.wait_ge(*k.next("a_sd"))
                step(v.reciprocal(small[:, 56:58], small[:, 54:56]))
                for i in range(2):
                    v.scalar_tensor_tensor(ysb[:, i, :], ysb[:, i, :], small[:, 56 + i:57 + i], gln[:],
                                           ALU.mult, ALU.mult).then_inc(*k.up("dve" if i == 0 else "a_y"))
                take_y(7, h)

            for h in range(4):
                split(3 * h + 1)
                split(3 * h + 2)
                split((3 * h + 3) % 12)
                if h:
                    diff_end(h - 1)
                for m in range(2):
                    score(m, nd_causal[:], slope(SLOPE_A + h))
                bring_max(2)
                dve.wait_ge(*k.next("exped"))
                step(v.reciprocal(rinv[:, 0:4], ssum[:, 0:4]))
                step(v.tensor_scalar(rinv[:, 2:4], rinv[:, 2:4], small[:, 52:53], None, ALU.mult))
                normalise(2, "dve")
                own()
                v.tensor_tensor(pr[:, 0], pr[:, 0], pr[:, 1], ALU.add).then_inc(*k.up("normed"))
            diff_end(3)

            dve.wait_ge(*k.next("small_hi"))
            v.tensor_tensor(small_l[:, 0:4 * KC], p_col("w_cf", 0, 4 * KC), small_h[:, 0:4 * KC].bitcast(F32),
                            ALU.subtract).then_inc(*k.up("small_lo"))
            take(7)
            v.tensor_tensor(small[:, 16:24].rearrange("p (i h) -> p i h", i=2),
                            ps[:, 7, 0:P].rearrange("p (i c) -> p i c", i=2)[:, :, 0:4],
                            p_col("fox_b_f", 0, 4).unsqueeze(1).to_broadcast([P, 2, 4]),
                            ALU.add).then_inc(*k.up("free_v7"))
            flag("lsm_a")
            dve.wait_ge(*k.next("lsm_b"))
            step(v.tensor_scalar(small[:, 24:32], small[:, 24:32], 1.0, None, ALU.add))
            flag("lsm_a")
            dve.wait_ge(*k.next("lsm_b"))
            step(v.tensor_scalar(small[:, 16:24], small[:, 16:24], 0.0, None, ALU.min))
            v.tensor_tensor(cumq[:, 8:16], small[:, 16:24], small[:, 24:32], ALU.subtract)\
                .then_inc(*k.up("lsm_c"))
            take(7)
            v.tensor_copy(cumq[:, 0:8], ps[:, 7, 0:8]).then_inc(*k.up("free_v7"))
            own()

            for h in range(4):
                lf = cumq[:, 8:16].rearrange("p (s h) -> p h s", s=2)[:, bass.ds(h, 1), :]
                v.tensor_scalar(cumq[:, 16:18], lf.rearrange("p o s -> p (o s)"), -1.0, None, ALU.mult)\
                    .then_inc(*k.up("cum_ready"))
                split(3 * h + 1)
                split(3 * h + 2)
                split((3 * h + 3) % 12)
                if h:
                    take_y(6, h + 7)
                take(2)
                for i in range(2):
                    cq = cumq[:, bass.ds(h + 4 * i, 1)]
                    v.scalar_tensor_tensor(pr[:, 0, i, :], ps[:, 2, i * T:(i + 1) * T], cq, nd2[:, 1, i, :],
                                           ALU.add, ALU.add).then_inc(*k.up("free_v2" if i else "dve"))
                bring_max(1)
                dve.wait_ge(*k.next("exped"))
                step(v.reciprocal(rinv[:, 0:2], ssum[:, 0:2]))
                normalise(1)
                own()
            take_y(6, 11)

            step(v.tensor_scalar(small[:, 12:20], p_col("sinks", 0, 8), -1.0, None, ALU.mult))
            split(1)
            split(2)
            for pair in range(4):
                split((3 + pair) % 6)
                if pair:
                    take_y(6, 12 + pair - 1)
                for m in range(2):
                    score(m, nd2[:, 0], slope(SLOPE_D + 2 * pair + m))
                bring_max(2, "dve")
                own()
                for m in range(2):
                    c = slice(2 * m, 2 * m + 2)
                    v.tensor_scalar(nmax[:, c], nmax[:, c], small[:, 12 + 2 * pair + m:13 + 2 * pair + m], None,
                                    ALU.min).then_inc(*k.up("scored" if m else "dve"))
                dve.wait_ge(*k.next("exped"))
                step(v.tensor_tensor(rinv[:, 0:4], ssum[:, 0:4], small[:, 40:44], ALU.add))
                step(v.reciprocal(rinv[:, 0:4], rinv[:, 0:4]))
                normalise(2)
                own()
            take_y(6, 15)
            flag("masks_free")

            def mixed(j, jj, n_gates, banks):
                dve.wait_ge(*k.next("gate_ready"))
                for n in range(n_gates):
                    take(banks[n])
                    o = dyn(mixT, j) if n == 0 else mtmp[:]
                    v.tensor_tensor(o, gt[:, 4 * jj + n, :], ps[:, banks[n], 0:T],
                                    ALU.mult).then_inc(*k.up(f"free_v{banks[n]}"))
                    own()
                    if n:
                        step(v.tensor_tensor(dyn(mixT, j), dyn(mixT, j), mtmp[:], ALU.add))

            with k.loop("mix", dve, KC // 2) as i:
                for jj in range(2):
                    for n in range(5):
                        split((5 * jj + n + 1) % 10)
                    mixed(i * 2 + jj, jj, 4, (4, 5, 6, 7))
            residual(mixT, "out", KC // 2)
            norm(hT, "norm_ffn")
            with k.loop("ffn", dve, FT // 2) as i:
                for n in range(2):
                    split(2 * n + 1)
                    split((2 * n + 2) % 4)
                    dve.wait_ge(*k.next("gate_ready"))
                    take(4 + n)
                    v.tensor_tensor(dyn(hidT, i * 2 + n), gt2[:, n, :], ps[:, 4 + n, 0:T],
                                    ALU.mult).then_inc(*k.up(f"free_v{4 + n}"))
            residual(hidT, "down", FT // 2)
            norm(hT, "norm_final", hT)

            norm(hT, "norm_mix_2")
            dve.wait_ge(S["table_ready"], 2)
            for j, dil in ((1, 4), (2, 16)):
                step(v.tensor_scalar(dist_m[:], dist_i[:], dil - 1, None, ALU.bitwise_and))
                step(v.tensor_scalar(mask_f[:], dist_m[:], 0.0, None, ALU.is_equal))
                step(v.tensor_scalar(mask_f[:], mask_f[:], -NEG, NEG, ALU.mult, ALU.add))
                step(v.tensor_tensor(nd2[:, j], nd2[:, j], mask_f[:], ALU.add))

            for h in range(4):
                for g in range(3):
                    for n in range(3):
                        split((9 * h + 3 * g + n + 1) % 36)
                    if h and g == 0:
                        take_y(6, h - 1)
                    score(g, nd2[:, g], slope(SLOPE_DIL + 4 * g + h))
                own()
                v.tensor_reduce(nmax[:, 0:2], pr[:, 0:3].rearrange("p m i s -> p i m s"), AX.XY, ALU.max,
                                negate=True).then_inc(*k.up("scored"))
                dve.wait_ge(*k.next("exped"))
                step(v.tensor_reduce(rinv[:, 0:2], ssum[:, 0:6].rearrange("p (m i) -> p i m", m=3), AX.X,
                                     ALU.add))
                step(v.reciprocal(rinv[:, 0:2], rinv[:, 0:2]))
                for m in range(3):
                    v.tensor_tensor(pr[:, m], pr[:, m], rinv[:, 0:2].unsqueeze(2).to_broadcast([P, 2, T]),
                                    ALU.mult).then_inc(*k.up("normed" if m == 2 else "dve"))
                own()
            take_y(6, 3)

            flag("w1_free")
            for j in range(6):
                split((j + 1) % 6)
            dve.wait_ge(*k.next("small_hi"))
            v.tensor_tensor(small_l[:], small_w[:], small_h[:].bitcast(F32),
                            ALU.subtract).then_inc(*k.up("small_lo"))
            dve.wait_ge(*k.next("kv_ready"))
            for kv, pe_name in ((0, "pe_k"), (1, "pe_v")):
                src = kcv[:, kv].rearrange("p (c b) -> p b c", b=16)
                for a in range(2):
                    v.tensor_tensor(xw[:, 16 * a:16 * a + 16, :], src[:, :, a:a + C_CMP],
                                    p_col(pe_name, 16 * a, 16).unsqueeze(2).to_broadcast([P, 16, C_CMP]),
                                    ALU.add).then_inc(*k.up("cmp_in" if a else "dve"))
                take(7)
                if kv == 0:
                    v.tensor_copy(kcd[:, :, 0:C_CMP],
                                  ps[:, 7, 0:32].rearrange("p (g c) -> p g c", g=2)[:, :, 0:C_CMP])\
                        .then_inc(*k.up("free_v7"))
                    flag("cmp_s")
                else:
                    v.tensor_copy(vcd[0:C_CMP, :, :],
                                  ps[0:C_CMP, 7, 0:P].rearrange("p (g c) -> p g c", g=2))\
                        .then_inc(*k.up("free_v7"))
                    own()
            step(v.memset(pc[:], 0.0))
            flag("kv2_ready")

            def softmax_cmp(h0, hh_off):
                s4 = sc[:, :, :, 0:C_CMP]
                ok = ok_cmp[:].unsqueeze(1).to_broadcast([P, 2, 2, C_CMP])
                step(v.tensor_tensor(s4, s4, ok, ALU.mult))
                step(v.tensor_reduce(small[:, 44:48].rearrange("p (a b) -> p a b", a=2), s4, AX.X, ALU.add))
                step(v.tensor_scalar(small[:, 44:48], small[:, 44:48], 1e-30, None, ALU.max))
                step(v.reciprocal(small[:, 44:48], small[:, 44:48]))

            for pair in range(8):
                split((pair + 1) % 8)
                if pair:
                    take_y(6, pair + 3)
                head = [2 * pair + hh for hh in range(2)]
                for hh in range(2):
                    for br in range(2):
                        score(2 * hh + br, nd_causal[:], slope(head[hh] + SLOPE_B))
                for hh in range(2):
                    take(6 + hh)
                    v.scalar_tensor_tensor(
                        sc[:, hh, :, 0:C_CMP], nd_cmp[:], slope(head[hh] + SLOPE_B),
                        ps[:, 6 + hh, 0:32].rearrange("p (i c) -> p i c", i=2)[:, :, 0:C_CMP],
                        ALU.mult, ALU.add).then_inc(*k.up(f"free_v{6 + hh}"))
                own()
                s4 = sc[:, :, :, 0:C_CMP]
                m4 = small[:, 40:44].rearrange("p (a b) -> p a b", a=2)
                step(v.tensor_reduce(m4, s4, AX.X, ALU.max))
                step(v.tensor_tensor(s4, s4, m4.unsqueeze(3).to_broadcast([P, 2, 2, C_CMP]),
                                     ALU.subtract))
                bring_max(4)
                dve.wait_ge(*k.next("exped"))
                step(v.reciprocal(rinv[:], ssum[:]))
                softmax_cmp(0, 0)
                gates = bg2[:].rearrange("p i (h b) -> p h b i", b=3)
                for hh in range(2):
                    r4 = rinv[:, 4 * hh:4 * hh + 4].rearrange("p (b i) -> p b i", b=2)
                    gh = gates[:, bass.ds(head[hh], 1), :, :].rearrange("p o b i -> p (o b) i")
                    step(v.tensor_tensor(r4, r4, gh[:, 1:3, :], ALU.mult))
                    c2 = small[:, 44 + 2 * hh:46 + 2 * hh]
                    step(v.tensor_tensor(c2, c2, gh[:, 0, :], ALU.mult))
                step(v.tensor_tensor(
                    pc[:, :, :, 0:C_CMP], s4,
                    small[:, 44:48].rearrange("p (a b) -> p a b", a=2).unsqueeze(3)
                    .to_broadcast([P, 2, 2, C_CMP]), ALU.mult))
                normalise(4)
                own()
            take_y(6, 11)

            with k.loop("mix2", dve, KC // 2) as i:
                for jj in range(2):
                    for n in range(3):
                        split((3 * jj + n + 1) % 6, 12 * P if n == 1 else D)
                    mixed(i * 2 + jj, jj, 2, (4, 5))
            flag("w1_free")
            residual(mixT, "out2", KC // 2)
            norm(memT, "norm_mem_2")
            with k.loop("mem_kv", dve, 4):
                split(1)
                split(0)
            flag("mem_normed")
            norm(hT, "norm_x_2")
            for h in range(4):
                split((h + 1) % 4)
                if h:
                    take(6)
                    v.tensor_copy(yx[:, h - 1, :], ps[:, 6, 0:T]).then_inc(*k.up("free_v6"))
                take(2)
                v.tensor_copy(pr[:, 0], ps[:, 2, :].rearrange("p (i s) -> p i s", i=2)).then_inc(*k.up("free_v2"))
                bring_max(1)
                dve.wait_ge(*k.next("exped"))
                step(v.reciprocal(rinv[:, 0:2], ssum[:, 0:2]))
                normalise(1)
                own()
            take(6)
            v.tensor_copy(yx[:, 3, :], ps[:, 6, 0:T]).then_inc(*k.up("free_v6"))
            residual(yx, "xo", 2)
            norm(hT, "norm_ffn_2")
            with k.loop("pq", dve, 8) as h:
                split(1)
                split(0)
                take(2)
                v.tensor_copy(dyn(svs, h), ps[:, 2, :]).then_inc(*k.up("free_v2"))

            def own_then_max():
                own()
                v.memset(small[:, 62:63], 0.0).then_inc(*k.up("dve"))

            def first8(rows, vals, n):
                own_then_max()
                for r in range(n):
                    v.max(vals[:, r, 0:8], rows[:, r, :]).then_inc(*k.up("dve"))
                own()

            def without8(rows, scratch, vals, idx, n):
                own_then_max()
                for r in range(n):
                    v.max_index(idx[:, r, 0:8], vals[:, r, 0:8], rows[:, r, :]).then_inc(*k.up("dve"))
                    v.match_replace(scratch[:, r, :], vals[:, r, 0:8], rows[:, r, :], -3e38).then_inc(*k.up("dve"))
                own()

            def next8(scratch, vals, idx, n):
                own_then_max()
                for r in range(n):
                    v.max(vals[:, r, 8:16], scratch[:, r, :]).then_inc(*k.up("dve"))
                own_then_max()
                for r in range(n):
                    v.max_index(idx[:, r, 8:16], vals[:, r, 8:16], scratch[:, r, :]).then_inc(*k.up("dve"))
                own()

            def pairs(a, b, op, out):
                for i in range(2):
                    v.tensor_tensor(out[:, i, :].rearrange("p (s t) -> p s t", s=TOPK),
                                    a(i).unsqueeze(2).to_broadcast([P, TOPK, TOPK]),
                                    b(i).unsqueeze(1).to_broadcast([P, TOPK, TOPK]), op).then_inc(*k.up("dve"))
                own()

            def numbers(side, h):
                pairs(lambda i: cijf[:, side, i, :], lambda i: iota[:, 0:TOPK], ALU.is_equal, eqb)
                for i in range(2):
                    e = eqb[:, i, :].rearrange("p (s t) -> p s t", s=TOPK)
                    v.tensor_tensor(e, e, itf[:, 2 * i + side, :].unsqueeze(1).to_broadcast([P, TOPK, TOPK]),
                                    ALU.mult).then_inc(*k.up("dve"))
                own()
                for i in range(2):
                    v.tensor_reduce(etab[:, side, i, bass.ds(h * TOPK, TOPK)],
                                    eqb[:, i, :].rearrange("p (s t) -> p s t", s=TOPK), AX.X, ALU.add)\
                        .then_inc(*k.up("dve"))
                own()

            def search(part, h):
                if part == 0:
                    v.tensor_copy(sv[:].rearrange("p r c -> p (r c)"), dyn(svs, h)).then_inc(*k.up("dve"))
                    first8(sv, vtop, 4)
                elif part == 1:
                    without8(sv, sv2, vtop, itop, 4)
                elif part == 2:
                    next8(sv2, vtop, itop, 4)
                elif part == 3:
                    v.tensor_copy(itf[:], itop[:]).then_inc(*k.up("dve"))
                    pairs(lambda i: vtop[:, 2 * i, :], lambda i: vtop[:, 2 * i + 1, :], ALU.add, cand)
                    first8(cand, ctop, 2)
                elif part == 4:
                    without8(cand, cand2, ctop, cidx, 2)
                elif part == 5:
                    next8(cand2, ctop, cidx, 2)
                    v.tensor_tensor(etab[:, 2, :, bass.ds(h * TOPK, TOPK)], ctop[:],
                                    ctop[:, :, 0:1].to_broadcast([P, 2, TOPK]), ALU.subtract).then_inc(*k.up("dve"))
                    v.tensor_scalar(cij[:, 0], cidx[:], 4, None, ALU.logical_shift_right).then_inc(*k.up("dve"))
                    v.tensor_scalar(cij[:, 1], cidx[:], 15, None, ALU.bitwise_and).then_inc(*k.up("dve"))
                    own()
                    step(v.tensor_copy(cijf[:], cij[:]))
                else:
                    numbers(part - 6, h)

            def one_hots(keys, n, b):
                tok = bass.ds(n, 8)
                v.tensor_tensor(oh_r[:, b], keys[:, 0:HALF].unsqueeze(1).to_broadcast([P, 8, HALF]),
                                e1t[:, tok].unsqueeze(2).to_broadcast([P, 8, HALF]), ALU.is_equal)\
                    .then_inc(*k.up("er_ready"))
                v.tensor_tensor(oh_l[:, b], iota[:].unsqueeze(1).to_broadcast([P, 8, P]),
                                e2t[:, tok].unsqueeze(2).to_broadcast([P, 8, P]), ALU.is_equal)\
                    .then_inc(*k.up("oh_ready"))
                dve.wait_ge(S["er_ready"], k.at("er_ready"))
                v.tensor_tensor(oh_g[:, b, 2], oh_r[:, b], gate_parts[:, 2, tok].unsqueeze(2).to_broadcast([P, 8, HALF]),
                                ALU.mult).then_inc(*k.up("oh_ready"))

            with k.loop("u0", dve, 8) as h:
                for j in range(HALF // 8):
                    split((j + 1) % 8)
                    search(j, h)
            flag("top_m")
            dve.wait_ge(*k.next("top_e"))
            weights = etab[:, 2].rearrange("p i (h s) -> p (i h) s", s=TOPK)
            step(v.tensor_reduce(small[:, 20:36], weights, AX.X, ALU.add))
            step(v.reciprocal(small[:, 20:36], small[:, 20:36]))
            step(v.tensor_tensor(weights, weights, small[:, 20:36].unsqueeze(2).to_broadcast([P, 16, TOPK]),
                                 ALU.mult))
            flag("idx_ready")
            for n, dst in enumerate((e1t, e2t)):
                take(3 + n)
                v.tensor_copy(dst[:], ps[:, 3 + n, 0:T]).then_inc(*k.up(f"free_v{3 + n}"))
            take(5)
            v.tensor_copy(rest[:], ps[:, 5, 0:T]).then_inc(*k.up("free_v5"))
            own()
            for part in range(3):
                step(v.tensor_copy(gate_parts[:, part, :], rest[:]))
                if part < 2:
                    step(v.tensor_tensor(rest[:], rest[:], gate_parts[:, part, :], ALU.subtract))
            with k.loop("route0", dve, 4) as i:
                def weigh(b):
                    take(2 + b % 4)
                    a = ag[:, :, bass.ds(i * 64 + 8 * b, 8)]
                    v.tensor_tensor(a, a, ps[:, 2 + b % 4, :].rearrange("p (s e) -> p e s", s=8), ALU.mult)\
                        .then_inc(*k.up(f"free_v{2 + b % 4}"))

                for b in range(8):
                    one_hots(iota, i * 64 + 8 * b, b % 2)
                    if b:
                        weigh(b - 1)
                weigh(7)
            residual(ag, "v0", HALF // 2)
            flag("gate_free")
            flag("gate_free")
            with k.loop("route1", dve, 4) as i:
                for b in range(8):
                    routed(dve, 1, i, b)
                    one_hots(iota_hi, i * 64 + 8 * b, b % 2)
            dve.wait_ge(*k.next("g_stored"))
            with k.loop("u1", dve, HALF // 2) as i:
                for b in range(2):
                    split((b + 1) % 2)
                    dve.wait_ge(*k.next("gate_ready"))
                    a = dyn(ag, i * 2 + b)
                    v.tensor_tensor(a, a, gt3[:, b, :], ALU.mult).then_inc(*k.up("gate_free"))
            residual(ag, "v1", HALF // 2, more=False)
            norm(hT, "norm_final_2", tmp)
            flag("out_ready")
        @block.gpsimd
        def _(pool):
            k = Counts("Pool", S, found)
            g = nc.gpsimd

            def select(t, fill, base, pattern, mult, op=ALU.is_ge):
                pool.wait_ge(*k.own())
                g.affine_select(out=t, in_=t, compare_op=op, fill=fill, base=base, pattern=pattern,
                                channel_multiplier=mult).then_inc(*k.up("pool"))

            g.memset(ident[:], 1.0).then_inc(*k.up("pool"))
            select(ident[:], 0.0, 0, [[-1, P]], 1, ALU.is_equal)
            g.memset(ones[:], 1.0).then_inc(*k.up("pool"))
            g.iota(iota[:], [[1, P]], base=0, channel_multiplier=0,
                   allow_small_or_imprecise_dtypes=True).then_inc(*k.up("pool"))
            g.iota(iota_hi[:], [[1, P]], base=HALF, channel_multiplier=0,
                   allow_small_or_imprecise_dtypes=True).then_inc(*k.up("pool"))
            dist = [[-P, 2], [1, T]]
            g.iota(nd_causal[:], dist, base=0, channel_multiplier=-1,
                   allow_small_or_imprecise_dtypes=True).then_inc(*k.up("pool"))
            select(nd_causal[:], NEG, 0, [[P, 2], [-1, T]], 1)
            g.iota(nd_cmp[:], [[-P, 2], [16, C_CMP]], base=31, channel_multiplier=-1,
                   allow_small_or_imprecise_dtypes=True).then_inc(*k.up("pool"))
            select(nd_cmp[:], NEG, -31, [[P, 2], [-16, C_CMP]], 1)
            g.memset(ok_cmp[:], 1.0).then_inc(*k.up("pool"))
            select(ok_cmp[:], 0.0, -31, [[P, 2], [-16, C_CMP]], 1)
            g.iota(nd2[:, 0], dist, base=0, channel_multiplier=-1,
                   allow_small_or_imprecise_dtypes=True).then_inc(*k.up("pool"))
            select(nd2[:, 0], NEG, 0, [[P, 2], [-1, T]], 1)
            select(nd2[:, 0], NEG, 127, [[-P, 2], [1, T]], -1)
            g.memset(nd2[:, 1], 0.0).then_inc(*k.up("pool"))
            select(nd2[:, 1], NEG, 0, [[P, 2], [-1, T]], 1)
            g.memset(triu[:], 1.0).then_inc(*k.up("pool"))
            select(triu[:], 0.0, 0, [[-P, 2], [1, T]], -1)
            pool.wait_ge(*k.own())
            g.memset(rstd[:, 0:1], 0.0).then_inc(S["table_ready"], 1)
            pool.wait_ge(S["masks_free"], 1)
            for j in range(3):
                g.iota(nd2[:, j], dist, base=0, channel_multiplier=-1,
                       allow_small_or_imprecise_dtypes=True).then_inc(*k.up("pool"))
                select(nd2[:, j], NEG, 0, [[P, 2], [-1, T]], 1)
            select(nd2[:, 0], NEG, P, [[-P, 2], [1, T]], -1)
            pool.wait_ge(*k.own())
            g.iota(dist_i[:], [[P, 2], [-1, T]], base=0, channel_multiplier=1).then_inc(S["table_ready"], 1)

            loads = [("dil", 0, small_w[:], dram["w_bgate"], "small_in"), ("dil", 0, w2[:], dram["w_cmp2"], "small_in"),
                     ("nsa_kv", 1, w1[:], dram["w_cmp1"][0], "wk_in")]
            loads += [("nsa_kv", 1, w1v[q][:], dram["w_cmp1"][1][:, 8 * q:8 * q + 8, :], "wv_in") for q in range(4)]
            loads += [("mem", 2, memT[:], dram["mem"], "mem_in")]
            for phase, free, dst, src, landed in loads:
                if free:
                    pool.wait_ge(S["w1_free"], free)
                g.dma_start(dst, src).then_inc(S[landed], 16)

            for half in range(2):
                with k.loop(f"route{half}", pool, 4) as i:
                    for b in range(8):
                        tok, row = bass.ds(i * 64 + 8 * b, 8), oh_r[:, b % 2]
                        pool.wait_ge(*k.next("er_ready"))
                        routed(pool, half, i, b)
                        for part in range(2):
                            g.tensor_tensor(oh_g[:, b % 2, part], row, gate_parts[:, part, tok].unsqueeze(2)
                                            .to_broadcast([P, 8, HALF]), ALU.mult).then_inc(*k.up("lr_ready"))
    return found


def _tiles(w):
    w = np.asarray(w)
    n = w.shape[1] // P
    return np.ascontiguousarray(w.reshape(w.shape[0] // P, P, n, P).transpose(2, 1, 0, 3)).reshape(n, P, w.shape[0])


def _feature_major(a):
    return np.ascontiguousarray(np.asarray(a).reshape(T, KC, P).transpose(2, 1, 0))


def layout(x):
    x = {k: np.asarray(v) for k, v in x.items()}
    w_in, w_in2 = x["w_in"][0], x["w_in_2"][0]
    cf, bg = 4096, 6400
    arrays = {
        "x": _feature_major(x["x"][0]),
        "mem": _feature_major(x["mem_2"][0]),
        "w_in": _tiles(np.concatenate([w_in[:, :cf], w_in[:, cf + 4:]], axis=1)),
        "w_branch": np.ascontiguousarray(
            x["w_branch"][0].reshape(BRANCHES, 4, P, KC, P).transpose(3, 2, 0, 1, 4)).reshape(KC, P, D),
        "w_out": x["w_out"][0].reshape(KC, P, D),
        "w_ffn_gate": _tiles(x["w_ffn_gate"][0]),
        "w_ffn_up": _tiles(x["w_ffn_up"][0]),
        "w_ffn_down": x["w_ffn_down"][0].reshape(FT, P, D),
        "w_in_2": _tiles(np.concatenate([w_in2[:, :bg], w_in2[:, bg + 48:]], axis=1)),
        "w_up_2": _tiles(np.concatenate([x["w_up_a_2"][0], x["w_up_b_2"][0]], axis=0)),
        "w_out_2": x["w_out_2"][0].reshape(KC, P, D),
        "w_xq_2": _tiles(x["w_xq_2"][0]),
        "w_xkv_2": _tiles(x["w_xkv_2"][0]),
        "w_xo_2": x["w_xo_2"][0].reshape(4, P, D),
        "w_pq_2": _tiles(x["w_pq_2"][0]),
        "expert_u_2": np.ascontiguousarray(
            x["expert_u_2"][0].reshape(N_KEYS, P, KC, P).transpose(0, 3, 2, 1)).reshape(N_KEYS, P, D),
        "expert_v_2": x["expert_v_2"][0].reshape(N_KEYS, P, D),
        "sub_keys": np.ascontiguousarray(np.stack([x["sub_keys1_2"][0].T, x["sub_keys2_2"][0].T], axis=1)),
    }
    blocks = np.zeros((P, 2, 4, P), np.float32)
    for g, name in enumerate(("lru_wa", "lru_wx")):
        for n in range(8):
            o = 64 * (n % 2)
            blocks[o:o + 64, g, n // 2, o:o + 64] = x[name][0, n]
    arrays["w_ab"] = blocks
    arrays["w_bgate"] = np.ascontiguousarray(w_in2[:, bg:bg + 48].reshape(KC, P, 48).transpose(1, 0, 2)).reshape(P, -1)
    cmp1 = np.stack([x["w_cmp_k1_2"][0], x["w_cmp_v1_2"][0]]).reshape(2, 32, 64, P).transpose(0, 2, 1, 3)
    arrays["w_cmp1"] = np.concatenate([cmp1, cmp1], axis=1)
    cmp2 = np.stack([x["w_cmp_k2_2"][0], x["w_cmp_v2_2"][0]], axis=1)
    arrays["w_cmp2"] = np.concatenate([cmp2, cmp2], axis=2)

    def col(v):
        return v.reshape(-1, P).T

    def row(v):
        return np.broadcast_to(v.reshape(1, -1), (P, v.size))

    def alibi(n):
        return (2.0 ** (-8.0 * np.arange(1, n + 1) / n)).astype(np.float32)

    def pe_cols(v):
        return np.concatenate([v.T, v.T], axis=0)

    parts = {
        "norm_mix": col(x["norm_mix"][0]), "norm_ffn": col(x["norm_ffn"][0]), "norm_final": col(x["norm_final"]),
        "norm_mix_2": col(x["norm_mix_2"][0]), "norm_x_2": col(x["norm_x_2"][0]),
        "norm_mem_2": col(x["norm_mem_2"][0]), "norm_ffn_2": col(x["norm_ffn_2"][0]),
        "norm_final_2": col(x["norm_final_2"]), "b_gate": col(x["b_gate"][0]),
        "conv_w": col(x["lru_conv_w"][0].reshape(-1)), "conv_b": col(x["lru_conv_b"][0]), "ba": col(x["lru_ba"][0]),
        "bx": col(x["lru_bx"][0]), "lambda": col(x["lru_lambda"][0]), "fox_b_f": row(x["fox_b_f"][0]),
        "sinks": row(x["swa_sinks"][0]), "subln": row(x["diff_subln"][0]), "lq1": row(x["diff_lq1"][0]),
        "lk1": row(x["diff_lk1"][0]), "lq2": row(x["diff_lq2"][0]), "lk2": row(x["diff_lk2"][0]),
        "pe_k": pe_cols(x["pe_cmp_k_2"][0]), "pe_v": pe_cols(x["pe_cmp_v_2"][0]),
        "slopes": row(np.concatenate([alibi(4), alibi(8), alibi(12), alibi(16)])),
        "w_cf": w_in[:, cf:cf + 4].reshape(KC, P, 4).transpose(1, 0, 2).reshape(P, -1),
    }
    arrays["params"] = np.concatenate([parts[name] for name in PARAMS], axis=1)
    return arrays


def kernel(**inputs):
    import concourse.bacc as bacc
    from concourse.bass_utils import run_bass_kernel_spmd

    arrays = {f"in_{name}": np.ascontiguousarray(a) for name, a in layout(inputs).items()}
    nc = bacc.Bacc("TRN2", target_bir_lowering=False, num_devices=1)
    dram = {name[3:]: nc.dram_tensor(name, a.shape, F32, kind="ExternalInput").ap() for name, a in arrays.items()}
    out = nc.dram_tensor("out", (P, KC, T), F32, kind="ExternalOutput").ap()
    wrong = build(nc, dram, out)
    assert not wrong, wrong
    r = run_bass_kernel_spmd(nc, [arrays], core_ids=[0])
    return np.ascontiguousarray(r.results[0]["out"].transpose(2, 1, 0)).reshape(1, T, D)
```
